# Optimizing a Trainium2 kernel written in Bass

```python
import math
import jax, jax.numpy as jnp
from jax import lax
import numpy as np

'''Hybrid bidirectional encoder trunk, DEPTH layers of parallel head groups.

Each layer:  h = RMSNorm(x); one combined projection h @ w_in whose columns are
partitioned among three head groups that all read h:
  A) windowed grouped-query attention (+-128 tokens), per-head sink logit, ALiBi, banded 128-blocks
  B) differential attention (two softmax maps per head, learned lambda), ALiBi, 128-query blocks
  C) bidirectional RWKV-7 time mixing (centred short conv, data-dependent decay,
     generalized delta-rule state update, one scan per direction, summed)
Group outputs are concatenated and mapped by one output projection into the residual.
Then a pre-norm cross-attention (4 heads) into 256 memory tokens, then a pre-norm SwiGLU FFN.
A final RMSNorm is applied after the last layer.

Inputs:  x (BATCH, SEQ, D_MODEL), mem (BATCH, 256, D_MODEL), per-layer weights stacked on a leading DEPTH axis.
Output:  (BATCH, SEQ, D_MODEL).
'''

D_MODEL = 1024
BATCH = 1
SEQ = 1024
DEPTH = 1

N_MEM = 256
HEAD_DIM = 64
BLOCK = 128
WINDOW = 128
WIN_HEADS = 4
WIN_KV_HEADS = 2
DIFF_HEADS = 4
DIFF_QK_DIM = 64
DIFF_V_DIM = 2 * DIFF_QK_DIM
RWKV_HEADS = 4
RWKV_HEAD = 64
W_LORA = 64
A_LORA = 64
G_LORA = 128
X_HEADS = 4
X_HEAD_DIM = 128
D_FF = -(-8 * D_MODEL // (3 * 256)) * 256
RMS_EPS = 1e-6
GN_EPS = 64e-5

WIN_WIDTH = WIN_HEADS * HEAD_DIM
DIFF_WIDTH = DIFF_HEADS * DIFF_V_DIM
RWKV_WIDTH = RWKV_HEADS * RWKV_HEAD
MIX_WIDTH = WIN_WIDTH + DIFF_WIDTH + RWKV_WIDTH
RWKV_IN = 3 * RWKV_WIDTH + W_LORA + A_LORA + G_LORA
IN_SIZES = (WIN_WIDTH, WIN_KV_HEADS * HEAD_DIM, WIN_KV_HEADS * HEAD_DIM,
            2 * DIFF_HEADS * DIFF_QK_DIM, 2 * DIFF_HEADS * DIFF_QK_DIM, DIFF_WIDTH, RWKV_IN)
IN_WIDTH = sum(IN_SIZES)
RWKV_SIZES = (RWKV_WIDTH, RWKV_WIDTH, RWKV_WIDTH, W_LORA, A_LORA, G_LORA)

kernel_name = 'hybrid_parallel_heads_bidir_encoder'

f32 = jnp.float32

def split_last(z, sizes):
    idx = [int(i) for i in np.cumsum(sizes)[:-1]]
    return jnp.split(z, idx, axis=-1)

def rmsnorm(z, g):
    z32 = z.astype(f32)
    return (z32 * lax.rsqrt(jnp.mean(z32 * z32, axis=-1, keepdims=True) + RMS_EPS)).astype(z.dtype) * g

def alibi_slopes():
    n = WIN_HEADS + DIFF_HEADS
    s = jnp.exp2(-8.0 * jnp.arange(1, n + 1, dtype=f32) / n)
    return s[0::2], s[1::2]

def window_gqa(q, k, v, sink, slopes):
    b, t = q.shape[:2]
    nb = t // BLOCK
    g = WIN_HEADS // WIN_KV_HEADS
    qb = q.reshape(b, nb, BLOCK, WIN_KV_HEADS, g, HEAD_DIM)

    def band(z):
        zp = jnp.pad(z, ((0, 0), (BLOCK, BLOCK), (0, 0), (0, 0)))
        zb = zp.reshape(b, nb + 2, BLOCK, WIN_KV_HEADS, HEAD_DIM)
        return jnp.concatenate([zb[:, :-2], zb[:, 1:-1], zb[:, 2:]], axis=2)

    kb, vb = band(k), band(v)
    s = jnp.einsum('bnqhgd,bnkhd->bnhgqk', qb, kb).astype(f32) * (HEAD_DIM ** -0.5)
    qi = jnp.arange(BLOCK)[:, None]
    ki = jnp.arange(3 * BLOCK)[None, :] - BLOCK
    delta = ki - qi
    key_pos = jnp.arange(nb)[:, None] * BLOCK + ki
    in_range = (key_pos >= 0) & (key_pos < t)
    valid = (jnp.abs(delta) <= WINDOW)[None] & in_range[:, None, :]
    bias = -slopes.reshape(WIN_KV_HEADS, g, 1, 1) * jnp.abs(delta).astype(f32)
    s = jnp.where(valid[None, :, None, None], s + bias, -jnp.inf)
    sink_col = jnp.broadcast_to(sink.astype(f32).reshape(WIN_KV_HEADS, g, 1, 1), s.shape[:-1] + (1,))
    p = jax.nn.softmax(jnp.concatenate([s, sink_col], axis=-1), axis=-1)[..., :-1]
    o = jnp.einsum('bnhgqk,bnkhd->bnqhgd', p.astype(v.dtype), vb)
    return o.reshape(b, t, WIN_WIDTH)

def diff_attention(q, k, v, lam, lam_init, subln_g, slopes):
    b, t = q.shape[:2]
    nb = t // BLOCK
    qb = jnp.moveaxis(q.reshape(b, nb, BLOCK, DIFF_HEADS, 2, DIFF_QK_DIM), 1, 0)
    kpos = jnp.arange(t)

    def block(args):
        qblk, i = args
        s = jnp.einsum('bqhcd,bkhcd->bhcqk', qblk, k).astype(f32) * (DIFF_QK_DIM ** -0.5)
        qpos = i * BLOCK + jnp.arange(BLOCK)
        dist = jnp.abs(kpos[None, :] - qpos[:, None]).astype(f32)
        s = s - slopes[None, :, None, None, None] * dist[None, None, None]
        p = jax.nn.softmax(s, axis=-1)
        a = p[:, :, 0] - lam * p[:, :, 1]
        return jnp.einsum('bhqk,bkhe->bqhe', a.astype(v.dtype), v)

    o = lax.map(block, (qb, jnp.arange(nb)))
    o = jnp.moveaxis(o, 0, 1).reshape(b, t, DIFF_HEADS, DIFF_V_DIM)
    o = rmsnorm(o, subln_g) * (1.0 - lam_init)
    return o.reshape(b, t, DIFF_WIDTH)

def heads(z):
    return z.reshape(z.shape[:-1] + (RWKV_HEADS, RWKV_HEAD))

def time_major(z):
    z = jnp.stack([z[0], jnp.flip(z[1], axis=1)])
    return jnp.moveaxis(z, 2, 0).astype(f32)

def rwkv7_bidir(c, conv, w0, w_up, a0, a_up, g_up, k_k, k_a, r_k, ln_g, ln_b):
    b, t, _ = c.shape
    dt = c.dtype
    cp = jnp.pad(c, ((0, 0), (1, 1), (0, 0)))
    c = cp[:, :-2] * conv[0] + cp[:, 1:-1] * conv[1] + cp[:, 2:] * conv[2]
    r, k, v, wd, ad, gd = split_last(c.astype(f32), RWKV_SIZES)
    w_log = -jax.nn.softplus(-(w0[:, None, None] + jnp.einsum('btl,dlc->dbtc', jnp.tanh(wd), w_up))) - 0.5
    decay = jnp.exp(-jnp.exp(w_log))
    a = jax.nn.sigmoid(a0[:, None, None] + jnp.einsum('btl,dlc->dbtc', ad, a_up))
    g = jax.nn.sigmoid(gd) @ g_up
    kk = heads(k * k_k)
    kk = kk / jnp.maximum(jnp.linalg.norm(kk, axis=-1, keepdims=True), 1e-12)
    kd = heads(k * (1.0 + (a - 1.0) * k_a))
    rh, vh = heads(r), heads(v)
    shp = kd.shape
    xs = tuple(time_major(z) for z in (heads(decay), jnp.broadcast_to(kk, shp), kk * heads(a), kd,
                                       jnp.broadcast_to(vh, shp), jnp.broadcast_to(rh, shp)))

    def step(S, inp):
        wt, kkt, kat, kt, vt, rt = inp
        S = (S * wt[..., None, :]
             - jnp.einsum('...vk,...k->...v', S, kkt)[..., :, None] * kat[..., None, :]
             + vt[..., :, None] * kt[..., None, :])
        return S, jnp.einsum('...vk,...k->...v', S, rt)

    S0 = jnp.zeros((2, b, RWKV_HEADS, RWKV_HEAD, RWKV_HEAD), f32)
    _, y = lax.scan(step, S0, xs)
    y = jnp.moveaxis(y, 0, 2)
    y = y[0] + jnp.flip(y[1], axis=1)
    mu = jnp.mean(y, axis=-1, keepdims=True)
    var = jnp.mean(jnp.square(y - mu), axis=-1, keepdims=True)
    yn = (y - mu) * lax.rsqrt(var + GN_EPS) * heads(ln_g.astype(f32)) + heads(ln_b.astype(f32))
    bonus = jnp.sum(jnp.sum(rh * kd * r_k, axis=-1, keepdims=True), axis=0) * vh
    return ((yn + bonus).reshape(b, t, RWKV_WIDTH) * g).astype(dt)

def cross_attn(h, mem_n, wq, wkv, wo):
    b, t, _ = h.shape
    m = mem_n.shape[1]
    q = (h @ wq).reshape(b, t, X_HEADS, X_HEAD_DIM)
    kv = (mem_n @ wkv).reshape(b, m, 2, X_HEADS, X_HEAD_DIM)
    s = jnp.einsum('bqhd,bkhd->bhqk', q, kv[:, :, 0]).astype(f32) * (X_HEAD_DIM ** -0.5)
    p = jax.nn.softmax(s, axis=-1)
    o = jnp.einsum('bhqk,bkhd->bqhd', p.astype(h.dtype), kv[:, :, 1]).reshape(b, t, X_HEADS * X_HEAD_DIM)
    return o @ wo

def setup_inputs(seed: int = 0) -> dict:
    key = jax.random.key(seed)
    ks = iter(jax.random.split(key, 40))
    L = DEPTH

    def nrm(shape, scale):
        return jax.random.normal(next(ks), shape, f32) * scale

    def gain(shape):
        return 1.0 + nrm(shape, 0.02)

    return {
        'x': nrm((BATCH, SEQ, D_MODEL), 1.0),
        'mem': nrm((BATCH, N_MEM, D_MODEL), 1.0),
        'norm_mix': gain((L, D_MODEL)),
        'w_in': nrm((L, D_MODEL, IN_WIDTH), D_MODEL ** -0.5),
        'win_sink': nrm((L, WIN_HEADS), 0.5),
        'diff_lq1': nrm((L, DIFF_QK_DIM), 0.1),
        'diff_lk1': nrm((L, DIFF_QK_DIM), 0.1),
        'diff_lq2': nrm((L, DIFF_QK_DIM), 0.1),
        'diff_lk2': nrm((L, DIFF_QK_DIM), 0.1),
        'diff_subln': gain((L, DIFF_V_DIM)),
        'rwkv_conv': jnp.array([0.3, 1.0, 0.3], f32)[None, :, None] + nrm((L, 3, RWKV_IN), 0.1),
        'rwkv_w0': jax.random.uniform(next(ks), (L, 2, RWKV_WIDTH), f32, -6.0, 1.0),
        'rwkv_w_up': nrm((L, 2, W_LORA, RWKV_WIDTH), 0.1),
        'rwkv_a0': nrm((L, 2, RWKV_WIDTH), 0.5),
        'rwkv_a_up': nrm((L, 2, A_LORA, RWKV_WIDTH), A_LORA ** -0.5),
        'rwkv_g_up': nrm((L, G_LORA, RWKV_WIDTH), G_LORA ** -0.5),
        'rwkv_k_k': 0.85 + nrm((L, RWKV_WIDTH), 0.05),
        'rwkv_k_a': 1.0 + nrm((L, RWKV_WIDTH), 0.05),
        'rwkv_r_k': nrm((L, RWKV_HEADS, RWKV_HEAD), 0.1),
        'rwkv_ln_g': gain((L, RWKV_WIDTH)),
        'rwkv_ln_b': nrm((L, RWKV_WIDTH), 0.02),
        'w_out': nrm((L, MIX_WIDTH, D_MODEL), MIX_WIDTH ** -0.5),
        'norm_cross': gain((L, D_MODEL)),
        'norm_mem': gain((D_MODEL,)),
        'x_wq': nrm((L, D_MODEL, X_HEADS * X_HEAD_DIM), D_MODEL ** -0.5),
        'x_wkv': nrm((L, D_MODEL, 2 * X_HEADS * X_HEAD_DIM), D_MODEL ** -0.5),
        'x_wo': nrm((L, X_HEADS * X_HEAD_DIM, D_MODEL), (X_HEADS * X_HEAD_DIM) ** -0.5),
        'norm_ffn': gain((L, D_MODEL)),
        'ffn_w_gu': nrm((L, D_MODEL, 2 * D_FF), D_MODEL ** -0.5),
        'ffn_w_down': nrm((L, D_FF, D_MODEL), D_FF ** -0.5),
        'norm_final': gain((D_MODEL,)),
    }

def reference(x, mem, norm_mix, w_in, win_sink, diff_lq1, diff_lk1, diff_lq2, diff_lk2, diff_subln,
              rwkv_conv, rwkv_w0, rwkv_w_up, rwkv_a0, rwkv_a_up, rwkv_g_up, rwkv_k_k, rwkv_k_a, rwkv_r_k,
              rwkv_ln_g, rwkv_ln_b, w_out, norm_cross, norm_mem, x_wq, x_wkv, x_wo, norm_ffn,
              ffn_w_gu, ffn_w_down, norm_final):
    b, t, _ = x.shape
    slopes_win, slopes_diff = alibi_slopes()
    mem_n = rmsnorm(mem, norm_mem)
    for l in range(DEPTH):
        h = rmsnorm(x, norm_mix[l])
        aq, ak, av, bq, bk, bv, cin = split_last(h @ w_in[l], IN_SIZES)
        o_win = window_gqa(aq.reshape(b, t, WIN_HEADS, HEAD_DIM),
                           ak.reshape(b, t, WIN_KV_HEADS, HEAD_DIM),
                           av.reshape(b, t, WIN_KV_HEADS, HEAD_DIM), win_sink[l], slopes_win)
        lam_init = 0.8 - 0.6 * math.exp(-0.3 * l)
        lam = (jnp.exp(jnp.sum((diff_lq1[l] * diff_lk1[l]).astype(f32)))
               - jnp.exp(jnp.sum((diff_lq2[l] * diff_lk2[l]).astype(f32))) + lam_init)
        o_diff = diff_attention(bq.reshape(b, t, DIFF_HEADS, 2, DIFF_QK_DIM),
                                bk.reshape(b, t, DIFF_HEADS, 2, DIFF_QK_DIM),
                                bv.reshape(b, t, DIFF_HEADS, DIFF_V_DIM),
                                lam, lam_init, diff_subln[l], slopes_diff)
        o_rwkv = rwkv7_bidir(cin, rwkv_conv[l], rwkv_w0[l], rwkv_w_up[l], rwkv_a0[l], rwkv_a_up[l],
                             rwkv_g_up[l], rwkv_k_k[l], rwkv_k_a[l], rwkv_r_k[l], rwkv_ln_g[l], rwkv_ln_b[l])
        x = x + jnp.concatenate([o_win, o_diff, o_rwkv], axis=-1) @ w_out[l]
        x = x + cross_attn(rmsnorm(x, norm_cross[l]), mem_n, x_wq[l], x_wkv[l], x_wo[l])
        gate, up = jnp.split(rmsnorm(x, norm_ffn[l]) @ ffn_w_gu[l], 2, axis=-1)
        x = x + (jax.nn.silu(gate) * up) @ ffn_w_down[l]
    return rmsnorm(x, norm_final)


_drawn_inputs = setup_inputs


def setup_inputs(seed=0):
    import zlib

    import numpy as np

    out = dict(_drawn_inputs(seed))
    spreads = {}
    factors = {'win_sink': 8.0,
     'diff_lq1': 8.0,
     'diff_lk2': 2.807,
     'diff_subln': 4.986,
     'rwkv_w_up': 4.172,
     'rwkv_k_k': 4.171,
     'rwkv_k_a': 2.929,
     'rwkv_ln_g': 8.0,
     'rwkv_ln_b': 8.0,
     'norm_cross': 8.0,
     'norm_mem': 8.0,
     'norm_ffn': 4.935,
     'norm_final': 2.772}
    for name, (base, spread) in spreads.items():
        noise = np.random.default_rng([zlib.crc32(name.encode()), seed]).standard_normal(out[name].shape)
        drawn = base * np.exp(spread * noise) if base else spread * noise
        out[name] = __import__('jax').numpy.asarray(drawn.astype(out[name].dtype))
    for name, factor in factors.items():
        out[name] = (out[name] * factor).astype(out[name].dtype)
    return out
```

```python
import math
from contextlib import ExitStack

import concourse.bass as bass
from concourse import mybir

F32 = mybir.dt.float32
F32R = mybir.dt.float32r
ALU = mybir.AluOpType
ACT = mybir.ActivationFunctionType
AX_X = mybir.AxisListType.X

P = 128
D = 1024
T = 1024
NT = T // P
KD = D // P
MEM = 256
DFF = 2816
IN_W = 3072
PW = 256
PK = 2
NRAW = 3
NW = 6
RMS_EPS = 1e-6
GN_EPS = 64e-5
C = 64
NCH = T // C
LEVELS = [2, 4, 8, 16, 32]
E05 = math.exp(-0.5)
LAM_INIT = 0.8 - 0.6 * math.exp(-0.3 * 0)
FF_ITERS = DFF // PW

C_ID = 0
C_ONES = 128
C_MASK = {0: 256, 1: 384}
C_LT = {0: 512, 1: 512 + 384}
C_I64 = 1280
C_LEN = 1344
SLOPES = [2.0 ** -(k + 1) for k in range(8)]
WIN_SLOPES, DIFF_SLOPES = SLOPES[0::2], SLOPES[1::2]


def build(nc, io):
    out = io["out"]
    ctx = ExitStack()
    with ctx:
        base = 16512

        def at(name, kib, shape, dt=F32):
            return nc.alloc_sbuf_tensor_at(name, [P] + list(shape), dt, offset=base + int(kib * 1024))

        arena_end = 207.8
        ctx.enter_context(nc.sbuf_tensor("arena", [P, int(arena_end * 256)], F32))
        WH = at("WH", 0, [NW, PK, PW], F32R)
        WL = at("WL", 12, [NW, PK, PW], F32R)
        RAW = at("RAW", 24, [NRAW, PK, PW])
        CN = at("CN", 30, [C_LEN])
        WA = at("WA", 35.25, [2, 256])
        GU = at("GU", 37.25, [256])
        BC = at("BC", 38.25, [1024])
        SM = at("SM", 42.25, [432])
        HH = at("HH", 44, [KD, T], F32R)
        HL = at("HL", 76, [KD, T], F32R)
        MIX = at("MIX", 108, [8, T])
        BQ = at("BQ", 140, [4, T])
        BK = at("BK", 156, [4, T])
        BV = at("BV", 172, [NT, 512])
        GB = at("GB", 124, [D])
        XT = at("XT", 188, [2, D])
        XN = at("XN", 196, [2, D])
        E_ = at("E_", 124, [4, T])
        TAB = at("TAB", 188, [1920])
        AT_ = at("AT_", 195.5, [T])
        OB = at("OB", 199.5, [2, NT, 128])
        CIN = at("CIN", 140, [8, T + 2])
        AQ = at("AQ", 173, [2, T])
        AK = at("AK", 181, [2, T])
        AV = at("AV", 189, [NT, 128])
        WP_ = at("WP_", 44, [4, 384])
        WT_ = at("WT_", 50, [12, 128])
        WO_ = at("WO_", 56, [256])
        WB_ = at("WB_", 58, [4, 384])
        CV = at("CV", 44, [8, T])
        KK = at("KK", 76, [2, T])
        YY = at("YY", 84, [NT, 2, 2, 64])
        VT = at("VT", 92, [NT, 2, 2, 64])
        KS = at("KS", 100, [2, T])
        KR = at("KR", 140, [2, 2, NCH, C])
        BKt = at("BKt", 156, [2, 2, NCH, C])
        S1_ = at("S1_", 172, [2, T])
        S2_ = at("S2_", 180, [2, T])
        S3_ = at("S3_", 188, [2, T])
        YF = at("YF", 172, [NT, 2, 2, 64])
        G1 = at("G1", 172, [4, 2, 2, 2, C])
        LT = at("LT", 180, [8, C])
        QQ = at("QQ", 182, [2, 8, C])
        XX = at("XX", 186, [8, C])
        RH = at("RH", 188, [8, 2, C])
        BT = at("BT", 192, [8, C])
        KT = at("KT", 194, [8, C])
        WU = at("WU", 196, [8, 2, C])
        QT0 = at("QT0", 200, [8, C])
        EH = at("EH", 202, [32])
        DD = at("DD", 202.25, [32])
        HT = at("HT", 202.5, [32])
        SCM = at("SCM", 196, [T])
        FO = at("FO", 180, [2, D])
        X = at("X", 140, [NT, D])
        AH = at("AH", 108, [4, T], F32R)
        AL = at("AL", 124, [4, T], F32R)
        XN2 = at("XN2", 172, [2, D])
        QC = at("QC", 180, [4, T])
        KM = at("KM", 196, [4, MEM])
        VM = at("VM", 200, [2, 512])
        GBM = at("GBM", 116, [D])
        GBC = at("GBC", 120, [D])
        GBF = at("GBF", 196, [D])
        GBL = at("GBL", 200, [D])
        MX = at("MX", 180, [2, D])
        CP = at("CP", 172, [1024])
        CPT = at("CPT", 176, [1024])
        ACTB = at("ACTB", 172, [2, T])
        FU = at("FU", 180, [2, T])

        PS = ctx.enter_context(nc.psum_tensor("PS", [P, 8, 512], F32))

        def sem(name):
            return ctx.enter_context(nc.semaphore(name))

        ID = CN[:, C_ID:C_ID + 128]
        ONES = CN[:, C_ONES:C_ONES + 128]
        I64 = CN[:, C_I64:C_I64 + 64]
        LNG, LNB, SUB, SINK = BC[:, 0:256], BC[:, 256:512], BC[:, 512:640], BC[:, 640:644]
        LQ = [BC[:, 648 + 64 * i:712 + 64 * i] for i in range(4)]
        VR = BC[0:38, 904:1024]
        SS, RS = SM[:, 0:8], SM[:, 8:16]
        LAM = SM[:, 16:20]
        MM, NM, LL = SM[:, 20:24], SM[:, 24:28], SM[:, 28:32]
        PT = SM[:, 32:70]
        RB = SM[:, 72:80]
        CO = SM[:, 80:96]
        HS, HR = SM[:, 96:104], SM[:, 104:112]
        GS, GM = SM[:, 112:144], SM[:, 144:176]
        GV = SM[:, 176:208]
        BON = SM[:, 208:240]
        WM, WL4, WD4, WR = SM[:, 240:244], SM[:, 244:248], SM[:, 248:252], SM[:, 252:256]
        CM, CL, CR = SM[:, 256:260], SM[:, 260:264], SM[:, 264:268]
        MS, MR = SM[:, 268:270], SM[:, 270:272]
        FS, FR = SM[:, 272:280], SM[:, 280:288]
        AS, AR = SM[:, 288:296], SM[:, 296:304]
        BS, BR = SM[:, 304:312], SM[:, 312:320]
        NMD, MD, LD = SM[:, 320:324], SM[:, 324:328], SM[:, 328:332]
        VROWS = XN[0:38, 0, 0:128]
        PTC_CONV, PTC_W0, PTC_A0, PTC_KK, PTC_KA, PTC_RK = 0, 24, 28, 32, 34, 36

        def col(i):
            return PT[:, i:i + 1]

        raw_full = [sem(f"raw_full{i}") for i in range(NRAW)]
        w_hi, w_lo, w_used = sem("w_hi"), sem("w_lo"), sem("w_used")
        consts_in, vecs_in, tab_in = sem("consts_in"), sem("vecs_in"), sem("tab_in")
        vec_t, vec_c = sem("vec_t"), sem("vec_c")
        dve_chain, act_chain, pool_chain = sem("dve_chain"), sem("act_chain"), sem("pool_chain")

        w_in, w_out_, wq, wkv, wo = io["w_in"][0], io["w_out"][0], io["x_wq"][0], io["x_wkv"][0], io["x_wo"][0]
        w_gu, w_dn = io["ffn_w_gu"][0], io["ffn_w_down"][0]
        BQ0, BK0, BV0, CI0, AQ0, AK0 = 512, 1024, 1536, 2048, 0, 256

        def slab(w, c0, rows=D):
            return [(w, r, c0) for r in range(0, rows, PK * P)]

        proj_cols = [BQ0, BQ0 + PW, BK0, BK0 + PW, BV0, BV0 + PW, CI0, CI0 + PW, CI0 + 2 * PW, CI0 + 3 * PW, AQ0, AK0]
        pieces = []
        for c0 in proj_cols:
            pieces += slab(w_in, c0)
        for c0 in range(0, D, PW):
            pieces += slab(w_out_, c0)
        for c0 in range(0, 1024, PW):
            pieces += slab(wkv, c0)
        for c0 in range(0, 512, PW):
            pieces += slab(wq, c0)
        for c0 in range(0, D, PW):
            pieces += slab(wo, c0, 512)
        N_LIN = len(pieces)
        for i in range(FF_ITERS + 1):
            if i < FF_ITERS:
                pieces += slab(w_gu, i * PW) + slab(w_gu, DFF + i * PW)
            if i >= 1:
                pieces += [(w_dn, (i - 1) * PW, c0) for c0 in range(0, D, PW)]

        class Norm:
            def __init__(self, name, n):
                self.n = n
                self.full = [sem(f"{name}_full0"), sem(f"{name}_full1")]
                self.std, self.xn, self.tr, self.hi, self.lo = (sem(f"{name}_{k}") for k in ("std", "xn", "tr", "hi", "lo"))

        n1, nm, n2, n3 = Norm("n1", NT), Norm("nm", 2), Norm("n2", NT), Norm("n3", NT)
        gain_in = {k: sem(f"gain_{k}") for k in ("mix", "mem", "cross", "ffn", "final")}

        job_evac = sem("job_evac")
        NJ = len(proj_cols)
        jobs2 = ([("wout", i) for i in range(4)] + [("wkv", i) for i in range(4)] + [("wq", i) for i in range(2)]
                 + [("wo", i) for i in range(4)])
        job2_act, job2_dve = sem("job2_act"), sem("job2_dve")
        end2, e = [], 4 * NJ
        for kind, _ in jobs2:
            e += 2 if kind == "wo" else 4
            end2.append(e)

        def ff0(i):
            return N_LIN + 12 * i - (4 if i else 0)

        evac_of, n_act, n_dve = [], 0, 0
        for kind, _ in jobs2:
            if kind in ("wkv", "wq"):
                n_act += 1
                evac_of.append((job2_act, n_act))
            else:
                n_dve += 1
                evac_of.append((job2_dve, n_dve))

        qk_done, s_read, nm_done, exp_done = sem("qk_done"), sem("s_read"), sem("nm_done"), sem("exp_done")
        comb_done, tr_done, at_evac, pv_done, o_evac = (sem(k) for k in ("comb_done", "tr_done", "at_evac", "pv_done", "o_evac"))
        sq_done, hs_done, hstd, hn_done, ht_done, hm_evac = (sem(k) for k in ("sq_done", "hs_done", "hstd", "hn_done", "ht_done", "hm_evac"))
        lam_s, lam_e = sem("lam_s"), sem("lam_e")

        wb_in, w_qk, w_nm, w_exp, w_r, w_tr, w_pt, w_pv, w_on, w_ot, w_mix = (
            sem(k) for k in ("wb_in", "w_qk", "w_nm", "w_exp", "w_r", "w_tr", "w_pt", "w_pv", "w_on", "w_ot", "w_mix"))

        pads, r_conv, r_vt, r_vte, r_sq, r_kn, r_std, r_act, r_kk = (
            sem(k) for k in ("pads", "r_conv", "r_vt", "r_vte", "r_sq", "r_kn", "r_std", "r_act", "r_kk"))
        r_z, r_sig, r_c, r_exp, r_pre, r_scm, r_eh = (sem(k) for k in ("r_z", "r_sig", "r_c", "r_exp", "r_pre", "r_scm", "r_eh"))
        g_pe, g_act, g_dve, g_pool = sem("g_pe"), sem("g_act"), sem("g_dve"), sem("g_pool")
        c_mm, c_z, y_mm, y_add = sem("c_mm"), sem("c_z"), sem("y_mm"), sem("y_add")
        p_s, p_mm, p_std, p_bon, p_g, p_y, p_tr, p_mix = (sem(k) for k in ("p_s", "p_mm", "p_std", "p_bon", "p_g", "p_y", "p_tr", "p_mix"))
        mix_hi, mix_lo, x_in = sem("mix_hi"), sem("mix_lo"), sem("x_in")
        c_qk, c_max, c_exp, c_p, c_tr, c_pt, c_pv, c_hi, c_lo = (
            sem(k) for k in ("c_qk", "c_max", "c_exp", "c_p", "c_tr", "c_pt", "c_pv", "c_hi", "c_lo"))
        f_silu, f_mul, f_hi, f_lo, f_add = (sem(k) for k in ("f_silu", "f_mul", "f_hi", "f_lo", "f_add"))
        l_std, l_o, out_done = sem("l_std"), sem("l_o"), [sem("out_done0"), sem("out_done1")]

        NB = 4
        G_PE, G_ACT, G_DVE, G_POOL = 3 + 2 + 2 * 5 + 1 + 2, 2 + 2 + 5 + 1 + 1, 2 + 5 + 1, 6

        block = ctx.enter_context(nc.Block())

        @block.sync
        def _(sp):
            def load(p):
                w, r0, c0 = pieces[p]
                if p >= NRAW:
                    sp.wait_ge(w_hi, p - NRAW + 1)
                    sp.wait_ge(w_lo, p - NRAW + 1)
                sp.dma_start(RAW[:, p % NRAW], w[r0:r0 + PK * P, c0:c0 + PW].rearrange("(k p) c -> p k c", p=P)
                             ).then_inc(raw_full[p % NRAW], 16)

            sp.dma_start(XT[:, 0], io["x"][0, 0:P, :]).then_inc(n1.full[0], 16)
            sp.dma_start(GB[:, :], io["norm_mix"][0:1, :].broadcast_to([P, D])).then_inc(gain_in["mix"], 16)
            sp.dma_start(CN[:, :], io["consts"]).then_inc(consts_in, 16)
            sp.dma_start(XT[:, 1], io["x"][0, P:2 * P, :]).then_inc(n1.full[1], 16)
            for p in range(NRAW):
                load(p)
            for tt in range(2, NT):
                sp.wait_ge(n1.xn, tt - 1)
                sp.dma_start(XT[:, tt % 2], io["x"][0, tt * P:(tt + 1) * P, :]).then_inc(n1.full[tt % 2], 16)
            for p in range(NRAW, 4 * NJ):
                load(p)
            for p in range(4 * NJ, 4 * NJ + NRAW):
                load(p)
            sp.wait_ge(y_add, 8)
            for tt in range(NT):
                sp.dma_start(X[:, tt], io["x"][0, tt * P:(tt + 1) * P, :]).then_inc(x_in, 16)
            sp.wait_ge(mix_lo, 8)
            sp.wait_ge(mix_hi, 8)
            sp.dma_start(GBM[:, :], io["norm_mem"].rearrange("(a d) -> a d", a=1).broadcast_to([P, D])).then_inc(gain_in["mem"], 16)
            for tt in range(2):
                sp.dma_start(MX[:, tt], io["mem"][0, tt * P:(tt + 1) * P, :]).then_inc(nm.full[tt], 16)
            sp.dma_start(GBC[:, :], io["norm_cross"][0:1, :].broadcast_to([P, D])).then_inc(gain_in["cross"], 16)
            for p in range(4 * NJ + NRAW, N_LIN + NRAW):
                load(p)
            sp.wait_ge(c_lo, NT)
            sp.dma_start(GBF[:, :], io["norm_ffn"][0:1, :].broadcast_to([P, D])).then_inc(gain_in["ffn"], 16)
            sp.dma_start(GBL[:, :], io["norm_final"].rearrange("(a d) -> a d", a=1).broadcast_to([P, D])).then_inc(gain_in["final"], 16)
            for p in range(N_LIN + NRAW, len(pieces)):
                load(p)
            for tt in range(NT):
                sp.wait_ge(l_o, tt + 1)
                sp.dma_start(out[0, tt * P:(tt + 1) * P, :], FO[:, tt % 2]).then_inc(out_done[tt % 2], 16)
            for s in out_done:
                sp.wait_ge(s, 8 * NT)

        @block.gpsimd
        def _(pool):
            chain = [0]

            def link(ins):
                chain[0] += 1
                ins.then_inc(pool_chain, 1)
                pool.wait_ge(pool_chain, chain[0])

            pool.dma_start(VROWS[0:24, :], io["rwkv_conv"][0].rearrange("j (c p) -> (j c) p", p=P)).then_inc(vecs_in, 16)
            pool.dma_start(VROWS[24:28, :], io["rwkv_w0"][0].rearrange("d (c p) -> (d c) p", p=P)).then_inc(vecs_in, 16)
            pool.dma_start(VROWS[28:32, :], io["rwkv_a0"][0].rearrange("d (c p) -> (d c) p", p=P)).then_inc(vecs_in, 16)
            pool.dma_start(VROWS[32:34, :], io["rwkv_k_k"].rearrange("l (c p) -> (l c) p", p=P)).then_inc(vecs_in, 16)
            pool.dma_start(VROWS[34:36, :], io["rwkv_k_a"].rearrange("l (c p) -> (l c) p", p=P)).then_inc(vecs_in, 16)
            pool.dma_start(VROWS[36:38, :], io["rwkv_r_k"][0].rearrange("(c h) p -> c (h p)", h=2)).then_inc(vecs_in, 16)
            pool.dma_start(WA[0:64], io["rwkv_w_up"][0].rearrange("d l c -> l d c")).then_inc(vecs_in, 16)
            pool.dma_start(WA[64:128], io["rwkv_a_up"][0].rearrange("d l c -> l d c")).then_inc(vecs_in, 16)
            for b in range(2):
                def halves(dst, src):
                    return dst.rearrange("p (b a k) -> p b a k", b=2, a=2)[:, b], src.rearrange("l (a b k) -> l b a k", a=2, b=2)[:, b]

                pool.dma_start(*halves(GU[:, :], io["rwkv_g_up"][0])).then_inc(vecs_in, 16)
                pool.dma_start(*halves(LNG, io["rwkv_ln_g"].broadcast_to([P, 256]))).then_inc(vecs_in, 16)
                pool.dma_start(*halves(LNB, io["rwkv_ln_b"].broadcast_to([P, 256]))).then_inc(vecs_in, 16)
            pool.dma_start(SUB, io["diff_subln"].broadcast_to([P, 128])).then_inc(vecs_in, 16)
            pool.dma_start(SINK, io["win_sink"].broadcast_to([P, 4])).then_inc(vecs_in, 16)
            for i, k in enumerate(("diff_lq1", "diff_lk1", "diff_lq2", "diff_lk2")):
                pool.dma_start(LQ[i], io[k].broadcast_to([P, 64])).then_inc(vecs_in, 16)

            def lo(p):
                pool.wait_ge(w_hi, p + 1)
                pool.tensor_tensor(WL[:, p % NW], RAW[:, p % NRAW], WH[:, p % NW].bitcast(F32), ALU.subtract).then_inc(w_lo, 1)

            for p in range(24):
                lo(p)
            pool.dma_start(TAB[:, :], io["dist"]).then_inc(tab_in, 16)
            for p in range(24, 4 * NJ):
                lo(p)
            pool.wait_ge(w_used, 4 * NJ)
            pool.dma_start(WB_[:, :, :], io["win_bias"].rearrange("p (h k) -> p h k", h=4)).then_inc(wb_in, 16)
            pool.memset(CIN[:, :, 0:1], 0.0)
            pool.memset(CIN[:, :, T + 1:T + 2], 0.0).then_inc(pads, 1)
            for p in range(4 * NJ, 4 * NJ + NRAW):
                lo(p)
            for d in range(2):
                if d == 0:
                    pool.wait_ge(w_mix, NT)
                else:
                    pool.wait_ge(g_act, G_ACT * NB)
                    pool.wait_ge(g_pe, G_PE * NB)
                    pool.wait_ge(g_dve, G_DVE * NB)
                link(pool.memset(SCM[:, :], 1.0))
                pool.memset(SCM[:, 0:T:C], 0.0).then_inc(r_scm, 1)
                for b in range(NB):
                    n = d * NB + b
                    pool.wait_ge(g_dve, G_DVE * n + 1)
                    if n:
                        pool.wait_ge(g_pe, G_PE * n - 2)
                    abt = G1[:, :, 0, :, 0, :]
                    link(pool.tensor_tensor(QT0[:, :].rearrange("p (a b) k -> p a b k", b=2), abt,
                                            CN[:, C_LT[d]:C_LT[d] + 64].unsqueeze(1).unsqueeze(1).broadcast_to([P, 4, 2, 64]), ALU.mult))
                    pool.tensor_tensor(QQ[:, 1], QT0[:, :], I64.unsqueeze(1).broadcast_to([P, 8, 64]), ALU.subtract).then_inc(g_pool, 1)
                    for l, s in enumerate(LEVELS):
                        if l:
                            pool.wait_ge(g_pe, G_PE * n + 5 + 2 * (l - 1) + 1)
                        m0 = C_LT[d] + 64 * (l + 1)
                        pool.tensor_tensor(LT[:, :].rearrange("p (a b) k -> p a b k", b=2), abt,
                                           CN[:, m0:m0 + 64].unsqueeze(1).unsqueeze(1).broadcast_to([P, 4, 2, 64]), ALU.mult).then_inc(g_pool, 1)
            for p in range(4 * NJ + NRAW, len(pieces)):
                lo(p)

        @block.scalar
        def _(act):
            chain = [0]
            done_hi = [0]

            def link(ins):
                chain[0] += 1
                ins.then_inc(act_chain, 1)
                act.wait_ge(act_chain, chain[0])

            def hi(upto):
                while done_hi[0] < min(upto, len(pieces)):
                    p = done_hi[0]
                    act.wait_ge(raw_full[p % NRAW], 16 * (p // NRAW + 1))
                    if p >= NW:
                        act.wait_ge(w_used, p - NW + 1)
                        act.wait_ge(w_lo, p - NW + 1)
                    act.activation(WH[:, p % NW], RAW[:, p % NRAW], ACT.Copy).then_inc(w_hi, 1)
                    done_hi[0] += 1

            def norm(nn, src, junk, S, hdst, wait_src, width=P, dim=D):
                def stat(tt):
                    wait_src(tt)
                    if tt >= 2:
                        act.wait_ge(nn.tr, 2 * (tt - 1))
                    link(act.activation(junk(tt), src(tt), ACT.Square, accum_out=S[:, tt:tt + 1]))
                    act.activation(S[:, tt:tt + 1], S[:, tt:tt + 1], ACT.Sqrt, bias=RMS_EPS, scale=1.0 / dim).then_inc(nn.std, 1)

                stat(0)
                for tt in range(nn.n):
                    if tt + 1 < nn.n:
                        stat(tt + 1)
                    for b in range(2):
                        act.wait_ge(nn.tr, 2 * tt + b + 1)
                        act.activation(hdst(tt, b), PS[:, 2 * (tt % 4) + b, :].rearrange("p (k t) -> p k t", k=4), ACT.Copy).then_inc(nn.hi, 1)

            hi(NRAW)
            norm(n1, lambda tt: XT[:, tt % 2], lambda tt: XN[:, tt % 2], SS,
                 lambda tt, b: HH[:, 4 * b:4 * b + 4, tt * P:(tt + 1) * P],
                 lambda tt: (act.wait_ge(vec_t, 1), act.wait_ge(n1.full[tt % 2], 16 * (tt // 2 + 1))))

            def evac_proj(j):
                c0 = proj_cols[j]
                act.wait_ge(w_used, 4 * (j + 1))
                bank = [PS[:, 4 * (j % 2) + i, :] for i in range(4)]
                for i in range(4):
                    ct, half = i // 2, i % 2
                    t0 = half * 512
                    if BQ0 <= c0 < BK0:
                        k = (c0 - BQ0) // P + ct
                        act.activation(BQ[:, k, t0:t0 + 512], bank[i], ACT.Copy, scale=0.125).then_inc(job_evac, 1)
                    elif BK0 <= c0 < BV0:
                        k = (c0 - BK0) // P + ct
                        act.activation(BK[:, k, t0:t0 + 512], bank[i], ACT.Copy).then_inc(job_evac, 1)
                    elif BV0 <= c0 < CI0:
                        act.activation(BV[:, 2 * i:2 * i + 2, c0 - BV0:c0 - BV0 + PW], bank[i].rearrange("p (t c) -> p t c", t=2),
                                       ACT.Copy).then_inc(job_evac, 1)
                    elif c0 >= CI0:
                        k = (c0 - CI0) // P + ct
                        act.activation(CIN[:, k, 1 + t0:1 + t0 + 512], bank[i], ACT.Copy).then_inc(job_evac, 1)
                    elif c0 == AQ0:
                        act.activation(AQ[:, ct, t0:t0 + 512], bank[i], ACT.Copy, scale=0.125).then_inc(job_evac, 1)
                    elif i < 2:
                        t0 = i * 512
                        act.activation(AK[0:64, 0, t0:t0 + 512], bank[i][0:64], ACT.Copy)
                        act.activation(AK[64:128, 0, t0:t0 + 512], bank[i][0:64], ACT.Copy)
                        act.activation(AK[0:64, 1, t0:t0 + 512], bank[i][64:128], ACT.Copy)
                        act.activation(AK[64:128, 1, t0:t0 + 512], bank[i][64:128], ACT.Copy).then_inc(job_evac, 1)
                    else:
                        act.activation(AV[:, 4 * (i - 2):4 * (i - 2) + 4, :], bank[i].rearrange("p (t c) -> p t c", t=4),
                                       ACT.Copy).then_inc(job_evac, 1)

            for j in range(6):
                hi(min(4 * j + 10, 24 + NW))
                evac_proj(j)

            act.wait_ge(lam_s, 1)
            act.activation(LAM[:, 0:2], LAM[:, 0:2], ACT.Exp).then_inc(lam_e, 1)

            def d_exp(u):
                for c in range(2):
                    n = 2 * u + c
                    act.wait_ge(nm_done, n + 1)
                    e = E_[:, n % 4, :]
                    if u >= 2:
                        act.wait_ge(comb_done, u - 1)
                    act.activation(e, e, ACT.Exp, bias=NMD[:, n % 4:n % 4 + 1], accum_out=LD[:, n % 4:n % 4 + 1]).then_inc(exp_done, 1)

            def d_head(h):
                act.wait_ge(o_evac, 8 * h + 8)
                sq = BQ[:, h, :].rearrange("p (t c) -> p t c", t=NT)
                act.activation(sq, OB[:, h % 2], ACT.Square).then_inc(sq_done, 1)
                act.wait_ge(hs_done, h + 1)
                act.activation(HS, HS, ACT.Sqrt, bias=RMS_EPS, scale=1.0 / 128).then_inc(hstd, 1)
                for b in range(2):
                    act.wait_ge(ht_done, 2 * h + b + 1)
                    act.activation(MIX[:, h, b * 512:b * 512 + 512], PS[:, 7, :], ACT.Copy).then_inc(hm_evac, 1)

            d_exp(0)
            for u in range(32):
                h, qb = u // 8, u % 8
                if u + 1 < 32:
                    d_exp(u + 1)
                for b in range(2):
                    act.wait_ge(tr_done, 2 * u + b + 1)
                    if u and b == 0:
                        act.wait_ge(pv_done, u)
                    act.activation(AT_[:, b * 512:b * 512 + 512], PS[:, 4 + b, :], ACT.Copy).then_inc(at_evac, 1)
                act.wait_ge(pv_done, u + 1)
                if h >= 2 and qb == 0:
                    act.wait_ge(hn_done, h - 1)
                act.activation(OB[:, h % 2, qb, :], PS[:, 6, 0:128], ACT.Copy, scale=CO[:, 4 * (u % 2):4 * (u % 2) + 1]).then_inc(o_evac, 1)
                if qb == 1 and h:
                    d_head(h - 1)
            d_head(3)

            for j in range(6, NJ):
                hi(min(4 * j + 10, 4 * NJ + NRAW))
                evac_proj(j)
            hi(4 * NJ + NRAW)

            for qb in range(NT):
                lo_, hi_ = max(0, qb - 1), min(NT - 1, qb + 1)
                n = (hi_ - lo_ + 1) * P
                act.wait_ge(w_nm, qb + 1)
                for h in range(4):
                    act.activation(WP_[:, h, 0:n], WP_[:, h, 0:n], ACT.Exp, bias=WM[:, h:h + 1], accum_out=WL4[:, h:h + 1])
                act.activation(WD4, WD4, ACT.Exp).then_inc(w_exp, 1)
                act.wait_ge(w_tr, qb + 1)
                if qb:
                    act.wait_ge(w_pv, qb)
                for b in range(3):
                    a = act.activation(WT_[:, 4 * b:4 * b + 4, :], PS[:, 4 + b, :].rearrange("p (k q) -> p k q", k=4), ACT.Copy)
                a.then_inc(w_pt, 1)
                act.wait_ge(w_ot, qb + 1)
                act.activation(MIX[:, 4:6, qb * P:(qb + 1) * P], PS[:, 7, 256:512].rearrange("p (k q) -> p k q", k=2), ACT.Copy).then_inc(w_mix, 1)

            act.wait_ge(r_conv, 1)
            for tt in range(NT):
                act.wait_ge(r_vt, tt // 2 + 1)
                act.activation(VT[:, tt].rearrange("p b a k -> p a b k"),
                               PS[:, tt // 2, 256 * (tt % 2):256 * (tt % 2) + 256].rearrange("p (a b k) -> p a b k", a=2, b=2),
                               ACT.Copy).then_inc(r_vte, 1)
            act.wait_ge(r_sq, 1)
            act.activation(S1_[:, :, :], KK[:, :, :], ACT.Square).then_inc(r_act, 1)
            act.activation(CV[0:64, 6, :], CV[0:64, 6, :], ACT.Tanh).then_inc(r_act, 1)
            act.activation(CV[:, 7, :], CV[:, 7, :], ACT.Sigmoid).then_inc(r_act, 1)
            act.wait_ge(r_kn, 1)
            act.activation(S2_[:, :, :].rearrange("p a (b c) -> p (a b) c", c=512), PS[:, 4:8, :], ACT.Sqrt).then_inc(r_std, 1)

            for d in range(2):
                act.wait_ge(r_z, d + 1)
                if d == 0:
                    act.wait_ge(r_kk, 1)
                for ct in range(2):
                    act.activation(S1_[:, ct, :].rearrange("p (b c) -> p b c", c=512), PS[:, 2 * ct:2 * ct + 2, :], ACT.Sigmoid, bias=col(PTC_W0 + 2 * d + ct))
                for ct in range(2):
                    a = act.activation(S3_[:, ct, :].rearrange("p (b c) -> p b c", c=512), PS[:, 4 + 2 * ct:6 + 2 * ct, :], ACT.Sigmoid, bias=col(PTC_A0 + 2 * d + ct))
                a.then_inc(r_sig, 1)
                act.wait_ge(r_c, d + 1)
                c1, cx = ((S2_, 1.0), (S1_, 1.0)) if d == 0 else ((S1_, -1.0), (S2_, -1.0))

                def v4(t):
                    return t[:, :, :].rearrange("p a (c k) -> p (a c) k", k=C)

                act.activation(KR[:, 1].rearrange("p a c k -> p (a c) k"), v4(c1[0]), ACT.Exp, scale=c1[1])
                act.activation(BKt[:, 0].rearrange("p a c k -> p (a c) k"), v4(c1[0]), ACT.Exp, scale=-c1[1])
                act.activation(KR[:, 0].rearrange("p a c k -> p (a c) k"), v4(cx[0]), ACT.Exp, scale=cx[1])
                act.activation(EH[:, :], HT[:, :], ACT.Exp).then_inc(r_exp, 1)
                for b in range(NB):
                    n = d * NB + b
                    pe0, ac0 = G_PE * n, G_ACT * n
                    act.wait_ge(g_pe, pe0 + 3)
                    act.activation(RH[:, :, 0, :], PS[:, 6, :].rearrange("p (u k) -> p u k", k=C), ACT.Copy).then_inc(g_act, 1)
                    act.activation(BT[:, :, :], PS[:, 7, :].rearrange("p (u k) -> p u k", k=C), ACT.Copy).then_inc(g_act, 1)
                    act.wait_ge(g_pe, pe0 + 4)
                    act.activation(KT[:, :, :], PS[:, 0, :].rearrange("p (u k) -> p u k", k=C), ACT.Copy).then_inc(g_act, 1)
                    act.wait_ge(g_pe, pe0 + 5)
                    act.activation(RH[:, :, 1, :], PS[:, 1, :].rearrange("p (u k) -> p u k", k=C), ACT.Copy).then_inc(g_act, 1)
                    for l in range(5):
                        act.wait_ge(g_pe, pe0 + 5 + 2 * l + 1)
                        act.activation(XX[:, :, :], PS[:, 2, :].rearrange("p (u k) -> p u k", k=C), ACT.Copy).then_inc(g_act, 1)
                    act.wait_ge(g_pe, pe0 + 16)
                    act.activation(WU[:, :, :, :].rearrange("p (a u) b k -> p a (u b k)", a=2), PS[:, 5:7, :], ACT.Copy).then_inc(g_act, 1)
                    act.wait_ge(g_pe, pe0 + 17)
                    for cp in range(2):
                        a = act.activation(BKt[:, 1, :, 4 * b + cp:4 * b + 4:2, :].rearrange("p a t k -> p t a k"),
                                           PS[:, 2 + cp, 0:256].rearrange("p (t a k) -> p t a k", t=2, a=2), ACT.Copy)
                    a.then_inc(g_act, 1)

            act.wait_ge(p_s, 1)
            act.activation(S2_[:, :, :].rearrange("p a b -> p (a b)"), YY[:, :, :, :, :].rearrange("p t a b k -> p (t a b k)"), ACT.Square).then_inc(p_std, 1)
            act.wait_ge(p_s, 2)
            act.activation(GV, GV, ACT.Sqrt, bias=GN_EPS, scale=1.0 / C).then_inc(p_std, 1)
            act.wait_ge(p_mm, 1)
            act.activation(BON, PS[:, 2, 0:32], ACT.Copy).then_inc(p_bon, 1)
            for ct in range(2):
                for half in range(2):
                    act.wait_ge(p_tr, 2 * ct + half + 1)
                    act.activation(MIX[:, 6 + ct, half * 512:half * 512 + 512], PS[:, 2 * ct + half, :], ACT.Copy).then_inc(p_mix, 1)
            for k in range(8):
                src = (4, 5, 0, 1, 2, 3, 6, 7)[k]
                if k == 6:
                    act.wait_ge(p_mix, 4)
                if k == 0:
                    act.wait_ge(p_tr, 4)
                act.activation(HH[:, k, :], MIX[:, src, :], ACT.Copy).then_inc(mix_hi, 1)

            def from_dram(nn):
                return lambda tt: act.wait_ge(nn.full[tt % 2], 16 * (tt // 2 + 1))

            hi(4 * NJ + NW)
            act.wait_ge(mix_lo, 8)
            norm(nm, lambda tt: MX[:, tt], lambda tt: XN2[:, tt], MS,
                 lambda tt, b: AH[:, :, :].rearrange("p a (k t) -> p (a k) t", k=4)[:, 4 * b:4 * b + 4, tt * P:(tt + 1) * P], from_dram(nm))

            def evac2(j):
                kind, i = jobs2[j]
                bank = 4 * (j % 2)
                act.wait_ge(w_used, end2[j])
                if kind == "wkv" and i < 2:
                    act.activation(KM[:, 2 * i:2 * i + 2, :], PS[:, bank, :].rearrange("p (c t) -> p c t", c=2), ACT.Copy).then_inc(job2_act, 1)
                elif kind == "wkv":
                    act.activation(VM[:, :, (i - 2) * PW:(i - 1) * PW], PS[:, bank, :].rearrange("p (t c) -> p t c", t=2), ACT.Copy).then_inc(job2_act, 1)
                elif kind == "wq":
                    act.activation(QC[:, 2 * i:2 * i + 2, :].rearrange("p k (b c) -> p (k b) c", c=512), PS[:, bank:bank + 4, :], ACT.Copy).then_inc(job2_act, 1)

            p0 = 4 * NJ
            for j in range(8):
                hi(p0 + 4 * j + 10)
                if j >= 4:
                    evac2(j)
            norm(n2, lambda tt: X[:, tt], lambda tt: XN2[:, tt % 2], AS,
                 lambda tt, b: HH[:, 4 * b:4 * b + 4, tt * P:(tt + 1) * P],
                 lambda tt: act.wait_ge(job2_dve, 4))
            for j in (8, 9):
                hi(p0 + 4 * j + 10)
                evac2(j)
            sc = 128 ** -0.5
            for qb in range(NT):
                act.wait_ge(c_max, qb + 1)
                for h in range(4):
                    a = act.activation(CP[:, h * 256:h * 256 + 256], PS[:, h // 2, 256 * (h % 2):256 * (h % 2) + 256], ACT.Exp,
                                       bias=CM[:, h:h + 1], scale=sc, accum_out=CL[:, h:h + 1])
                a.then_inc(c_exp, 1)
                act.wait_ge(c_tr, qb + 1)
                if qb:
                    act.wait_ge(c_pv, qb)
                act.activation(CPT[:, :].rearrange("p (b c) -> p b c", c=512), PS[:, 2:4, :], ACT.Copy).then_inc(c_pt, 1)
                act.wait_ge(c_pv, qb + 1)
                act.activation(AH[:, :, qb * P:(qb + 1) * P], PS[:, 4, :].rearrange("p (k t) -> p k t", k=4), ACT.Copy).then_inc(c_hi, 1)
            hi(p0 + 40 + 6)
            for j in range(10, 14):
                hi(p0 + 40 + 2 * (j - 9) + 5)
            norm(n3, lambda tt: X[:, tt], lambda tt: XN2[:, tt % 2], BS,
                 lambda tt, b: HH[:, 4 * b:4 * b + 4, tt * P:(tt + 1) * P],
                 lambda tt: act.wait_ge(job2_dve, 8))
            for i in range(FF_ITERS + 1):
                q0 = ff0(i)
                if i < FF_ITERS:
                    hi(q0 + 9)
                    act.wait_ge(w_used, ff0(i) + 4)
                    for k in range(4):
                        if k == 0 and i:
                            act.wait_ge(f_mul, 4 * i)
                        act.activation(ACTB[:, k // 2, 512 * (k % 2):512 * (k % 2) + 512], PS[:, k, :], ACT.Silu).then_inc(f_silu, 1)
                    hi(q0 + 12)
                    if i >= 2:
                        act.wait_ge(w_used, ff0(i))
                    for k in range(4):
                        act.wait_ge(f_mul, 4 * i + k + 1)
                        act.activation(AH[:, 2 * (i % 2) + k // 2, 512 * (k % 2):512 * (k % 2) + 512],
                                       FU[:, k // 2, 512 * (k % 2):512 * (k % 2) + 512], ACT.Copy).then_inc(f_hi, 1)
                hi(q0 + 16)
            for tt in range(NT):
                if tt == 0:
                    act.wait_ge(f_add, 16 * FF_ITERS)
                if tt >= 2:
                    act.wait_ge(l_o, tt - 1)
                    act.wait_ge(out_done[tt % 2], 16 * (tt // 2))
                link(act.activation(FO[:, tt % 2], X[:, tt], ACT.Square, accum_out=FS[:, tt:tt + 1]))
                act.activation(FS[:, tt:tt + 1], FS[:, tt:tt + 1], ACT.Sqrt, bias=RMS_EPS, scale=1.0 / D).then_inc(l_std, 1)

        @block.vector
        def _(dve):
            chain = [0]

            def link(ins):
                chain[0] += 1
                ins.then_inc(dve_chain, 1)
                dve.wait_ge(dve_chain, chain[0])

            TT, TS, STT = dve.tensor_tensor, dve.tensor_scalar, dve.scalar_tensor_tensor

            def norm(nn, src, dst, S, R, gb, gain, hdst, ldst):
                def scale(tt):
                    dve.wait_ge(nn.std, tt + 1)
                    link(dve.reciprocal(R[:, tt:tt + 1], S[:, tt:tt + 1]))
                    if tt == 0:
                        dve.wait_ge(gain_in[gain], 16)
                    STT(dst(tt), src(tt), R[:, tt:tt + 1], gb, ALU.mult, ALU.mult).then_inc(nn.xn, 1)

                scale(0)
                for tt in range(nn.n):
                    if tt + 1 < nn.n:
                        scale(tt + 1)
                    for b in range(2):
                        dve.wait_ge(nn.hi, 2 * tt + b + 1)
                        TT(ldst(tt, b), PS[:, 2 * (tt % 4) + b, :].rearrange("p (k t) -> p k t", k=4), hdst(tt, b).bitcast(F32),
                           ALU.subtract).then_inc(nn.lo, 1)

            dve.wait_ge(vec_t, 1)
            dve.tensor_copy(PT, PS[:, 7, 0:38]).then_inc(vec_c, 1)
            dve.wait_ge(vec_c, 1)
            link(dve.memset(RB, 0.0))
            for ct in range(2):
                for hp in range(2):
                    r = slice(64 * hp, 64 * hp + 64)
                    dve.tensor_copy(RB[r, 4 * ct + 2 * hp + ct:4 * ct + 2 * hp + ct + 1], PT[r, PTC_RK + ct:PTC_RK + ct + 1])
            for i in range(2):
                link(TT(LQ[2 * i], LQ[2 * i], LQ[2 * i + 1], ALU.mult))
                s = dve.tensor_reduce(LAM[:, i:i + 1], LQ[2 * i], AX_X, ALU.add)
            s.then_inc(lam_s, 1)

            norm(n1, lambda tt: XT[:, tt % 2], lambda tt: XN[:, tt % 2], SS, RS, GB[:, :], "mix",
                 lambda tt, b: HH[:, 4 * b:4 * b + 4, tt * P:(tt + 1) * P], lambda tt, b: HL[:, 4 * b:4 * b + 4, tt * P:(tt + 1) * P])

            dve.wait_ge(lam_e, 1)
            link(TT(LAM[:, 2:3], LAM[:, 1:2], LAM[:, 0:1], ALU.subtract))
            link(TS(LAM[:, 2:3], LAM[:, 2:3], -LAM_INIT, None, ALU.add))
            dve.wait_ge(tab_in, 16)

            def d_max(u):
                h, qb = u // 8, u % 8
                if qb == 0 and h:
                    link(TS(TAB[:, :], TAB[:, :], DIFF_SLOPES[h] / DIFF_SLOPES[h - 1], None, ALU.mult))
                for c in range(2):
                    n = 2 * u + c
                    dve.wait_ge(qk_done, n + 1)
                    if u >= 2 and c == 0:
                        dve.wait_ge(tr_done, 2 * (u - 1))
                    t0 = 896 - P * qb
                    ins = dve.tensor_tensor_reduce(E_[:, n % 4, :].rearrange("p (b c) -> p b c", c=512), PS[:, 2 * c:2 * c + 2, :],
                                                   TAB[:, t0:t0 + T].rearrange("p (b c) -> p b c", c=512), 1.0, -3.0e38, ALU.add, ALU.max,
                                                   MD[:, n % 4:n % 4 + 1])
                    ins.then_inc(s_read, 1)
                    dve.wait_ge(s_read, n + 1)
                    TS(NMD[:, n % 4:n % 4 + 1], MD[:, n % 4:n % 4 + 1], -1.0, None, ALU.mult).then_inc(nm_done, 1)

            def d_head(h):
                dve.wait_ge(sq_done, h + 1)
                dve.tensor_reduce(HS, BQ[:, h, :].rearrange("p (t c) -> p t c", t=NT), AX_X, ALU.add).then_inc(hs_done, 1)
                dve.wait_ge(hstd, h + 1)
                link(dve.reciprocal(HR, HS))
                o = OB[:, h % 2]
                link(TT(o, o, HR.unsqueeze(2).broadcast_to([P, NT, 128]), ALU.mult))
                link(TS(o, o, 1.0 - LAM_INIT, None, ALU.mult))
                TT(BQ[:, h, :].rearrange("p (t c) -> p t c", t=NT), o, SUB.unsqueeze(1).broadcast_to([P, NT, 128]), ALU.mult).then_inc(hn_done, 1)

            d_max(0)
            for u in range(32):
                if u + 1 < 32:
                    d_max(u + 1)
                dve.wait_ge(exp_done, 2 * u + 2)
                k = 4 * (u % 2)
                e0, e1 = (2 * u) % 4, (2 * u + 1) % 4
                if u >= 2:
                    dve.wait_ge(o_evac, u - 1)
                link(dve.reciprocal(CO[:, k:k + 2], LD[:, e0:e0 + 2]))
                link(TS(CO[:, k + 2:k + 3], LD[:, e0:e0 + 1], CO[:, k + 1:k + 2], LAM[:, 2:3], ALU.mult, ALU.mult))
                STT(E_[:, e0, :], E_[:, e1, :], CO[:, k + 2:k + 3], E_[:, e0, :], ALU.mult, ALU.add).then_inc(comb_done, 1)
                if u % 8 == 1 and u > 8:
                    d_head(u // 8 - 1)
            d_head(3)

            dve.wait_ge(wb_in, 16)
            for qb in range(NT):
                lo_, hi_ = max(0, qb - 1), min(NT - 1, qb + 1)
                n = (hi_ - lo_ + 1) * P
                off = (lo_ - (qb - 1)) * P
                dve.wait_ge(w_qk, qb + 1)
                if qb:
                    dve.wait_ge(w_tr, qb)
                for h in range(4):
                    ins = dve.tensor_tensor_reduce(WP_[:, h, 0:n], PS[:, h, 0:n], WB_[:, h, off:off + n], 1.0, -3.0e38, ALU.add, ALU.max,
                                                   WM[:, h:h + 1])
                link(ins)
                link(TT(WM, WM, SINK, ALU.max))
                link(TT(WD4, SINK, WM, ALU.subtract))
                TS(WM, WM, -1.0, None, ALU.mult).then_inc(w_nm, 1)
                dve.wait_ge(w_exp, qb + 1)
                link(TT(WL4, WL4, WD4, ALU.add))
                link(dve.reciprocal(WR, WL4))
                dve.wait_ge(w_pv, qb + 1)
                TT(WO_[:, :].rearrange("p (h c) -> p h c", h=4), PS[:, 7, 0:256].rearrange("p (h c) -> p h c", h=4),
                   WR.unsqueeze(2).broadcast_to([P, 4, 64]), ALU.mult).then_inc(w_on, 1)

            dve.wait_ge(w_mix, NT)
            dve.wait_ge(pads, 1)
            dve.wait_ge(job_evac, 4 * NJ)
            for c in (4, 5, 2, 3, 6, 7, 0, 1):
                link(TS(CV[:, c, :], CIN[:, c, 0:T], col(PTC_CONV + c), None, ALU.mult))
                link(STT(CV[:, c, :], CIN[:, c, 1:T + 1], col(PTC_CONV + 8 + c), CV[:, c, :], ALU.mult, ALU.add))
                ins = STT(CV[:, c, :], CIN[:, c, 2:T + 2], col(PTC_CONV + 16 + c), CV[:, c, :], ALU.mult, ALU.add)
            ins.then_inc(r_conv, 1)
            dve.wait_ge(r_conv, 1)
            for ct in range(2):
                ins = TS(KK[:, ct, :], CV[:, 2 + ct, :], col(PTC_KK + ct), None, ALU.mult)
            ins.then_inc(r_sq, 1)
            dve.wait_ge(r_std, 1)
            link(TS(S2_[:, :, :], S2_[:, :, :], 1e-12, None, ALU.max))
            link(dve.reciprocal(S2_[:, :, :], S2_[:, :, :]))
            TT(KK[:, :, :], KK[:, :, :], S2_[:, :, :], ALU.mult).then_inc(r_kk, 1)

            def ch(t):
                return t[:, :, :].rearrange("p a (c k) -> p (a c) k", k=C)

            def slot(t, i):
                return t[:, i].rearrange("p a c k -> p (a c) k")

            for d in range(2):
                dve.wait_ge(r_sig, d + 1)
                link(TS(S1_[:, :, :], S1_[:, :, :], -E05, None, ALU.mult))
                dve.wait_ge(r_scm, d + 1)
                for ct in range(2):
                    ins = dve.tensor_tensor_scan(S2_[:, ct, :], SCM[:, :], S1_[:, ct, :], 0.0, ALU.mult, ALU.add)
                link(ins)
                link(TS(HT[:, :], S2_[:, :, C - 1:T:C].rearrange("p a c -> p (a c)"), 0.5, None, ALU.mult))
                link(TT(ch(S2_), ch(S2_), HT[:, :].unsqueeze(2).broadcast_to([P, 32, C]), ALU.subtract))
                TT(S1_[:, :, :], S2_[:, :, :], S1_[:, :, :], ALU.subtract).then_inc(r_c, 1)
                dve.wait_ge(r_exp, d + 1)
                for ct in range(2):
                    ins = TS(S2_[:, ct, :], S3_[:, ct, :], -1.0, col(PTC_KA + ct), ALU.add, ALU.mult)
                link(ins)
                link(STT(S2_[:, :, :], S2_[:, :, :], 1.0, CV[:, 2:4, :], ALU.add, ALU.mult))
                if d == 0:
                    dve.tensor_copy(KS[:, :, :], S2_[:, :, :])
                else:
                    TT(KS[:, :, :], KS[:, :, :], S2_[:, :, :], ALU.add)
                TT(slot(BKt, 1), ch(S2_), slot(BKt, 0), ALU.mult)
                link(TT(S3_[:, :, :], S3_[:, :, :], KK[:, :, :], ALU.mult))
                TT(slot(BKt, 0), ch(S3_), slot(BKt, 0), ALU.mult)
                TT(slot(KR, 1), slot(KR, 1), CV[:, 0:2, :].rearrange("p a (c k) -> p (a c) k", k=C), ALU.mult)
                TT(slot(KR, 0), slot(KR, 0), ch(KK), ALU.mult)
                link(dve.memset(DD[:, :], 0.0))
                e2, d2 = EH[:, :].rearrange("p (a c) -> p a c", a=2), DD[:, :].rearrange("p (a c) -> p a c", a=2)
                dst = d2[:, :, 0:15] if d == 0 else d2[:, :, 1:16]
                TT(dst, e2[:, :, 0:15], e2[:, :, 1:16], ALU.mult).then_inc(r_pre, 1)
                for b in range(NB):
                    n = d * NB + b
                    pe0, dv0 = G_PE * n, G_DVE * n
                    dve.wait_ge(g_pe, pe0 + 1)
                    for k in range(4):
                        ins = TT(G1[:, k].rearrange("p a b c k -> p (a b) (c k)"), PS[:, k, :].rearrange("p (a c) -> p a c", c=128),
                                 CN[:, C_MASK[d]:C_MASK[d] + 128].unsqueeze(1).broadcast_to([P, 4, 128]), ALU.mult)
                    ins.then_inc(g_dve, 1)
                    dve.wait_ge(g_pe, pe0 + 2)
                    q = QQ[:, 0]
                    for hp in range(2):
                        for t in range(2):
                            ins = TT(QQ[:, 0, 4 * t + 2 * hp:4 * t + 2 * hp + 2, :], PS[:, 4 + hp, 128 * t:128 * t + 128].rearrange("p (a k) -> p a k", k=C),
                                     CN[:, C_LT[1 - d]:C_LT[1 - d] + 64].unsqueeze(1).broadcast_to([P, 2, 64]), ALU.mult)
                    link(ins)
                    TT(q, q, I64.unsqueeze(1).broadcast_to([P, 8, 64]), ALU.subtract).then_inc(g_dve, 1)
                    for l in range(5):
                        dve.wait_ge(g_pe, pe0 + 7 + 2 * l)
                        if l == 0:
                            dve.wait_ge(g_pool, 6 * n + 1)
                        if l < 4:
                            qq = QQ[:, :, :, :].rearrange("p a u k -> p a (u k)")
                            TT(qq, PS[:, 3:5, :], qq, ALU.add).then_inc(g_dve, 1)
                        else:
                            qq = QQ[:, 1].rearrange("p u k -> p (u k)")
                            TT(qq, PS[:, 4, :], qq, ALU.add).then_inc(g_dve, 1)
                    dve.wait_ge(g_pe, pe0 + 17)
                    for cp in range(2):
                        cs = slice(4 * b + cp, 4 * b + 4, 2)
                        g = KR[:, 1, :, cs, :].rearrange("p a t k -> p t a k")
                        TT(g, PS[:, cp, 0:256].rearrange("p (t a k) -> p t a k", t=2, a=2), g, ALU.add)
                        m = BKt[:, 0, :, cs, :].rearrange("p a t k -> p t a k")
                        TT(m, PS[:, cp, 256:512].rearrange("p (t a k) -> p t a k", t=2, a=2),
                           I64.unsqueeze(1).unsqueeze(1).broadcast_to([P, 2, 2, 64]), ALU.add)
                    dve.wait_ge(g_pe, pe0 + 18)
                    y = YY[:, 2 * b:2 * b + 2].rearrange("p t b a k -> p (t b a k)")
                    if d == 0:
                        dve.tensor_copy(y, PS[:, 7, :]).then_inc(g_dve, 1)
                    else:
                        TT(y, PS[:, 7, :], y, ALU.add).then_inc(g_dve, 1)
                dve.wait_ge(g_act, G_ACT * NB * (d + 1))
                dve.wait_ge(g_dve, G_DVE * NB * (d + 1))
                order = list(range(NCH)) if d == 0 else list(range(NCH - 1, -1, -1))
                link(TT(slot(BKt, 1), slot(BKt, 1), DD[:, :].unsqueeze(2).broadcast_to([P, 32, C]), ALU.mult))
                dve.memset(KR[:, 0, :, order[0], :], 0.0)
                dve.tensor_copy(KR[:, 0, :, order[1], :], BKt[:, 1, :, order[0], :]).then_inc(c_z, 1)
                for i in range(1, NCH - 1):
                    dve.wait_ge(c_mm, 14 * d + i)
                    for ct in range(2):
                        ins = STT(KR[:, 0, ct, order[i + 1], :], PS[:, 0, 64 * ct:64 * ct + 64], DD[:, 16 * ct + order[i]:16 * ct + order[i] + 1],
                                  BKt[:, 1, ct, order[i], :], ALU.mult, ALU.add)
                    ins.then_inc(c_z, 1)
                for q4 in range(2):
                    dve.wait_ge(y_mm, 2 * d + q4 + 1)
                    for hp in range(2):
                        y = YY[:, 4 * q4:4 * q4 + 4, hp].rearrange("p t a k -> p t (a k)")
                        TT(y, PS[:, 2 + 2 * q4 + hp, :].rearrange("p (t c) -> p t c", t=4), y, ALU.add).then_inc(y_add, 1)
            dve.wait_ge(y_add, 8)
            TT(CV[:, 0:2, :], CV[:, 0:2, :], KS[:, :, :], ALU.mult).then_inc(p_bon, 1)
            y32 = YY[:, :, :, :, :].rearrange("p t b a k -> p (t b a) k")
            y8 = YY[:, :, :, :, :].rearrange("p t b a k -> p t (b a k)")
            v32 = VT[:, :, :, :, :].rearrange("p t b a k -> p (t b a) k")
            link(dve.tensor_reduce(GM, y32, AX_X, ALU.add))
            link(TS(GM, GM, 1.0 / C, None, ALU.mult))
            TT(y32, y32, GM.unsqueeze(2).broadcast_to([P, 32, C]), ALU.subtract).then_inc(p_s, 1)
            dve.wait_ge(p_std, 1)
            dve.tensor_reduce(GV, S2_[:, :, :].rearrange("p a (c k) -> p (a c) k", k=C), AX_X, ALU.add).then_inc(p_s, 1)
            dve.wait_ge(p_std, 2)
            link(dve.reciprocal(GS, GV))
            link(TT(y32, y32, GS.unsqueeze(2).broadcast_to([P, 32, C]), ALU.mult))
            link(TT(y8, y8, LNG.unsqueeze(1).broadcast_to([P, NT, 256]), ALU.mult))
            link(TT(y8, y8, LNB.unsqueeze(1).broadcast_to([P, NT, 256]), ALU.add))
            dve.wait_ge(p_bon, 2)
            link(TT(v32, v32, BON.unsqueeze(2).broadcast_to([P, 32, C]), ALU.mult))
            link(TT(y32, y32, v32, ALU.add))
            dve.wait_ge(p_mm, 2)
            gate = PS[:, 4:8, :].rearrange("p n (t b a k) -> p (n t) b a k", t=2, b=2, a=2)
            for hp in range(2):
                ins = TT(YF[:, :, :, hp, :], gate[:, :, hp], YY[:, :, hp], ALU.mult)
            ins.then_inc(p_y, 1)
            dve.wait_ge(p_tr, 4)
            for k in range(8):
                src = (4, 5, 0, 1, 2, 3, 6, 7)[k]
                dve.wait_ge(mix_hi, k + 1)
                TT(HL[:, k, :], MIX[:, src, :], HH[:, k, :].bitcast(F32), ALU.subtract).then_inc(mix_lo, 1)
            mt = "p a (k t) -> p (a k) t"
            norm(nm, lambda tt: MX[:, tt], lambda tt: XN2[:, tt], MS, MR, GBM[:, :], "mem",
                 lambda tt, b: AH[:, :, :].rearrange(mt, k=4)[:, 4 * b:4 * b + 4, tt * P:(tt + 1) * P],
                 lambda tt, b: AL[:, :, :].rearrange(mt, k=4)[:, 4 * b:4 * b + 4, tt * P:(tt + 1) * P])

            def add_x(j, i):
                dve.wait_ge(w_used, end2[j])
                for k in range(4):
                    xs = X[:, 2 * k:2 * k + 2, i * PW:(i + 1) * PW]
                    ins = TT(xs, PS[:, 4 * (j % 2) + k, :].rearrange("p (t c) -> p t c", t=2), xs, ALU.add)
                ins.then_inc(job2_dve, 1)

            dve.wait_ge(x_in, 16 * NT)
            for i in range(4):
                add_x(i, i)
            dve.wait_ge(job2_dve, 4)
            norm(n2, lambda tt: X[:, tt], lambda tt: XN2[:, tt % 2], AS, AR, GBC[:, :], "cross",
                 lambda tt, b: HH[:, 4 * b:4 * b + 4, tt * P:(tt + 1) * P], lambda tt, b: HL[:, 4 * b:4 * b + 4, tt * P:(tt + 1) * P])
            for qb in range(NT):
                dve.wait_ge(c_qk, qb + 1)
                link(dve.tensor_reduce(CM, PS[:, 0:2, :].rearrange("p b (h c) -> p (b h) c", h=2), AX_X, ALU.max))
                TS(CM, CM, -(128 ** -0.5), None, ALU.mult).then_inc(c_max, 1)
                dve.wait_ge(c_exp, qb + 1)
                link(dve.reciprocal(CR, CL))
                p4 = CP[:, :].rearrange("p (h c) -> p h c", h=4)
                TT(p4, p4, CR.unsqueeze(2).broadcast_to([P, 4, 256]), ALU.mult).then_inc(c_p, 1)
                dve.wait_ge(c_hi, qb + 1)
                TT(AL[:, :, qb * P:(qb + 1) * P], PS[:, 4, :].rearrange("p (k t) -> p k t", k=4),
                   AH[:, :, qb * P:(qb + 1) * P].bitcast(F32), ALU.subtract).then_inc(c_lo, 1)
            for i in range(4):
                add_x(10 + i, i)
            dve.wait_ge(job2_dve, 8)
            norm(n3, lambda tt: X[:, tt], lambda tt: XN2[:, tt % 2], BS, BR, GBF[:, :], "ffn",
                 lambda tt, b: HH[:, 4 * b:4 * b + 4, tt * P:(tt + 1) * P], lambda tt, b: HL[:, 4 * b:4 * b + 4, tt * P:(tt + 1) * P])
            for i in range(FF_ITERS + 1):
                if i < FF_ITERS:
                    dve.wait_ge(w_used, ff0(i) + 8)
                    for k in range(4):
                        c0 = 512 * (k % 2)
                        dve.wait_ge(f_silu, 4 * i + k + 1)
                        if i:
                            dve.wait_ge(f_lo, 4 * (i - 1) + k + 1)
                        TT(FU[:, k // 2, c0:c0 + 512], PS[:, 4 + k, :], ACTB[:, k // 2, c0:c0 + 512], ALU.mult).then_inc(f_mul, 1)
                    for k in range(4):
                        c0, a = 512 * (k % 2), 2 * (i % 2) + k // 2
                        dve.wait_ge(f_hi, 4 * i + k + 1)
                        TT(AL[:, a, c0:c0 + 512], FU[:, k // 2, c0:c0 + 512], AH[:, a, c0:c0 + 512].bitcast(F32), ALU.subtract).then_inc(f_lo, 1)
                if i:
                    for s in range(4):
                        dve.wait_ge(w_used, ff0(i) + (8 if i < FF_ITERS else 0) + s + 1)
                        if i > 1:
                            dve.wait_ge(f_add, 16 * (i - 2) + 4 * s + 4)
                        for k in range(4):
                            xs = X[:, 2 * k:2 * k + 2, s * PW:(s + 1) * PW]
                            TT(xs, PS[:, 4 * (s % 2) + k, :].rearrange("p (t c) -> p t c", t=2), xs, ALU.add).then_inc(f_add, 1)
            dve.wait_ge(gain_in["final"], 16)
            for tt in range(NT):
                dve.wait_ge(l_std, tt + 1)
                link(dve.reciprocal(FR[:, tt:tt + 1], FS[:, tt:tt + 1]))
                STT(FO[:, tt % 2], X[:, tt], FR[:, tt:tt + 1], GBL[:, :], ALU.mult, ALU.mult).then_inc(l_o, 1)

        @block.tensor
        def _(pe):
            piece = [0]

            def take():
                p = piece[0]
                piece[0] += 1
                pe.wait_ge(w_hi, p + 1)
                pe.wait_ge(w_lo, p + 1)
                return WH[:, p % NW], WL[:, p % NW]

            def feature_job(npieces, ah, al, where, starts=lambda ct, i: True, cts=(0, 1), cols=((0, 512), (512, 512)), extra=None):
                for q in range(npieces):
                    wh, wl = take()
                    for k in range(PK):
                        kt = q * PK + k
                        first, last = kt == 0, kt == npieces * PK - 1
                        for ct in cts:
                            c = slice(ct * P, ct * P + P)
                            for i, (t0, n) in enumerate(cols):
                                pe.matmul(where(ct, i), wh[:, k, c], ah(kt)[:, t0:t0 + n], start=first and starts(ct, i), stop=False, skip_group_check=True)
                                pe.matmul(where(ct, i), wh[:, k, c], al(kt)[:, t0:t0 + n], start=False, stop=False, skip_group_check=True)
                            for i, (t0, n) in enumerate(cols):
                                mm = pe.matmul(where(ct, i), wl[:, k, c], ah(kt)[:, t0:t0 + n], start=False, stop=last, skip_group_check=True)
                        if extra:
                            mm = extra(wh, wl, k, kt, first, last)
                    mm.then_inc(w_used, 1)

            def token_mm(dst, wh, wl, ah, al, kt, tt, start, last):
                t = slice(tt * P, tt * P + P)
                pe.matmul(dst, ah(kt)[:, t], wh, start=start, stop=False, skip_group_check=True)
                pe.matmul(dst, ah(kt)[:, t], wl, start=False, stop=False, skip_group_check=True)
                return pe.matmul(dst, al(kt)[:, t], wh, start=False, stop=last, skip_group_check=True)

            def token_job(npieces, ah, al, bank, nt=NT):
                for q in range(npieces):
                    wh, wl = take()
                    for k in range(PK):
                        kt = q * PK + k
                        for tt in range(nt):
                            mm = token_mm(PS[:, bank + tt // 2, 256 * (tt % 2):256 * (tt % 2) + 256], wh[:, k, :], wl[:, k, :], ah, al, kt, tt,
                                          kt == 0 and tt % 2 == 0, kt == npieces * PK - 1)
                    mm.then_inc(w_used, 1)

            def norm(nn, src):
                for tt in range(nn.n):
                    pe.wait_ge(nn.xn, tt + 1)
                    for b in range(2):
                        if tt >= 4:
                            pe.wait_ge(nn.lo, 2 * (tt - 4) + b + 1)
                        for k in range(4):
                            kt = 4 * b + k
                            mm = pe.transpose(PS[:, 2 * (tt % 4) + b, k * P:(k + 1) * P], src(tt)[:, kt * P:(kt + 1) * P], ID)
                        mm.then_inc(nn.tr, 1)
                pe.wait_ge(nn.lo, 2 * nn.n)

            hh, hl = (lambda kt: HH[:, kt, :]), (lambda kt: HL[:, kt, :])

            pe.wait_ge(consts_in, 16)
            pe.wait_ge(vecs_in, 16 * 20)
            pe.transpose(PS[:, 7, 0:38], VROWS, ID[0:38, 0:38]).then_inc(vec_t, 1)
            pe.wait_ge(vec_c, 1)
            norm(n1, lambda tt: XN[:, tt % 2])

            def proj(j):
                if j >= 2:
                    pe.wait_ge(job_evac, 4 * (j - 1))
                c0, bank = proj_cols[j], 4 * (j % 2)
                if BV0 <= c0 < CI0:
                    token_job(4, hh, hl, bank)
                elif c0 == AK0:
                    def values(wh, wl, k, kt, first, last):
                        for tt in range(NT):
                            mm = token_mm(PS[:, bank + 2 + tt // 4, P * (tt % 4):P * (tt % 4) + P], wh[:, k, P:2 * P], wl[:, k, P:2 * P], hh, hl, kt, tt,
                                          first and tt % 4 == 0, last)
                        return mm

                    feature_job(4, hh, hl, lambda ct, i: PS[:, bank + i, :], cts=(0,), extra=values)
                else:
                    feature_job(4, hh, hl, lambda ct, i: PS[:, bank + 2 * ct + i, :])

            for j in range(6):
                proj(j)

            pe.wait_ge(job_evac, 24)

            def d_scores(u):
                h, qb = u // 8, u % 8
                for c in range(2):
                    if u:
                        pe.wait_ge(s_read, 2 * (u - 1) + c + 1)
                    r = slice(64 * c, 64 * c + 64)
                    for half in range(2):
                        mm = pe.matmul(PS[:, 2 * c + half, :], BQ[r, h, qb * P:(qb + 1) * P], BK[r, h, 512 * half:512 * half + 512], start=True, stop=True)
                    mm.then_inc(qk_done, 1)

            def d_head(h):
                pe.wait_ge(hn_done, h + 1)
                for b in range(2):
                    if b or h:
                        pe.wait_ge(hm_evac, 2 * h + b)
                    for k in range(4):
                        tt = 4 * b + k
                        mm = pe.transpose(PS[:, 7, k * P:(k + 1) * P], BQ[:, h, tt * P:(tt + 1) * P], ID)
                    mm.then_inc(ht_done, 1)

            d_scores(0)
            for u in range(32):
                h, qb = u // 8, u % 8
                if u + 1 < 32:
                    d_scores(u + 1)
                pe.wait_ge(comb_done, u + 1)
                for b in range(2):
                    if u:
                        pe.wait_ge(at_evac, 2 * (u - 1) + b + 1)
                    for k in range(4):
                        kt = 4 * b + k
                        mm = pe.transpose(PS[:, 4 + b, k * P:(k + 1) * P], E_[:, (2 * u) % 4, kt * P:(kt + 1) * P], ID)
                    mm.then_inc(tr_done, 1)
                pe.wait_ge(at_evac, 2 * u + 2)
                if u:
                    pe.wait_ge(o_evac, u)
                for kt in range(NT):
                    mm = pe.matmul(PS[:, 6, 0:P], AT_[:, kt * P:(kt + 1) * P], BV[:, kt, h * P:(h + 1) * P], start=(kt == 0), stop=(kt == NT - 1))
                mm.then_inc(pv_done, 1)
                if qb == 1 and h:
                    d_head(h - 1)
            d_head(3)
            pe.wait_ge(hm_evac, 8)

            for j in range(6, NJ):
                proj(j)
            pe.wait_ge(job_evac, 4 * NJ)

            for qb in range(NT):
                lo_, hi_ = max(0, qb - 1), min(NT - 1, qb + 1)
                nk = hi_ - lo_ + 1
                if qb:
                    pe.wait_ge(w_nm, qb)
                for h in range(4):
                    kv, r = h // 2, slice(64 * (h % 2), 64 * (h % 2) + 64)
                    mm = pe.matmul(PS[:, h, 0:nk * P], AQ[r, kv, qb * P:(qb + 1) * P], AK[r, kv, lo_ * P:(hi_ + 1) * P], start=True, stop=True)
                mm.then_inc(w_qk, 1)
                pe.wait_ge(w_exp, qb + 1)
                if qb:
                    pe.wait_ge(w_pt, qb)
                for h in range(4):
                    for k in range(3):
                        if k < nk:
                            i = 3 * h + k
                            mm = pe.transpose(PS[:, 4 + i // 4, P * (i % 4):P * (i % 4) + P], WP_[:, h, k * P:(k + 1) * P], ID)
                        elif qb == 0:
                            i = 3 * h + k
                            mm = pe.transpose(PS[:, 4 + i // 4, P * (i % 4):P * (i % 4) + P], ID, ID)
                mm.then_inc(w_tr, 1)
                pe.wait_ge(w_pt, qb + 1)
                if qb:
                    pe.wait_ge(w_mix, qb)
                for h in range(4):
                    kv = h // 2
                    for k in range(nk):
                        mm = pe.matmul(PS[:, 7, 64 * h:64 * h + 64], WT_[:, 3 * h + k, :], AV[:, lo_ + k, 64 * kv:64 * kv + 64], start=(k == 0), stop=(k == nk - 1))
                mm.then_inc(w_pv, 1)
                pe.wait_ge(w_on, qb + 1)
                for k in range(2):
                    mm = pe.transpose(PS[:, 7, 256 + P * k:256 + P * k + P], WO_[:, P * k:P * k + P], ID)
                mm.then_inc(w_ot, 1)
            pe.wait_ge(w_mix, NT)

            pe.wait_ge(r_conv, 1)
            for tt in range(NT):
                for ct in range(2):
                    mm = pe.transpose(PS[:, tt // 2, 256 * (tt % 2) + P * ct:256 * (tt % 2) + P * ct + P], CV[:, 4 + ct, tt * P:(tt + 1) * P], ID)
                if tt % 2:
                    mm.then_inc(r_vt, 1)
            pe.wait_ge(r_act, 1)
            for ct in range(2):
                for half in range(2):
                    mm = pe.matmul(PS[:, 4 + 2 * ct + half, :], ONES, S1_[:, ct, 512 * half:512 * half + 512], start=True, stop=True)
            mm.then_inc(r_kn, 1)
            pe.wait_ge(r_act, 3)
            pe.wait_ge(r_vte, NT)
            pe.wait_ge(r_kk, 1)

            def tok(t, i, ct, tile):
                return t[:, i, ct, 2 * tile:2 * tile + 2, :].rearrange("p c k -> p (c k)")

            for d in range(2):
                for ct in range(2):
                    for half in range(2):
                        t0 = 512 * half
                        pe.matmul(PS[:, 2 * ct + half, :], WA[0:64, d, P * ct:P * ct + P], CV[0:64, 6, t0:t0 + 512], start=True, stop=True)
                        mm = pe.matmul(PS[:, 4 + 2 * ct + half, :], WA[64:128, d, P * ct:P * ct + P], CV[64:128, 6, t0:t0 + 512], start=True, stop=True)
                mm.then_inc(r_z, 1)
                pe.wait_ge(r_pre, d + 1)
                pe.wait_ge(r_exp, d + 1)
                for b in range(NB):
                    n = d * NB + b
                    dv0, ac0, po0 = G_DVE * n, G_ACT * n, G_POOL * n
                    if n:
                        pe.wait_ge(g_dve, dv0)
                        pe.wait_ge(g_act, ac0)
                    for kind in range(2):
                        for t in range(2):
                            for h2 in range(2):
                                for cp in range(2):
                                    for hp in range(2):
                                        cq = cp ^ hp
                                        c, r = 4 * b + 2 * t + cq, slice(64 * hp, 64 * hp + 64)
                                        mm = pe.matmul(PS[64 * cq:64 * cq + 64, 2 * t + hp, 256 * kind + 128 * h2:256 * kind + 128 * h2 + 128],
                                                       BKt[r, kind, h2, c, :], KR[r, :, h2, c, :], start=True, stop=True, skip_group_check=True)
                    mm.then_inc(g_pe, 1)
                    for t in range(2):
                        for h2 in range(2):
                            for cp in range(2):
                                for hp in range(2):
                                    cq = cp ^ hp
                                    c, r = 4 * b + 2 * t + cq, slice(64 * hp, 64 * hp + 64)
                                    mm = pe.matmul(PS[64 * cq:64 * cq + 64, 4 + hp, 128 * t + 64 * h2:128 * t + 64 * h2 + 64],
                                                   KR[r, 0, h2, c, :], BKt[r, 0, h2, c, :], start=True, stop=True, skip_group_check=True)
                    mm.then_inc(g_pe, 1)

                    def turn(bank, t4, i):
                        for t in range(2):
                            for ct in range(2):
                                o = PS[:, bank, 256 * t:256 * t + 256].rearrange("p (b a k) -> p a b k", b=2, a=2)[:, ct]
                                m = pe.transpose(o, tok(t4, i, ct, 2 * b + t), ID)
                        return m

                    turn(6, KR, 0)
                    turn(7, BKt, 0).then_inc(g_pe, 1)
                    pe.wait_ge(g_dve, dv0 + 1)
                    turn(0, BKt, 1).then_inc(g_pe, 1)

                    def units():
                        for t in range(2):
                            for hp in range(2):
                                for h2 in range(2):
                                    for cp in range(2):
                                        yield t, hp, h2, cp, 4 * t + 2 * hp + h2, slice(64 * cp, 64 * cp + 64)

                    def vtok(t, hp, h2, r):
                        return VT[r, 4 * (b // 2) + 2 * (b % 2) + t, hp, h2, :]

                    for t, hp, h2, cp, u, r in units():
                        mm = pe.matmul(PS[r, 1, 64 * u:64 * u + 64], G1[r, 2 * t + hp, 1, h2, 0, :], vtok(t, hp, h2, r), start=True, stop=True, skip_group_check=True)
                    mm.then_inc(g_pe, 1)
                    for l in range(5):
                        pe.wait_ge(g_pool, po0 + 2 + l)
                        pe.wait_ge(g_dve, dv0 + 2 + l)
                        for t, hp, h2, cp, u, r in units():
                            mm = pe.matmul(PS[r, 2, 64 * u:64 * u + 64], LT[r, u, :], QQ[r, 0, u, :], start=True, stop=True, skip_group_check=True)
                        mm.then_inc(g_pe, 1)
                        pe.wait_ge(g_act, ac0 + 5 + l)
                        if l < 4:
                            for t, hp, h2, cp, u, r in units():
                                pe.matmul(PS[r, 3, 64 * u:64 * u + 64], QQ[r, 1, u, :], XX[r, u, :], start=True, stop=True, skip_group_check=True)
                        for t, hp, h2, cp, u, r in units():
                            mm = pe.matmul(PS[r, 4, 64 * u:64 * u + 64], XX[r, u, :], QQ[r, 1, u, :], start=True, stop=True, skip_group_check=True)
                        mm.then_inc(g_pe, 1)
                    pe.wait_ge(g_dve, dv0 + 7)
                    for t, hp, h2, cp, u, r in units():
                        mm = pe.matmul(PS[r, 5 + t, 128 * (u % 4):128 * (u % 4) + 128], QQ[r, 1, u, :], RH[r, u, :, :].rearrange("p b k -> p (b k)"),
                                       start=True, stop=True, skip_group_check=True)
                    mm.then_inc(g_pe, 1)
                    pe.wait_ge(g_act, ac0 + 10)
                    for t in range(2):
                        for h2 in range(2):
                            for hp in range(2):
                                for cq in range(2):
                                    cp = cq ^ hp
                                    u, r, o = 4 * t + 2 * hp + h2, slice(64 * cp, 64 * cp + 64), slice(64 * hp, 64 * hp + 64)
                                    f = 128 * t + 64 * h2
                                    pe.matmul(PS[o, cp, f:f + 64], WU[r, u, 0, :], G1[r, 2 * t + hp, 0, h2, 1, :], start=True, stop=True, skip_group_check=True)
                                    pe.matmul(PS[o, cp, 256 + f:256 + f + 64], WU[r, u, 0, :], BT[r, u, :], start=True, stop=True, skip_group_check=True)
                                    pe.matmul(PS[o, 2 + cp, f:f + 64], KT[r, u, :], vtok(t, hp, h2, r), start=True, stop=False, skip_group_check=True)
                                    mm = pe.matmul(PS[o, 2 + cp, f:f + 64], BT[r, u, :], WU[r, u, 1, :], start=False, stop=True, skip_group_check=True)
                    mm.then_inc(g_pe, 1)
                    for t, hp, h2, cp, u, r in units():
                        pe.matmul(PS[r, 7, 64 * u:64 * u + 64], G1[r, 2 * t + hp, 1, h2, 1, :], vtok(t, hp, h2, r), start=True, stop=False, skip_group_check=True)
                        mm = pe.matmul(PS[r, 7, 64 * u:64 * u + 64], G1[r, 2 * t + hp, 0, h2, 1, :], WU[r, u, 1, :], start=False, stop=True, skip_group_check=True)
                    mm.then_inc(g_pe, 1)
                order = list(range(NCH)) if d == 0 else list(range(NCH - 1, -1, -1))
                for i in range(1, NCH - 1):
                    pe.wait_ge(c_z, 15 * d + i)
                    for ct in range(2):
                        for hp in range(2):
                            r = slice(64 * hp, 64 * hp + 64)
                            mm = pe.matmul(PS[r, 0, 64 * ct:64 * ct + 64], BKt[r, 0, ct, order[i], :], KR[r, 0, ct, order[i], :], start=True, stop=True, skip_group_check=True)
                    mm.then_inc(c_mm, 1)
                pe.wait_ge(c_z, 15 * d + 15)
                for q4 in range(2):
                    for t in range(4):
                        for h2 in range(2):
                            for cp in range(2):
                                for hp in range(2):
                                    cq = cp ^ hp
                                    c, r = 2 * (4 * q4 + t) + cq, slice(64 * hp, 64 * hp + 64)
                                    mm = pe.matmul(PS[64 * cq:64 * cq + 64, 2 + 2 * q4 + hp, 128 * t + 64 * h2:128 * t + 64 * h2 + 64],
                                                   KR[r, 1, h2, c, :], KR[r, 0, h2, c, :], start=True, stop=True, skip_group_check=True)
                    mm.then_inc(y_mm, 1)
                pe.wait_ge(y_add, 4 * (d + 1))

            pe.wait_ge(p_bon, 1)
            for tt in range(NT):
                for ct in range(2):
                    mm = pe.matmul(PS[:, 2, 4 * tt:4 * tt + 4], CV[:, ct, tt * P:(tt + 1) * P], RB[:, 4 * ct:4 * ct + 4], start=(ct == 0), stop=(ct == 1), skip_group_check=True)
            mm.then_inc(p_mm, 1)
            for tt in range(NT):
                mm = pe.matmul(PS[:, 4 + tt // 2, 256 * (tt % 2):256 * (tt % 2) + 256], CV[:, 7, tt * P:(tt + 1) * P], GU[:, :], start=True, stop=True, skip_group_check=True)
            mm.then_inc(p_mm, 1)
            pe.wait_ge(p_y, 1)
            for ct in range(2):
                for half in range(2):
                    if ct == 1 and half == 0:
                        pe.wait_ge(p_bon, 2)
                    for k in range(4):
                        mm = pe.transpose(PS[:, 2 * ct + half, k * P:(k + 1) * P], YF[:, 4 * half + k, ct].rearrange("p b k -> p (b k)"), ID)
                    mm.then_inc(p_tr, 1)

            pe.wait_ge(p_mix, 4)
            norm(nm, lambda tt: XN2[:, tt])
            mh, ml = ((lambda kt, t=t: t[:, kt // 4, 256 * (kt % 4):256 * (kt % 4) + 256]) for t in (AH, AL))
            oh, ol = (lambda kt: AH[:, kt, :]), (lambda kt: AL[:, kt, :])
            pe.wait_ge(mix_lo, 8)
            for j, (kind, i) in enumerate(jobs2):
                if j >= 2:
                    pe.wait_ge(*evac_of[j - 2])
                bank = 4 * (j % 2)
                if kind == "wout":
                    token_job(4, hh, hl, bank)
                elif kind == "wkv" and i < 2:
                    feature_job(4, mh, ml, lambda ct, _: PS[:, bank, 256 * ct:256 * ct + 256], starts=lambda ct, _: ct == 0, cols=((0, 256),))
                elif kind == "wkv":
                    token_job(4, mh, ml, bank, nt=2)
                elif kind == "wq":
                    if i == 0:
                        for e in evac_of[4:8]:
                            pe.wait_ge(*e)
                        norm(n2, lambda tt: XN2[:, tt % 2])
                    feature_job(4, hh, hl, lambda ct, k: PS[:, bank + 2 * ct + k, :])
                else:
                    if i == 0:
                        pe.wait_ge(*evac_of[9])
                        cross()
                    token_job(2, oh, ol, bank)
                if kind == "wq" and i == 1:
                    def cross():
                        for qb in range(NT):
                            if qb:
                                pe.wait_ge(c_exp, qb)
                            for h in range(4):
                                mm = pe.matmul(PS[:, h // 2, 256 * (h % 2):256 * (h % 2) + 256], QC[:, h, qb * P:(qb + 1) * P], KM[:, h, :], start=True, stop=True, skip_group_check=True)
                            mm.then_inc(c_qk, 1)
                            pe.wait_ge(c_p, qb + 1)
                            if qb:
                                pe.wait_ge(c_pt, qb)
                            for k in range(8):
                                mm = pe.transpose(PS[:, 2 + k // 4, P * (k % 4):P * (k % 4) + P], CP[:, P * k:P * k + P], ID)
                            mm.then_inc(c_tr, 1)
                            pe.wait_ge(c_pt, qb + 1)
                            if qb:
                                pe.wait_ge(c_lo, qb)
                            for h in range(4):
                                for m in range(2):
                                    mm = pe.matmul(PS[:, 4, P * h:P * h + P], VM[:, m, P * h:P * h + P], CPT[:, P * (2 * h + m):P * (2 * h + m) + P],
                                                   start=(m == 0), stop=(m == 1), skip_group_check=True)
                            mm.then_inc(c_pv, 1)
                        pe.wait_ge(c_lo, NT)
            for e in evac_of[12:]:
                pe.wait_ge(*e)
            norm(n3, lambda tt: XN2[:, tt % 2])
            for i in range(FF_ITERS + 1):
                if i < FF_ITERS:
                    if i == 1:
                        pe.wait_ge(f_silu, 4)
                    elif i:
                        pe.wait_ge(f_add, 16 * (i - 2) + 12)
                    feature_job(4, hh, hl, lambda ct, k: PS[:, 2 * ct + k, :])
                    if i == 1:
                        pe.wait_ge(f_mul, 4)
                    elif i:
                        pe.wait_ge(f_add, 16 * (i - 2) + 16)
                    feature_job(4, hh, hl, lambda ct, k: PS[:, 4 + 2 * ct + k, :])
                if i:
                    m = i - 1
                    pe.wait_ge(f_lo, 4 * m + 4)
                    for s in range(4):
                        if s >= 2:
                            pe.wait_ge(f_add, 16 * m + 4 * (s - 1))
                        elif i < FF_ITERS:
                            pe.wait_ge(*((f_silu, 4 * i + 4) if s == 0 else (f_mul, 4 * i + 4)))
                        else:
                            pe.wait_ge(f_add, 16 * (m - 1) + 12 + 4 * s)
                        token_job(1, lambda kt: AH[:, 2 * (m % 2) + kt, :], lambda kt: AL[:, 2 * (m % 2) + kt, :], 4 * (s % 2))


INPUTS = ["x", "mem", "norm_mix", "w_in", "win_sink", "diff_lq1", "diff_lk1", "diff_lq2", "diff_lk2", "diff_subln",
          "rwkv_conv", "rwkv_w0", "rwkv_w_up", "rwkv_a0", "rwkv_a_up", "rwkv_g_up", "rwkv_k_k", "rwkv_k_a", "rwkv_r_k",
          "rwkv_ln_g", "rwkv_ln_b", "w_out", "norm_cross", "norm_mem", "x_wq", "x_wkv", "x_wo", "norm_ffn",
          "ffn_w_gu", "ffn_w_down", "norm_final"]


def shape_constants():
    import numpy as np

    row, colm = np.arange(P) % C, np.arange(C)
    j, t = row[:, None], colm[None, :]
    cn = np.zeros((P, C_LEN), np.float32)
    cn[:, C_ID:C_ID + P] = np.eye(P)
    cn[:, C_ONES:C_ONES + P] = np.kron(np.eye(2), np.ones((C, C)))
    cn[:, C_MASK[0]:C_MASK[0] + 128] = np.concatenate([t > j, t >= j], 1)
    cn[:, C_MASK[1]:C_MASK[1] + 128] = np.concatenate([t < j, t <= j], 1)
    for l, s in enumerate([1] + LEVELS):
        later = (t // s % 2 == 1) & (j // s == t // s - 1)
        earlier = (j // s % 2 == 1) & (t // s == j // s - 1)
        cn[:, C_LT[0] + 64 * l:C_LT[0] + 64 * l + 64] = later
        cn[:, C_LT[1] + 64 * l:C_LT[1] + 64 * l + 64] = earlier
    cn[:, C_I64:C_I64 + 64] = j == t
    p = np.arange(P)[:, None]
    dist = (-DIFF_SLOPES[0] * np.abs(np.arange(1920)[None, :] - 896 - p)).astype(np.float32)
    delta = np.abs(np.arange(384)[None, :] - P - p)
    win = np.concatenate([np.where(delta <= 128, -s * delta, -1e30) for s in WIN_SLOPES], 1).astype(np.float32)
    return {"consts": cn, "dist": dist, "win_bias": win}


def kernel(**inputs):
    import numpy as np
    import concourse.bacc as bacc
    from concourse.bass_utils import run_bass_kernel_spmd

    nc = bacc.Bacc("TRN2", target_bir_lowering=False, num_devices=1)
    arrays = {f"in_{k}": np.ascontiguousarray(inputs[k]) for k in INPUTS}
    arrays.update({f"in_{k}": v for k, v in shape_constants().items()})
    io = {k[3:]: nc.dram_tensor(k, v.shape, mybir.dt.from_np(v.dtype), kind="ExternalInput").ap() for k, v in arrays.items()}
    io["out"] = nc.dram_tensor("out_x", (1, T, D), F32, kind="ExternalOutput").ap()
    build(nc, io)
    r = run_bass_kernel_spmd(nc, [arrays], core_ids=[0])
    return r.results[0]["out_x"]
```

```python
import math
from contextlib import ExitStack

import concourse.bass as bass
from concourse import mybir

F32 = mybir.dt.float32
F32R = mybir.dt.float32r
ALU = mybir.AluOpType
ACT = mybir.ActivationFunctionType
AX_X = mybir.AxisListType.X

P = 128
D = 1024
T = 1024
NT = T // P
KD = D // P
MEM = 256
DFF = 2816
IN_W = 3072
PW = 256
PK = 2
NRAW = 3
NW = 6
RMS_EPS = 1e-6
GN_EPS = 64e-5
C = 64
NCH = T // C
LEVELS = [2, 4, 8, 16, 32]
E05 = math.exp(-0.5)
LAM_INIT = 0.8 - 0.6 * math.exp(-0.3 * 0)
FF_ITERS = DFF // PW

C_ID = 0
C_ONES = 128
C_MASK = {0: 256, 1: 384}
C_LT = {0: 512, 1: 512 + 384}
C_I64 = 1280
C_LEN = 1344
SLOPES = [2.0 ** -(k + 1) for k in range(8)]
WIN_SLOPES, DIFF_SLOPES = SLOPES[0::2], SLOPES[1::2]


def build(nc, io):
    out = io["out"]
    ctx = ExitStack()
    with ctx:
        base = 16512

        def at(name, kib, shape, dt=F32):
            return nc.alloc_sbuf_tensor_at(name, [P] + list(shape), dt, offset=base + int(kib * 1024))

        arena_end = 207.8
        ctx.enter_context(nc.sbuf_tensor("arena", [P, int(arena_end * 256)], F32))
        WH = at("WH", 0, [NW, PK, PW], F32R)
        WL = at("WL", 12, [NW, PK, PW], F32R)
        RAW = at("RAW", 24, [NRAW, PK, PW])
        CN = at("CN", 30, [C_LEN])
        WA = at("WA", 35.25, [2, 256])
        GU = at("GU", 37.25, [256])
        BC = at("BC", 38.25, [1024])
        SM = at("SM", 42.25, [432])
        HH = at("HH", 44, [KD, T], F32R)
        HL = at("HL", 76, [KD, T], F32R)
        MIX = at("MIX", 108, [8, T])
        BQ = at("BQ", 140, [4, T])
        BK = at("BK", 156, [4, T])
        BV = at("BV", 172, [NT, 512])
        GB = at("GB", 124, [D])
        XT = at("XT", 188, [2, D])
        XN = at("XN", 196, [2, D])
        E_ = at("E_", 124, [4, T])
        TAB = at("TAB", 188, [1920])
        AT_ = at("AT_", 195.5, [T])
        OB = at("OB", 199.5, [2, NT, 128])
        KST = at("KST", 0, [2, 2, T], F32R)
        QST = at("QST", 16, [2, 2, 2, 2 * P], F32R)
        CIN = at("CIN", 140, [8, T + 2])
        QW = at("QW", 173, [4, T], F32R)
        KW = at("KW", 189, [2, 2, T], F32R)
        AV = at("AV", 132, [NT, 128])
        WP_ = at("WP_", 44, [3, 2, 384])
        WT_ = at("WT_", 53, [2, 6, 128])
        WB_ = at("WB_", 59, [4, 384])
        CV = at("CV", 44, [8, T])
        KK = at("KK", 76, [2, T])
        YY = at("YY", 84, [NT, 2, 2, 64])
        VT = at("VT", 92, [NT, 2, 2, 64])
        KS = at("KS", 100, [2, T])
        KR = at("KR", 140, [2, 2, NCH, C])
        BKt = at("BKt", 156, [2, 2, NCH, C])
        S1_ = at("S1_", 172, [2, T])
        S2_ = at("S2_", 180, [2, T])
        S3_ = at("S3_", 188, [2, T])
        YF = at("YF", 172, [NT, 2, 2, 64])
        G1 = at("G1", 172, [4, 2, 2, 2, C])
        LT = at("LT", 180, [8, C])
        QQ = at("QQ", 182, [2, 8, C])
        XX = at("XX", 186, [8, C])
        RH = at("RH", 188, [8, 2, C])
        BT = at("BT", 192, [8, C])
        KT = at("KT", 194, [8, C])
        WU = at("WU", 196, [8, 2, C])
        QT0 = at("QT0", 200, [8, C])
        EH = at("EH", 202, [32])
        DD = at("DD", 202.25, [32])
        HT = at("HT", 202.5, [32])
        SCM = at("SCM", 196, [T])
        FO = at("FO", 180, [2, D])
        X = at("X", 140, [NT, D])
        AH = at("AH", 108, [4, T], F32R)
        AL = at("AL", 124, [4, T], F32R)
        XN2 = at("XN2", 172, [2, D])
        QC = at("QC", 180, [4, T])
        KM = at("KM", 196, [4, MEM])
        VM = at("VM", 200, [2, 512])
        GBM = at("GBM", 116, [D])
        GBC = at("GBC", 120, [D])
        GBF = at("GBF", 196, [D])
        GBL = at("GBL", 200, [D])
        MX = at("MX", 180, [2, D])
        CP = at("CP", 44, [2, 1024])
        CPT = at("CPT", 52, [2, 1024])
        ACTB = at("ACTB", 172, [2, T])
        FU = at("FU", 180, [2, T])

        PS = ctx.enter_context(nc.psum_tensor("PS", [P, 8, 512], F32))

        def sem(name):
            return ctx.enter_context(nc.semaphore(name))

        ID = CN[:, C_ID:C_ID + 128]
        ONES = CN[:, C_ONES:C_ONES + 128]
        I64 = CN[:, C_I64:C_I64 + 64]
        LNG, LNB, SUB, SINK = BC[:, 0:256], BC[:, 256:512], BC[:, 512:640], BC[:, 640:644]
        LQ = [BC[:, 648 + 64 * i:712 + 64 * i] for i in range(4)]
        VR = BC[0:38, 904:1024]
        SS, RS = SM[:, 0:8], SM[:, 8:16]
        LAM = SM[:, 16:20]
        MM, NM, LL = SM[:, 20:24], SM[:, 24:28], SM[:, 28:32]
        PT = SM[:, 32:70]
        RB = SM[:, 72:80]
        CO = SM[:, 80:96]
        HS, HR = SM[:, 96:104], SM[:, 104:112]
        GS, GM = SM[:, 112:144], SM[:, 144:176]
        GV = SM[:, 176:208]
        BON = SM[:, 208:240]
        WM, WSUM, WSNK, WR = (SM[:, c:c + 6] for c in (332, 338, 344, 350))
        CM, CL, CR = (SM[:, c:c + 8] for c in (356, 364, 372))
        MS, MR = SM[:, 268:270], SM[:, 270:272]
        FS, FR = SM[:, 272:280], SM[:, 280:288]
        AS, AR = SM[:, 288:296], SM[:, 296:304]
        BS, BR = SM[:, 304:312], SM[:, 312:320]
        NMD, MD, LD = SM[:, 320:324], SM[:, 324:328], SM[:, 328:332]
        VROWS = XN[0:38, 0, 0:128]
        PTC_CONV, PTC_W0, PTC_A0, PTC_KK, PTC_KA, PTC_RK = 0, 24, 28, 32, 34, 36

        def col(i):
            return PT[:, i:i + 1]

        raw_full = [sem(f"raw_full{i}") for i in range(NRAW)]
        w_hi, w_lo, w_used = sem("w_hi"), sem("w_lo"), sem("w_used")
        consts_in, vecs_in, tab_in = sem("consts_in"), sem("vecs_in"), sem("tab_in")
        vec_t, vec_c = sem("vec_t"), sem("vec_c")
        dve_chain, act_chain, pool_chain = sem("dve_chain"), sem("act_chain"), sem("pool_chain")

        w_in, w_out_, wq, wkv, wo = io["w_in"][0], io["w_out"][0], io["x_wq"][0], io["x_wkv"][0], io["x_wo"][0]
        w_gu, w_dn = io["ffn_w_gu"][0], io["ffn_w_down"][0]
        BQ0, BK0, BV0, CI0, AQ0, AK0 = 512, 1024, 1536, 2048, 0, 256

        def slab(w, c0, rows=D):
            return [(w, r, c0) for r in range(0, rows, PK * P)]

        proj_cols = [BQ0, BQ0 + PW, BK0, BK0 + PW, BV0, BV0 + PW, CI0, CI0 + PW, CI0 + 2 * PW, CI0 + 3 * PW, AQ0, AK0]
        pieces = []
        for c0 in proj_cols:
            pieces += slab(w_in, c0)
        for c0 in range(0, D, PW):
            pieces += slab(w_out_, c0)
        for c0 in range(0, 1024, PW):
            pieces += slab(wkv, c0)
        for c0 in range(0, 512, PW):
            pieces += slab(wq, c0)
        for c0 in range(0, D, PW):
            pieces += slab(wo, c0, 512)
        N_LIN = len(pieces)
        for i in range(FF_ITERS + 1):
            if i < FF_ITERS:
                pieces += slab(w_gu, i * PW) + slab(w_gu, DFF + i * PW)
            if i >= 1:
                pieces += [(w_dn, (i - 1) * PW, c0) for c0 in range(0, D, PW)]

        class Norm:
            def __init__(self, name, n):
                self.n = n
                self.full = [sem(f"{name}_full0"), sem(f"{name}_full1")]
                self.std, self.xn, self.tr, self.hi, self.lo = (sem(f"{name}_{k}") for k in ("std", "xn", "tr", "hi", "lo"))

        n1, nm, n2, n3 = Norm("n1", NT), Norm("nm", 2), Norm("n2", NT), Norm("n3", NT)
        gain_in = {k: sem(f"gain_{k}") for k in ("mix", "mem", "cross", "ffn", "final")}

        job_evac = sem("job_evac")
        NJ = len(proj_cols)
        jobs2 = ([("wout", i) for i in range(4)] + [("wkv", i) for i in range(4)] + [("wq", i) for i in range(2)]
                 + [("wo", i) for i in range(4)])
        job2_act, job2_dve = sem("job2_act"), sem("job2_dve")
        end2, e = [], 4 * NJ
        for kind, _ in jobs2:
            e += 2 if kind == "wo" else 4
            end2.append(e)

        def ff0(i):
            return N_LIN + 12 * i - (4 if i else 0)

        evac_of, n_act, n_dve = [], 0, 0
        for kind, _ in jobs2:
            if kind in ("wkv", "wq"):
                n_act += 1
                evac_of.append((job2_act, n_act))
            else:
                n_dve += 1
                evac_of.append((job2_dve, n_dve))

        qk_done, s_read, nm_done, exp_done = sem("qk_done"), sem("s_read"), sem("nm_done"), sem("exp_done")
        comb_done, tr_done, at_evac, pv_done, o_evac = (sem(k) for k in ("comb_done", "tr_done", "at_evac", "pv_done", "o_evac"))
        sq_done, hs_done, hstd, hn_done, ht_done, hm_evac = (sem(k) for k in ("sq_done", "hs_done", "hstd", "hn_done", "ht_done", "hm_evac"))
        lam_s, lam_e = sem("lam_s"), sem("lam_e")
        k_staged, q_staged = sem("k_staged"), sem("q_staged")

        wb_in, qw_lo, w_qk, w_nm, w_exp, w_p, w_tr, w_pt, w_pv, w_mix = (
            sem(k) for k in ("wb_in", "qw_lo", "w_qk", "w_nm", "w_exp", "w_p", "w_tr", "w_pt", "w_pv", "w_mix"))
        NWU = 2 * NT

        def window(u):
            qb, kv = u // 2, u % 2
            first, last = max(0, qb - 1), min(NT - 1, qb + 1)
            return qb, kv, first, last - first + 1


        pads, r_conv, r_vt, r_vte, r_sq, r_kn, r_std, r_act, r_kk = (
            sem(k) for k in ("pads", "r_conv", "r_vt", "r_vte", "r_sq", "r_kn", "r_std", "r_act", "r_kk"))
        r_z, r_sig, r_c, r_exp, r_pre, r_scm, r_eh = (sem(k) for k in ("r_z", "r_sig", "r_c", "r_exp", "r_pre", "r_scm", "r_eh"))
        g_pe, g_act, g_dve, g_pool = sem("g_pe"), sem("g_act"), sem("g_dve"), sem("g_pool")
        c_mm, c_z, y_mm, y_add = sem("c_mm"), sem("c_z"), sem("y_mm"), sem("y_add")
        p_s, p_mm, p_std, p_bon, p_g, p_y, p_tr, p_mix = (sem(k) for k in ("p_s", "p_mm", "p_std", "p_bon", "p_g", "p_y", "p_tr", "p_mix"))
        mix_hi, mix_lo, x_in = sem("mix_hi"), sem("mix_lo"), sem("x_in")
        c_qk, c_max, c_exp, c_p, c_tr, c_pt, c_pv, c_hi, c_lo = (
            sem(k) for k in ("c_qk", "c_max", "c_exp", "c_p", "c_tr", "c_pt", "c_pv", "c_hi", "c_lo"))
        f_silu, f_mul, f_hi, f_lo, f_add = (sem(k) for k in ("f_silu", "f_mul", "f_hi", "f_lo", "f_add"))
        l_std, l_o, out_done = sem("l_std"), sem("l_o"), [sem("out_done0"), sem("out_done1")]

        NB = 4
        G_PE, G_ACT, G_DVE, G_POOL = 3 + 2 + 2 * 5 + 1 + 2, 2 + 2 + 5 + 1 + 1, 2 + 5 + 1, 6

        block = ctx.enter_context(nc.Block())

        @block.sync
        def _(sp):
            def load(p):
                w, r0, c0 = pieces[p]
                if p >= NRAW:
                    sp.wait_ge(w_hi, p - NRAW + 1)
                    sp.wait_ge(w_lo, p - NRAW + 1)
                sp.dma_start(RAW[:, p % NRAW], w[r0:r0 + PK * P, c0:c0 + PW].rearrange("(k p) c -> p k c", p=P)
                             ).then_inc(raw_full[p % NRAW], 16)

            sp.dma_start(XT[:, 0], io["x"][0, 0:P, :]).then_inc(n1.full[0], 16)
            sp.dma_start(GB[:, :], io["norm_mix"][0:1, :].broadcast_to([P, D])).then_inc(gain_in["mix"], 16)
            sp.dma_start(CN[:, :], io["consts"]).then_inc(consts_in, 16)
            sp.dma_start(XT[:, 1], io["x"][0, P:2 * P, :]).then_inc(n1.full[1], 16)
            for p in range(NRAW):
                load(p)
            for tt in range(2, NT):
                sp.wait_ge(n1.xn, tt - 1)
                sp.dma_start(XT[:, tt % 2], io["x"][0, tt * P:(tt + 1) * P, :]).then_inc(n1.full[tt % 2], 16)
            for p in range(NRAW, 4 * NJ):
                load(p)
            for p in range(4 * NJ, 4 * NJ + NRAW):
                load(p)
            sp.wait_ge(y_add, 8)
            for tt in range(NT):
                sp.dma_start(X[:, tt], io["x"][0, tt * P:(tt + 1) * P, :]).then_inc(x_in, 16)
            sp.wait_ge(mix_lo, 8)
            sp.wait_ge(mix_hi, 8)
            sp.dma_start(GBM[:, :], io["norm_mem"].rearrange("(a d) -> a d", a=1).broadcast_to([P, D])).then_inc(gain_in["mem"], 16)
            for tt in range(2):
                sp.dma_start(MX[:, tt], io["mem"][0, tt * P:(tt + 1) * P, :]).then_inc(nm.full[tt], 16)
            sp.dma_start(GBC[:, :], io["norm_cross"][0:1, :].broadcast_to([P, D])).then_inc(gain_in["cross"], 16)
            for p in range(4 * NJ + NRAW, N_LIN + NRAW):
                load(p)
            sp.wait_ge(c_lo, NT)
            sp.dma_start(GBF[:, :], io["norm_ffn"][0:1, :].broadcast_to([P, D])).then_inc(gain_in["ffn"], 16)
            sp.dma_start(GBL[:, :], io["norm_final"].rearrange("(a d) -> a d", a=1).broadcast_to([P, D])).then_inc(gain_in["final"], 16)
            for p in range(N_LIN + NRAW, len(pieces)):
                load(p)
            for tt in range(NT):
                sp.wait_ge(l_o, tt + 1)
                sp.dma_start(out[0, tt * P:(tt + 1) * P, :], FO[:, tt % 2]).then_inc(out_done[tt % 2], 16)
            for s in out_done:
                sp.wait_ge(s, 8 * NT)

        @block.gpsimd
        def _(pool):
            chain = [0]

            def link(ins):
                chain[0] += 1
                ins.then_inc(pool_chain, 1)
                pool.wait_ge(pool_chain, chain[0])

            pool.dma_start(VROWS[0:24, :], io["rwkv_conv"][0].rearrange("j (c p) -> (j c) p", p=P)).then_inc(vecs_in, 16)
            pool.dma_start(VROWS[24:28, :], io["rwkv_w0"][0].rearrange("d (c p) -> (d c) p", p=P)).then_inc(vecs_in, 16)
            pool.dma_start(VROWS[28:32, :], io["rwkv_a0"][0].rearrange("d (c p) -> (d c) p", p=P)).then_inc(vecs_in, 16)
            pool.dma_start(VROWS[32:34, :], io["rwkv_k_k"].rearrange("l (c p) -> (l c) p", p=P)).then_inc(vecs_in, 16)
            pool.dma_start(VROWS[34:36, :], io["rwkv_k_a"].rearrange("l (c p) -> (l c) p", p=P)).then_inc(vecs_in, 16)
            pool.dma_start(VROWS[36:38, :], io["rwkv_r_k"][0].rearrange("(c h) p -> c (h p)", h=2)).then_inc(vecs_in, 16)
            pool.dma_start(WA[0:64], io["rwkv_w_up"][0].rearrange("d l c -> l d c")).then_inc(vecs_in, 16)
            pool.dma_start(WA[64:128], io["rwkv_a_up"][0].rearrange("d l c -> l d c")).then_inc(vecs_in, 16)
            for b in range(2):
                def halves(dst, src):
                    return dst.rearrange("p (b a k) -> p b a k", b=2, a=2)[:, b], src.rearrange("l (a b k) -> l b a k", a=2, b=2)[:, b]

                pool.dma_start(*halves(GU[:, :], io["rwkv_g_up"][0])).then_inc(vecs_in, 16)
                pool.dma_start(*halves(LNG, io["rwkv_ln_g"].broadcast_to([P, 256]))).then_inc(vecs_in, 16)
                pool.dma_start(*halves(LNB, io["rwkv_ln_b"].broadcast_to([P, 256]))).then_inc(vecs_in, 16)
            pool.dma_start(SUB, io["diff_subln"].broadcast_to([P, 128])).then_inc(vecs_in, 16)
            pool.dma_start(SINK, io["win_sink"].broadcast_to([P, 4])).then_inc(vecs_in, 16)
            for i, k in enumerate(("diff_lq1", "diff_lk1", "diff_lq2", "diff_lk2")):
                pool.dma_start(LQ[i], io[k].broadcast_to([P, 64])).then_inc(vecs_in, 16)

            def lo(p):
                pool.wait_ge(w_hi, p + 1)
                pool.tensor_tensor(WL[:, p % NW], RAW[:, p % NRAW], WH[:, p % NW].bitcast(F32), ALU.subtract).then_inc(w_lo, 1)

            for p in range(24):
                lo(p)
            pool.dma_start(TAB[:, :], io["dist"]).then_inc(tab_in, 16)
            pool.wait_ge(w_used, 24)
            pool.wait_ge(w_lo, 24)
            pool.wait_ge(job_evac, 24)

            def stage(dst_hi, dst_lo, src):
                link(pool.tensor_copy(dst_hi, src))
                return pool.tensor_tensor(dst_lo, src, dst_hi.bitcast(F32), ALU.subtract)

            for h in range(4):
                if h >= 2:
                    pool.wait_ge(qk_done, 16 * (h - 1))
                for c in range(2):
                    same, other = slice(64 * c, 64 * c + 64), slice(64 - 64 * c, 128 - 64 * c)
                    ins = stage(KST[same, h % 2, c, :], KST[other, h % 2, c, :], BK[same, h, :])
                ins.then_inc(k_staged, 1)
                for g in range(4):
                    n = 4 * h + g
                    if n >= 2:
                        pool.wait_ge(qk_done, 4 * (n - 1))
                    for c in range(2):
                        same, other = slice(64 * c, 64 * c + 64), slice(64 - 64 * c, 128 - 64 * c)
                        src = BQ[same, h, 2 * P * g:2 * P * (g + 1)]
                        link(stage(QST[same, n % 2, 0, c, :], QST[same, n % 2, 1, c, :], src))
                        for part in range(2):
                            ins = pool.tensor_copy(QST[other, n % 2, part, c, :], QST[same, n % 2, part, c, :].bitcast(F32))
                    ins.then_inc(q_staged, 1)
            for p in range(24, 4 * NJ):
                lo(p)
            pool.wait_ge(w_used, 4 * NJ)
            pool.dma_start(WB_[:, :, :], io["win_bias"].rearrange("p (h k) -> p h k", h=4)).then_inc(wb_in, 16)
            pool.memset(CIN[:, :, 0:1], 0.0)
            pool.memset(CIN[:, :, T + 1:T + 2], 0.0).then_inc(pads, 1)
            for p in range(4 * NJ, 4 * NJ + NRAW):
                lo(p)
            for d in range(2):
                if d == 0:
                    pool.wait_ge(w_mix, NWU)
                else:
                    pool.wait_ge(g_act, G_ACT * NB)
                    pool.wait_ge(g_pe, G_PE * NB)
                    pool.wait_ge(g_dve, G_DVE * NB)
                link(pool.memset(SCM[:, :], 1.0))
                pool.memset(SCM[:, 0:T:C], 0.0).then_inc(r_scm, 1)
                for b in range(NB):
                    n = d * NB + b
                    pool.wait_ge(g_dve, G_DVE * n + 1)
                    if n:
                        pool.wait_ge(g_pe, G_PE * n - 2)
                    abt = G1[:, :, 0, :, 0, :]
                    link(pool.tensor_tensor(QT0[:, :].rearrange("p (a b) k -> p a b k", b=2), abt,
                                            CN[:, C_LT[d]:C_LT[d] + 64].unsqueeze(1).unsqueeze(1).broadcast_to([P, 4, 2, 64]), ALU.mult))
                    pool.tensor_tensor(QQ[:, 1], QT0[:, :], I64.unsqueeze(1).broadcast_to([P, 8, 64]), ALU.subtract).then_inc(g_pool, 1)
                    for l, s in enumerate(LEVELS):
                        if l:
                            pool.wait_ge(g_pe, G_PE * n + 5 + 2 * (l - 1) + 1)
                        m0 = C_LT[d] + 64 * (l + 1)
                        pool.tensor_tensor(LT[:, :].rearrange("p (a b) k -> p a b k", b=2), abt,
                                           CN[:, m0:m0 + 64].unsqueeze(1).unsqueeze(1).broadcast_to([P, 4, 2, 64]), ALU.mult).then_inc(g_pool, 1)
            for p in range(4 * NJ + NRAW, len(pieces)):
                lo(p)

        @block.scalar
        def _(act):
            chain = [0]
            done_hi = [0]

            def link(ins):
                chain[0] += 1
                ins.then_inc(act_chain, 1)
                act.wait_ge(act_chain, chain[0])

            def hi(upto):
                while done_hi[0] < min(upto, len(pieces)):
                    p = done_hi[0]
                    act.wait_ge(raw_full[p % NRAW], 16 * (p // NRAW + 1))
                    if p >= NW:
                        act.wait_ge(w_used, p - NW + 1)
                        act.wait_ge(w_lo, p - NW + 1)
                    act.activation(WH[:, p % NW], RAW[:, p % NRAW], ACT.Copy).then_inc(w_hi, 1)
                    done_hi[0] += 1

            def norm(nn, src, junk, S, hdst, wait_src, width=P, dim=D):
                def stat(tt):
                    wait_src(tt)
                    if tt >= 2:
                        act.wait_ge(nn.tr, 2 * (tt - 1))
                    link(act.activation(junk(tt), src(tt), ACT.Square, accum_out=S[:, tt:tt + 1]))
                    act.activation(S[:, tt:tt + 1], S[:, tt:tt + 1], ACT.Sqrt, bias=RMS_EPS, scale=1.0 / dim).then_inc(nn.std, 1)

                stat(0)
                for tt in range(nn.n):
                    if tt + 1 < nn.n:
                        stat(tt + 1)
                    for b in range(2):
                        act.wait_ge(nn.tr, 2 * tt + b + 1)
                        act.activation(hdst(tt, b), PS[:, 2 * (tt % 4) + b, :].rearrange("p (k t) -> p k t", k=4), ACT.Copy).then_inc(nn.hi, 1)

            hi(NRAW)
            norm(n1, lambda tt: XT[:, tt % 2], lambda tt: XN[:, tt % 2], SS,
                 lambda tt, b: HH[:, 4 * b:4 * b + 4, tt * P:(tt + 1) * P],
                 lambda tt: (act.wait_ge(vec_t, 1), act.wait_ge(n1.full[tt % 2], 16 * (tt // 2 + 1))))

            def evac_proj(j):
                c0 = proj_cols[j]
                act.wait_ge(w_used, 4 * (j + 1))
                bank = [PS[:, 4 * (j % 2) + i, :] for i in range(4)]
                for i in range(4):
                    ct, half = i // 2, i % 2
                    t0 = half * 512
                    if BQ0 <= c0 < BK0:
                        k = (c0 - BQ0) // P + ct
                        act.activation(BQ[:, k, t0:t0 + 512], bank[i], ACT.Copy, scale=0.125).then_inc(job_evac, 1)
                    elif BK0 <= c0 < BV0:
                        k = (c0 - BK0) // P + ct
                        act.activation(BK[:, k, t0:t0 + 512], bank[i], ACT.Copy).then_inc(job_evac, 1)
                    elif BV0 <= c0 < CI0:
                        act.activation(BV[:, 2 * i:2 * i + 2, c0 - BV0:c0 - BV0 + PW], bank[i].rearrange("p (t c) -> p t c", t=2),
                                       ACT.Copy).then_inc(job_evac, 1)
                    elif c0 >= CI0:
                        k = (c0 - CI0) // P + ct
                        act.activation(CIN[:, k, 1 + t0:1 + t0 + 512], bank[i], ACT.Copy).then_inc(job_evac, 1)
                    elif c0 == AQ0:
                        for hp in range(2):
                            rows = slice(64 * hp, 64 * hp + 64)
                            a = act.activation(QW[rows, 2 * ct + hp, t0:t0 + 512], bank[i][rows], ACT.Copy, scale=0.125)
                        a.then_inc(job_evac, 1)
                    elif i < 2:
                        t0 = i * 512
                        for kv in range(2):
                            for hp in range(2):
                                a = act.activation(KW[64 * hp:64 * hp + 64, kv, 0, t0:t0 + 512], bank[i][64 * kv:64 * kv + 64], ACT.Copy)
                        a.then_inc(job_evac, 1)
                    else:
                        act.activation(AV[:, 4 * (i - 2):4 * (i - 2) + 4, :], bank[i].rearrange("p (t c) -> p t c", t=4),
                                       ACT.Copy).then_inc(job_evac, 1)

            for j in range(6):
                hi(min(4 * j + 10, 24))
                evac_proj(j)

            act.wait_ge(lam_s, 1)
            act.activation(LAM[:, 0:2], LAM[:, 0:2], ACT.Exp).then_inc(lam_e, 1)

            def d_exp(u):
                for i, c in enumerate((1, 0)):
                    n = 2 * u + c
                    act.wait_ge(nm_done, 2 * u + i + 1)
                    e = E_[:, n % 4, :]
                    if u >= 2:
                        act.wait_ge(comb_done, u - 1)
                    act.activation(e, e, ACT.Exp, bias=NMD[:, n % 4:n % 4 + 1], accum_out=LD[:, n % 4:n % 4 + 1]).then_inc(exp_done, 1)

            def d_square(h):
                act.wait_ge(o_evac, 8 * h + 8)
                sq = BQ[:, h, :].rearrange("p (t c) -> p t c", t=NT)
                act.activation(sq, OB[:, h % 2], ACT.Square).then_inc(sq_done, 1)

            def d_std(h):
                act.wait_ge(hs_done, h + 1)
                act.activation(HS, HS, ACT.Sqrt, bias=RMS_EPS, scale=1.0 / 128).then_inc(hstd, 1)

            def d_evac(h):
                for b in range(2):
                    act.wait_ge(ht_done, 2 * h + b + 1)
                    act.activation(MIX[:, h, b * 512:b * 512 + 512], PS[:, 7, :], ACT.Copy).then_inc(hm_evac, 1)

            d_exp(0)
            d_exp(1)
            for u in range(32):
                h, qb = u // 8, u % 8
                for b in range(2):
                    act.wait_ge(tr_done, 2 * u + b + 1)
                    if u and b == 0:
                        act.wait_ge(pv_done, u)
                    act.activation(AT_[:, b * 512:b * 512 + 512], PS[:, 4 + b, :], ACT.Copy).then_inc(at_evac, 1)
                if u + 2 < 32:
                    d_exp(u + 2)
                act.wait_ge(pv_done, u + 1)
                if h >= 2 and qb == 0:
                    act.wait_ge(hn_done, h - 1)
                act.activation(OB[:, h % 2, qb, :], PS[:, 6, 0:128], ACT.Copy, scale=CO[:, 4 * (u % 2):4 * (u % 2) + 1]).then_inc(o_evac, 1)
                if h and qb == 0:
                    d_square(h - 1)
                if h and qb == 2:
                    d_std(h - 1)
                if h and qb == 4:
                    d_evac(h - 1)
            d_square(3)
            d_std(3)
            d_evac(3)

            act.wait_ge(qk_done, 64)
            for j in range(6, NJ):
                hi(min(4 * j + 10, 4 * NJ + NRAW))
                evac_proj(j)
            hi(4 * NJ + NRAW)

            def w_exps(u):
                _, _, _, nk = window(u)
                act.wait_ge(w_nm, u + 1)
                for g in range(2):
                    c = 2 * (u % 3) + g
                    act.activation(WP_[:, u % 3, g, 0:nk * P], WP_[:, u % 3, g, 0:nk * P], ACT.Exp, bias=WM[:, c:c + 1], accum_out=WSUM[:, c:c + 1])
                snk = WSNK[:, 2 * (u % 3):2 * (u % 3) + 2]
                act.activation(snk, snk, ACT.Exp).then_inc(w_exp, 1)

            def w_out_evac(u):
                qb, kv, _, _ = window(u)
                act.wait_ge(w_pv, u + 1)
                act.activation(MIX[:, 4 + kv, qb * P:(qb + 1) * P], PS[:, 6 + u % 2, 0:P], ACT.Copy).then_inc(w_mix, 1)

            w_exps(0)
            w_exps(1)
            for u in range(NWU):
                _, _, _, nk = window(u)
                if u + 2 < NWU:
                    w_exps(u + 2)
                act.wait_ge(w_tr, u + 1)
                if u >= 2:
                    act.wait_ge(w_pv, u - 1)
                a = act.activation(WT_[:, u % 2, 0:4, :], PS[:, 4, :].rearrange("p (k q) -> p k q", k=4), ACT.Copy)
                if nk == 3:
                    a = act.activation(WT_[:, u % 2, 4:6, :], PS[:, 5, 0:256].rearrange("p (k q) -> p k q", k=2), ACT.Copy)
                a.then_inc(w_pt, 1)
                if u:
                    w_out_evac(u - 1)
            w_out_evac(NWU - 1)

            act.wait_ge(r_conv, 1)
            for tt in range(NT):
                act.wait_ge(r_vt, tt // 2 + 1)
                act.activation(VT[:, tt].rearrange("p b a k -> p a b k"),
                               PS[:, tt // 2, 256 * (tt % 2):256 * (tt % 2) + 256].rearrange("p (a b k) -> p a b k", a=2, b=2),
                               ACT.Copy).then_inc(r_vte, 1)
            act.wait_ge(r_sq, 1)
            act.activation(S1_[:, :, :], KK[:, :, :], ACT.Square).then_inc(r_act, 1)
            act.activation(CV[0:64, 6, :], CV[0:64, 6, :], ACT.Tanh).then_inc(r_act, 1)
            act.activation(CV[:, 7, :], CV[:, 7, :], ACT.Sigmoid).then_inc(r_act, 1)
            act.wait_ge(r_kn, 1)
            act.activation(S2_[:, :, :].rearrange("p a (b c) -> p (a b) c", c=512), PS[:, 4:8, :], ACT.Sqrt).then_inc(r_std, 1)

            for d in range(2):
                act.wait_ge(r_z, d + 1)
                if d == 0:
                    act.wait_ge(r_kk, 1)
                for ct in range(2):
                    act.activation(S1_[:, ct, :].rearrange("p (b c) -> p b c", c=512), PS[:, 2 * ct:2 * ct + 2, :], ACT.Sigmoid, bias=col(PTC_W0 + 2 * d + ct))
                for ct in range(2):
                    a = act.activation(S3_[:, ct, :].rearrange("p (b c) -> p b c", c=512), PS[:, 4 + 2 * ct:6 + 2 * ct, :], ACT.Sigmoid, bias=col(PTC_A0 + 2 * d + ct))
                a.then_inc(r_sig, 1)
                act.wait_ge(r_c, d + 1)
                c1, cx = ((S2_, 1.0), (S1_, 1.0)) if d == 0 else ((S1_, -1.0), (S2_, -1.0))

                def v4(t):
                    return t[:, :, :].rearrange("p a (c k) -> p (a c) k", k=C)

                act.activation(KR[:, 1].rearrange("p a c k -> p (a c) k"), v4(c1[0]), ACT.Exp, scale=c1[1])
                act.activation(BKt[:, 0].rearrange("p a c k -> p (a c) k"), v4(c1[0]), ACT.Exp, scale=-c1[1])
                act.activation(KR[:, 0].rearrange("p a c k -> p (a c) k"), v4(cx[0]), ACT.Exp, scale=cx[1])
                act.activation(EH[:, :], HT[:, :], ACT.Exp).then_inc(r_exp, 1)
                for b in range(NB):
                    n = d * NB + b
                    pe0, ac0 = G_PE * n, G_ACT * n
                    act.wait_ge(g_pe, pe0 + 3)
                    act.activation(RH[:, :, 0, :], PS[:, 6, :].rearrange("p (u k) -> p u k", k=C), ACT.Copy).then_inc(g_act, 1)
                    act.activation(BT[:, :, :], PS[:, 7, :].rearrange("p (u k) -> p u k", k=C), ACT.Copy).then_inc(g_act, 1)
                    act.wait_ge(g_pe, pe0 + 4)
                    act.activation(KT[:, :, :], PS[:, 0, :].rearrange("p (u k) -> p u k", k=C), ACT.Copy).then_inc(g_act, 1)
                    act.wait_ge(g_pe, pe0 + 5)
                    act.activation(RH[:, :, 1, :], PS[:, 1, :].rearrange("p (u k) -> p u k", k=C), ACT.Copy).then_inc(g_act, 1)
                    for l in range(5):
                        act.wait_ge(g_pe, pe0 + 5 + 2 * l + 1)
                        act.activation(XX[:, :, :], PS[:, 2, :].rearrange("p (u k) -> p u k", k=C), ACT.Copy).then_inc(g_act, 1)
                    act.wait_ge(g_pe, pe0 + 16)
                    act.activation(WU[:, :, :, :].rearrange("p (a u) b k -> p a (u b k)", a=2), PS[:, 5:7, :], ACT.Copy).then_inc(g_act, 1)
                    act.wait_ge(g_pe, pe0 + 17)
                    for cp in range(2):
                        a = act.activation(BKt[:, 1, :, 4 * b + cp:4 * b + 4:2, :].rearrange("p a t k -> p t a k"),
                                           PS[:, 2 + cp, 0:256].rearrange("p (t a k) -> p t a k", t=2, a=2), ACT.Copy)
                    a.then_inc(g_act, 1)

            act.wait_ge(p_s, 1)
            act.activation(S2_[:, :, :].rearrange("p a b -> p (a b)"), YY[:, :, :, :, :].rearrange("p t a b k -> p (t a b k)"), ACT.Square).then_inc(p_std, 1)
            act.wait_ge(p_s, 2)
            act.activation(GV, GV, ACT.Sqrt, bias=GN_EPS, scale=1.0 / C).then_inc(p_std, 1)
            act.wait_ge(p_mm, 1)
            act.activation(BON, PS[:, 2, 0:32], ACT.Copy).then_inc(p_bon, 1)
            for ct in range(2):
                for half in range(2):
                    act.wait_ge(p_tr, 2 * ct + half + 1)
                    act.activation(MIX[:, 6 + ct, half * 512:half * 512 + 512], PS[:, 2 * ct + half, :], ACT.Copy).then_inc(p_mix, 1)
            for k in range(8):
                src = (4, 5, 0, 1, 2, 3, 6, 7)[k]
                if k == 6:
                    act.wait_ge(p_mix, 4)
                if k == 0:
                    act.wait_ge(p_tr, 4)
                act.activation(HH[:, k, :], MIX[:, src, :], ACT.Copy).then_inc(mix_hi, 1)

            def from_dram(nn):
                return lambda tt: act.wait_ge(nn.full[tt % 2], 16 * (tt // 2 + 1))

            hi(4 * NJ + NW)
            act.wait_ge(mix_lo, 8)
            norm(nm, lambda tt: MX[:, tt], lambda tt: XN2[:, tt], MS,
                 lambda tt, b: AH[:, :, :].rearrange("p a (k t) -> p (a k) t", k=4)[:, 4 * b:4 * b + 4, tt * P:(tt + 1) * P], from_dram(nm))

            def evac2(j):
                kind, i = jobs2[j]
                bank = 4 * (j % 2)
                act.wait_ge(w_used, end2[j])
                if kind == "wkv" and i < 2:
                    act.activation(KM[:, 2 * i:2 * i + 2, :], PS[:, bank, :].rearrange("p (c t) -> p c t", c=2), ACT.Copy).then_inc(job2_act, 1)
                elif kind == "wkv":
                    act.activation(VM[:, :, (i - 2) * PW:(i - 1) * PW], PS[:, bank, :].rearrange("p (t c) -> p t c", t=2), ACT.Copy).then_inc(job2_act, 1)
                elif kind == "wq":
                    act.activation(QC[:, 2 * i:2 * i + 2, :].rearrange("p k (b c) -> p (k b) c", c=512), PS[:, bank:bank + 4, :], ACT.Copy).then_inc(job2_act, 1)

            p0 = 4 * NJ
            for j in range(8):
                hi(p0 + 4 * j + 10)
                if j >= 4:
                    evac2(j)
            norm(n2, lambda tt: X[:, tt], lambda tt: XN2[:, tt % 2], AS,
                 lambda tt, b: HH[:, 4 * b:4 * b + 4, tt * P:(tt + 1) * P],
                 lambda tt: act.wait_ge(job2_dve, 4))
            for j in (8, 9):
                hi(p0 + 4 * j + 10)
                evac2(j)
            sc = 128 ** -0.5
            def c_exps(qb):
                act.wait_ge(c_max, qb + 1)
                if qb >= 2:
                    act.wait_ge(c_tr, qb - 1)
                for h in range(4):
                    c = 4 * (qb % 2) + h
                    a = act.activation(CP[:, qb % 2, h * 256:h * 256 + 256], PS[:, 6 * (qb % 2) + h // 2, 256 * (h % 2):256 * (h % 2) + 256], ACT.Exp,
                                       bias=CM[:, c:c + 1], scale=sc, accum_out=CL[:, c:c + 1])
                a.then_inc(c_exp, 1)

            def c_first(qb):
                act.wait_ge(c_pv, qb + 1)
                act.activation(AH[:, :, qb * P:(qb + 1) * P], PS[:, 4 + qb % 2, :].rearrange("p (k t) -> p k t", k=4), ACT.Copy).then_inc(c_hi, 1)

            c_exps(0)
            for qb in range(NT):
                if qb + 1 < NT:
                    c_exps(qb + 1)
                act.wait_ge(c_tr, qb + 1)
                if qb >= 2:
                    act.wait_ge(c_pv, qb - 1)
                act.activation(CPT[:, qb % 2, :].rearrange("p (b c) -> p b c", c=512), PS[:, 2:4, :], ACT.Copy).then_inc(c_pt, 1)
                if qb:
                    c_first(qb - 1)
            c_first(NT - 1)
            hi(p0 + 40 + 6)
            for j in range(10, 14):
                hi(p0 + 40 + 2 * (j - 9) + 5)
            norm(n3, lambda tt: X[:, tt], lambda tt: XN2[:, tt % 2], BS,
                 lambda tt, b: HH[:, 4 * b:4 * b + 4, tt * P:(tt + 1) * P],
                 lambda tt: act.wait_ge(job2_dve, 8))
            for i in range(FF_ITERS + 1):
                q0 = ff0(i)
                if i < FF_ITERS:
                    hi(q0 + 9)
                    act.wait_ge(w_used, ff0(i) + 4)
                    for k in range(4):
                        if k == 0 and i:
                            act.wait_ge(f_mul, 4 * i)
                        act.activation(ACTB[:, k // 2, 512 * (k % 2):512 * (k % 2) + 512], PS[:, k, :], ACT.Silu).then_inc(f_silu, 1)
                    hi(q0 + 12)
                    if i >= 2:
                        act.wait_ge(w_used, ff0(i))
                    for k in range(4):
                        act.wait_ge(f_mul, 4 * i + k + 1)
                        act.activation(AH[:, 2 * (i % 2) + k // 2, 512 * (k % 2):512 * (k % 2) + 512],
                                       FU[:, k // 2, 512 * (k % 2):512 * (k % 2) + 512], ACT.Copy).then_inc(f_hi, 1)
                hi(q0 + 16)
            for tt in range(NT):
                if tt == 0:
                    act.wait_ge(f_add, 16 * FF_ITERS)
                if tt >= 2:
                    act.wait_ge(l_o, tt - 1)
                    act.wait_ge(out_done[tt % 2], 16 * (tt // 2))
                link(act.activation(FO[:, tt % 2], X[:, tt], ACT.Square, accum_out=FS[:, tt:tt + 1]))
                act.activation(FS[:, tt:tt + 1], FS[:, tt:tt + 1], ACT.Sqrt, bias=RMS_EPS, scale=1.0 / D).then_inc(l_std, 1)

        @block.vector
        def _(dve):
            chain = [0]

            def link(ins):
                chain[0] += 1
                ins.then_inc(dve_chain, 1)
                dve.wait_ge(dve_chain, chain[0])

            TT, TS, STT = dve.tensor_tensor, dve.tensor_scalar, dve.scalar_tensor_tensor

            def norm(nn, src, dst, S, R, gb, gain, hdst, ldst):
                def scale(tt):
                    dve.wait_ge(nn.std, tt + 1)
                    link(dve.reciprocal(R[:, tt:tt + 1], S[:, tt:tt + 1]))
                    if tt == 0:
                        dve.wait_ge(gain_in[gain], 16)
                    STT(dst(tt), src(tt), R[:, tt:tt + 1], gb, ALU.mult, ALU.mult).then_inc(nn.xn, 1)

                scale(0)
                for tt in range(nn.n):
                    if tt + 1 < nn.n:
                        scale(tt + 1)
                    for b in range(2):
                        dve.wait_ge(nn.hi, 2 * tt + b + 1)
                        TT(ldst(tt, b), PS[:, 2 * (tt % 4) + b, :].rearrange("p (k t) -> p k t", k=4), hdst(tt, b).bitcast(F32),
                           ALU.subtract).then_inc(nn.lo, 1)

            dve.wait_ge(vec_t, 1)
            dve.tensor_copy(PT, PS[:, 7, 0:38]).then_inc(vec_c, 1)
            dve.wait_ge(vec_c, 1)
            link(dve.memset(RB, 0.0))
            for ct in range(2):
                for hp in range(2):
                    r = slice(64 * hp, 64 * hp + 64)
                    dve.tensor_copy(RB[r, 4 * ct + 2 * hp + ct:4 * ct + 2 * hp + ct + 1], PT[r, PTC_RK + ct:PTC_RK + ct + 1])
            for i in range(2):
                link(TT(LQ[2 * i], LQ[2 * i], LQ[2 * i + 1], ALU.mult))
                s = dve.tensor_reduce(LAM[:, i:i + 1], LQ[2 * i], AX_X, ALU.add)
            s.then_inc(lam_s, 1)

            norm(n1, lambda tt: XT[:, tt % 2], lambda tt: XN[:, tt % 2], SS, RS, GB[:, :], "mix",
                 lambda tt, b: HH[:, 4 * b:4 * b + 4, tt * P:(tt + 1) * P], lambda tt, b: HL[:, 4 * b:4 * b + 4, tt * P:(tt + 1) * P])

            dve.wait_ge(lam_e, 1)
            link(TT(LAM[:, 2:3], LAM[:, 1:2], LAM[:, 0:1], ALU.subtract))
            link(TS(LAM[:, 2:3], LAM[:, 2:3], -LAM_INIT, None, ALU.add))
            dve.wait_ge(tab_in, 16)

            def d_max(u):
                h, qb = u // 8, u % 8
                if qb == 0 and h:
                    link(TS(TAB[:, :], TAB[:, :], DIFF_SLOPES[h] / DIFF_SLOPES[h - 1], None, ALU.mult))
                for i, c in enumerate((1, 0)):
                    n = 2 * u + c
                    dve.wait_ge(qk_done, 2 * u + i + 1)
                    if u >= 2 and c == 1:
                        dve.wait_ge(comb_done, u - 1)
                    if u >= 2 and c == 0:
                        dve.wait_ge(tr_done, 2 * (u - 1))
                    t0 = 896 - P * qb
                    ins = dve.tensor_tensor_reduce(E_[:, n % 4, :].rearrange("p (b c) -> p b c", c=512), PS[:, 2 * c:2 * c + 2, :],
                                                   TAB[:, t0:t0 + T].rearrange("p (b c) -> p b c", c=512), 1.0, -3.0e38, ALU.add, ALU.max,
                                                   MD[:, n % 4:n % 4 + 1])
                    ins.then_inc(s_read, 1)
                    dve.wait_ge(s_read, 2 * u + i + 1)
                    TS(NMD[:, n % 4:n % 4 + 1], MD[:, n % 4:n % 4 + 1], -1.0, None, ALU.mult).then_inc(nm_done, 1)

            def d_sums(h):
                dve.wait_ge(sq_done, h + 1)
                dve.tensor_reduce(HS, BQ[:, h, :].rearrange("p (t c) -> p t c", t=NT), AX_X, ALU.add).then_inc(hs_done, 1)

            def d_scale(h):
                dve.wait_ge(hstd, h + 1)
                link(dve.reciprocal(HR, HS))
                o = OB[:, h % 2]
                link(TT(o, o, HR.unsqueeze(2).broadcast_to([P, NT, 128]), ALU.mult))
                link(TS(o, o, 1.0 - LAM_INIT, None, ALU.mult))
                TT(BQ[:, h, :].rearrange("p (t c) -> p t c", t=NT), o, SUB.unsqueeze(1).broadcast_to([P, NT, 128]), ALU.mult).then_inc(hn_done, 1)

            d_max(0)
            d_max(1)
            for u in range(32):
                dve.wait_ge(exp_done, 2 * u + 2)
                k = 4 * (u % 2)
                e0, e1 = (2 * u) % 4, (2 * u + 1) % 4
                if u >= 2:
                    dve.wait_ge(o_evac, u - 1)
                link(dve.reciprocal(CO[:, k:k + 2], LD[:, e0:e0 + 2]))
                link(TS(CO[:, k + 2:k + 3], LD[:, e0:e0 + 1], CO[:, k + 1:k + 2], LAM[:, 2:3], ALU.mult, ALU.mult))
                STT(E_[:, e0, :], E_[:, e1, :], CO[:, k + 2:k + 3], E_[:, e0, :], ALU.mult, ALU.add).then_inc(comb_done, 1)
                if u + 2 < 32:
                    d_max(u + 2)
                if u % 8 == 1 and u > 8:
                    d_sums(u // 8 - 1)
                if u % 8 == 3 and u > 8:
                    d_scale(u // 8 - 1)
            d_sums(3)
            d_scale(3)

            dve.wait_ge(job_evac, 4 * (NJ - 1))
            for ct in range(2):
                for half in range(2):
                    for hp in range(2):
                        rows, other, t = slice(64 * hp, 64 * hp + 64), slice(64 - 64 * hp, 128 - 64 * hp), slice(512 * half, 512 * half + 512)
                        STT(QW[other, 2 * ct + hp, t], PS[rows, 4 * ((NJ - 2) % 2) + 2 * ct + half, :], 0.125, QW[rows, 2 * ct + hp, t].bitcast(F32),
                            ALU.mult, ALU.subtract)
            dve.wait_ge(job_evac, 4 * (NJ - 1) + 2)
            for half in range(2):
                for kv in range(2):
                    for hp in range(2):
                        rows, t = slice(64 * kv, 64 * kv + 64), slice(512 * half, 512 * half + 512)
                        ins = TT(KW[64 * hp:64 * hp + 64, kv, 1, t], PS[rows, 4 * ((NJ - 1) % 2) + half, :], KW[rows, kv, 0, t].bitcast(F32), ALU.subtract)
            ins.then_inc(qw_lo, 1)
            dve.wait_ge(wb_in, 16)

            def w_max(u):
                _, kv, first, nk = window(u)
                off, n, m = (first - (u // 2 - 1)) * P, nk * P, WM[:, 2 * (u % 3):2 * (u % 3) + 2]
                dve.wait_ge(w_qk, u + 1)
                if u >= 3:
                    dve.wait_ge(w_tr, u - 2)
                for g in range(2):
                    ins = dve.tensor_tensor_reduce(WP_[:, u % 3, g, 0:n], PS[:, 2 * (u % 2) + g, 0:n], WB_[:, 2 * kv + g, off:off + n], 1.0, -3.0e38,
                                                   ALU.add, ALU.max, m[:, g:g + 1])
                link(ins)
                sink = SINK[:, 2 * kv:2 * kv + 2]
                link(TT(m, m, sink, ALU.max))
                link(TT(WSNK[:, 2 * (u % 3):2 * (u % 3) + 2], sink, m, ALU.subtract))
                TS(m, m, -1.0, None, ALU.mult).then_inc(w_nm, 1)

            def w_norm(u):
                _, _, _, nk = window(u)
                c = slice(2 * (u % 3), 2 * (u % 3) + 2)
                dve.wait_ge(w_exp, u + 1)
                link(TT(WR[:, c], WSUM[:, c], WSNK[:, c], ALU.add))
                link(dve.reciprocal(WR[:, c], WR[:, c]))
                pr = WP_[:, u % 3, :, 0:nk * P]
                TT(pr, pr, WR[:, c].unsqueeze(2).broadcast_to([P, 2, nk * P]), ALU.mult).then_inc(w_p, 1)

            w_max(0)
            w_max(1)
            w_norm(0)
            for u in range(NWU):
                if u + 2 < NWU:
                    w_max(u + 2)
                if u + 1 < NWU:
                    w_norm(u + 1)

            dve.wait_ge(w_mix, NWU)
            dve.wait_ge(pads, 1)
            dve.wait_ge(job_evac, 4 * NJ)
            for c in (4, 5, 2, 3, 6, 7, 0, 1):
                link(TS(CV[:, c, :], CIN[:, c, 0:T], col(PTC_CONV + c), None, ALU.mult))
                link(STT(CV[:, c, :], CIN[:, c, 1:T + 1], col(PTC_CONV + 8 + c), CV[:, c, :], ALU.mult, ALU.add))
                ins = STT(CV[:, c, :], CIN[:, c, 2:T + 2], col(PTC_CONV + 16 + c), CV[:, c, :], ALU.mult, ALU.add)
            ins.then_inc(r_conv, 1)
            dve.wait_ge(r_conv, 1)
            for ct in range(2):
                ins = TS(KK[:, ct, :], CV[:, 2 + ct, :], col(PTC_KK + ct), None, ALU.mult)
            ins.then_inc(r_sq, 1)
            dve.wait_ge(r_std, 1)
            link(TS(S2_[:, :, :], S2_[:, :, :], 1e-12, None, ALU.max))
            link(dve.reciprocal(S2_[:, :, :], S2_[:, :, :]))
            TT(KK[:, :, :], KK[:, :, :], S2_[:, :, :], ALU.mult).then_inc(r_kk, 1)

            def ch(t):
                return t[:, :, :].rearrange("p a (c k) -> p (a c) k", k=C)

            def slot(t, i):
                return t[:, i].rearrange("p a c k -> p (a c) k")

            for d in range(2):
                dve.wait_ge(r_sig, d + 1)
                link(TS(S1_[:, :, :], S1_[:, :, :], -E05, None, ALU.mult))
                dve.wait_ge(r_scm, d + 1)
                for ct in range(2):
                    ins = dve.tensor_tensor_scan(S2_[:, ct, :], SCM[:, :], S1_[:, ct, :], 0.0, ALU.mult, ALU.add)
                link(ins)
                link(TS(HT[:, :], S2_[:, :, C - 1:T:C].rearrange("p a c -> p (a c)"), 0.5, None, ALU.mult))
                link(TT(ch(S2_), ch(S2_), HT[:, :].unsqueeze(2).broadcast_to([P, 32, C]), ALU.subtract))
                TT(S1_[:, :, :], S2_[:, :, :], S1_[:, :, :], ALU.subtract).then_inc(r_c, 1)
                dve.wait_ge(r_exp, d + 1)
                for ct in range(2):
                    ins = TS(S2_[:, ct, :], S3_[:, ct, :], -1.0, col(PTC_KA + ct), ALU.add, ALU.mult)
                link(ins)
                link(STT(S2_[:, :, :], S2_[:, :, :], 1.0, CV[:, 2:4, :], ALU.add, ALU.mult))
                if d == 0:
                    dve.tensor_copy(KS[:, :, :], S2_[:, :, :])
                else:
                    TT(KS[:, :, :], KS[:, :, :], S2_[:, :, :], ALU.add)
                TT(slot(BKt, 1), ch(S2_), slot(BKt, 0), ALU.mult)
                link(TT(S3_[:, :, :], S3_[:, :, :], KK[:, :, :], ALU.mult))
                TT(slot(BKt, 0), ch(S3_), slot(BKt, 0), ALU.mult)
                TT(slot(KR, 1), slot(KR, 1), CV[:, 0:2, :].rearrange("p a (c k) -> p (a c) k", k=C), ALU.mult)
                TT(slot(KR, 0), slot(KR, 0), ch(KK), ALU.mult)
                link(dve.memset(DD[:, :], 0.0))
                e2, d2 = EH[:, :].rearrange("p (a c) -> p a c", a=2), DD[:, :].rearrange("p (a c) -> p a c", a=2)
                dst = d2[:, :, 0:15] if d == 0 else d2[:, :, 1:16]
                TT(dst, e2[:, :, 0:15], e2[:, :, 1:16], ALU.mult).then_inc(r_pre, 1)
                for b in range(NB):
                    n = d * NB + b
                    pe0, dv0 = G_PE * n, G_DVE * n
                    dve.wait_ge(g_pe, pe0 + 1)
                    for k in range(4):
                        ins = TT(G1[:, k].rearrange("p a b c k -> p (a b) (c k)"), PS[:, k, :].rearrange("p (a c) -> p a c", c=128),
                                 CN[:, C_MASK[d]:C_MASK[d] + 128].unsqueeze(1).broadcast_to([P, 4, 128]), ALU.mult)
                    ins.then_inc(g_dve, 1)
                    dve.wait_ge(g_pe, pe0 + 2)
                    q = QQ[:, 0]
                    for hp in range(2):
                        for t in range(2):
                            ins = TT(QQ[:, 0, 4 * t + 2 * hp:4 * t + 2 * hp + 2, :], PS[:, 4 + hp, 128 * t:128 * t + 128].rearrange("p (a k) -> p a k", k=C),
                                     CN[:, C_LT[1 - d]:C_LT[1 - d] + 64].unsqueeze(1).broadcast_to([P, 2, 64]), ALU.mult)
                    link(ins)
                    TT(q, q, I64.unsqueeze(1).broadcast_to([P, 8, 64]), ALU.subtract).then_inc(g_dve, 1)
                    for l in range(5):
                        dve.wait_ge(g_pe, pe0 + 7 + 2 * l)
                        if l == 0:
                            dve.wait_ge(g_pool, 6 * n + 1)
                        if l < 4:
                            qq = QQ[:, :, :, :].rearrange("p a u k -> p a (u k)")
                            TT(qq, PS[:, 3:5, :], qq, ALU.add).then_inc(g_dve, 1)
                        else:
                            qq = QQ[:, 1].rearrange("p u k -> p (u k)")
                            TT(qq, PS[:, 4, :], qq, ALU.add).then_inc(g_dve, 1)
                    dve.wait_ge(g_pe, pe0 + 17)
                    for cp in range(2):
                        cs = slice(4 * b + cp, 4 * b + 4, 2)
                        g = KR[:, 1, :, cs, :].rearrange("p a t k -> p t a k")
                        TT(g, PS[:, cp, 0:256].rearrange("p (t a k) -> p t a k", t=2, a=2), g, ALU.add)
                        m = BKt[:, 0, :, cs, :].rearrange("p a t k -> p t a k")
                        TT(m, PS[:, cp, 256:512].rearrange("p (t a k) -> p t a k", t=2, a=2),
                           I64.unsqueeze(1).unsqueeze(1).broadcast_to([P, 2, 2, 64]), ALU.add)
                    dve.wait_ge(g_pe, pe0 + 18)
                    y = YY[:, 2 * b:2 * b + 2].rearrange("p t b a k -> p (t b a k)")
                    if d == 0:
                        dve.tensor_copy(y, PS[:, 7, :]).then_inc(g_dve, 1)
                    else:
                        TT(y, PS[:, 7, :], y, ALU.add).then_inc(g_dve, 1)
                dve.wait_ge(g_act, G_ACT * NB * (d + 1))
                dve.wait_ge(g_dve, G_DVE * NB * (d + 1))
                order = list(range(NCH)) if d == 0 else list(range(NCH - 1, -1, -1))
                link(TT(slot(BKt, 1), slot(BKt, 1), DD[:, :].unsqueeze(2).broadcast_to([P, 32, C]), ALU.mult))
                dve.memset(KR[:, 0, :, order[0], :], 0.0)
                dve.tensor_copy(KR[:, 0, :, order[1], :], BKt[:, 1, :, order[0], :]).then_inc(c_z, 1)
                for i in range(1, NCH - 1):
                    dve.wait_ge(c_mm, 14 * d + i)
                    for ct in range(2):
                        ins = STT(KR[:, 0, ct, order[i + 1], :], PS[:, 0, 64 * ct:64 * ct + 64], DD[:, 16 * ct + order[i]:16 * ct + order[i] + 1],
                                  BKt[:, 1, ct, order[i], :], ALU.mult, ALU.add)
                    ins.then_inc(c_z, 1)
                for q4 in range(2):
                    dve.wait_ge(y_mm, 2 * d + q4 + 1)
                    for hp in range(2):
                        y = YY[:, 4 * q4:4 * q4 + 4, hp].rearrange("p t a k -> p t (a k)")
                        TT(y, PS[:, 2 + 2 * q4 + hp, :].rearrange("p (t c) -> p t c", t=4), y, ALU.add).then_inc(y_add, 1)
            dve.wait_ge(y_add, 8)
            TT(CV[:, 0:2, :], CV[:, 0:2, :], KS[:, :, :], ALU.mult).then_inc(p_bon, 1)
            y32 = YY[:, :, :, :, :].rearrange("p t b a k -> p (t b a) k")
            y8 = YY[:, :, :, :, :].rearrange("p t b a k -> p t (b a k)")
            v32 = VT[:, :, :, :, :].rearrange("p t b a k -> p (t b a) k")
            link(dve.tensor_reduce(GM, y32, AX_X, ALU.add))
            link(TS(GM, GM, 1.0 / C, None, ALU.mult))
            TT(y32, y32, GM.unsqueeze(2).broadcast_to([P, 32, C]), ALU.subtract).then_inc(p_s, 1)
            dve.wait_ge(p_std, 1)
            dve.tensor_reduce(GV, S2_[:, :, :].rearrange("p a (c k) -> p (a c) k", k=C), AX_X, ALU.add).then_inc(p_s, 1)
            dve.wait_ge(p_std, 2)
            link(dve.reciprocal(GS, GV))
            link(TT(y32, y32, GS.unsqueeze(2).broadcast_to([P, 32, C]), ALU.mult))
            link(TT(y8, y8, LNG.unsqueeze(1).broadcast_to([P, NT, 256]), ALU.mult))
            link(TT(y8, y8, LNB.unsqueeze(1).broadcast_to([P, NT, 256]), ALU.add))
            dve.wait_ge(p_bon, 2)
            link(TT(v32, v32, BON.unsqueeze(2).broadcast_to([P, 32, C]), ALU.mult))
            link(TT(y32, y32, v32, ALU.add))
            dve.wait_ge(p_mm, 2)
            gate = PS[:, 4:8, :].rearrange("p n (t b a k) -> p (n t) b a k", t=2, b=2, a=2)
            for hp in range(2):
                ins = TT(YF[:, :, :, hp, :], gate[:, :, hp], YY[:, :, hp], ALU.mult)
            ins.then_inc(p_y, 1)
            dve.wait_ge(p_tr, 4)
            for k in range(8):
                src = (4, 5, 0, 1, 2, 3, 6, 7)[k]
                dve.wait_ge(mix_hi, k + 1)
                TT(HL[:, k, :], MIX[:, src, :], HH[:, k, :].bitcast(F32), ALU.subtract).then_inc(mix_lo, 1)
            mt = "p a (k t) -> p (a k) t"
            norm(nm, lambda tt: MX[:, tt], lambda tt: XN2[:, tt], MS, MR, GBM[:, :], "mem",
                 lambda tt, b: AH[:, :, :].rearrange(mt, k=4)[:, 4 * b:4 * b + 4, tt * P:(tt + 1) * P],
                 lambda tt, b: AL[:, :, :].rearrange(mt, k=4)[:, 4 * b:4 * b + 4, tt * P:(tt + 1) * P])

            def add_x(j, i):
                dve.wait_ge(w_used, end2[j])
                for k in range(4):
                    xs = X[:, 2 * k:2 * k + 2, i * PW:(i + 1) * PW]
                    ins = TT(xs, PS[:, 4 * (j % 2) + k, :].rearrange("p (t c) -> p t c", t=2), xs, ALU.add)
                ins.then_inc(job2_dve, 1)

            dve.wait_ge(x_in, 16 * NT)
            for i in range(4):
                add_x(i, i)
            dve.wait_ge(job2_dve, 4)
            norm(n2, lambda tt: X[:, tt], lambda tt: XN2[:, tt % 2], AS, AR, GBC[:, :], "cross",
                 lambda tt, b: HH[:, 4 * b:4 * b + 4, tt * P:(tt + 1) * P], lambda tt, b: HL[:, 4 * b:4 * b + 4, tt * P:(tt + 1) * P])
            def c_prob(qb):
                c = slice(4 * (qb % 2), 4 * (qb % 2) + 4)
                dve.wait_ge(c_qk, qb + 1)
                link(dve.tensor_reduce(CM[:, c], PS[:, 6 * (qb % 2):6 * (qb % 2) + 2, :].rearrange("p b (h c) -> p (b h) c", h=2), AX_X, ALU.max))
                TS(CM[:, c], CM[:, c], -(128 ** -0.5), None, ALU.mult).then_inc(c_max, 1)
                dve.wait_ge(c_exp, qb + 1)
                link(dve.reciprocal(CR[:, c], CL[:, c]))
                p4 = CP[:, qb % 2, :].rearrange("p (h c) -> p h c", h=4)
                TT(p4, p4, CR[:, c].unsqueeze(2).broadcast_to([P, 4, 256]), ALU.mult).then_inc(c_p, 1)

            def c_second(qb):
                dve.wait_ge(c_hi, qb + 1)
                TT(AL[:, :, qb * P:(qb + 1) * P], PS[:, 4 + qb % 2, :].rearrange("p (k t) -> p k t", k=4),
                   AH[:, :, qb * P:(qb + 1) * P].bitcast(F32), ALU.subtract).then_inc(c_lo, 1)

            c_prob(0)
            for qb in range(NT):
                if qb + 1 < NT:
                    c_prob(qb + 1)
                if qb:
                    c_second(qb - 1)
            c_second(NT - 1)
            for i in range(4):
                add_x(10 + i, i)
            dve.wait_ge(job2_dve, 8)
            norm(n3, lambda tt: X[:, tt], lambda tt: XN2[:, tt % 2], BS, BR, GBF[:, :], "ffn",
                 lambda tt, b: HH[:, 4 * b:4 * b + 4, tt * P:(tt + 1) * P], lambda tt, b: HL[:, 4 * b:4 * b + 4, tt * P:(tt + 1) * P])
            for i in range(FF_ITERS + 1):
                if i < FF_ITERS:
                    dve.wait_ge(w_used, ff0(i) + 8)
                    for k in range(4):
                        c0 = 512 * (k % 2)
                        dve.wait_ge(f_silu, 4 * i + k + 1)
                        if i:
                            dve.wait_ge(f_lo, 4 * (i - 1) + k + 1)
                        TT(FU[:, k // 2, c0:c0 + 512], PS[:, 4 + k, :], ACTB[:, k // 2, c0:c0 + 512], ALU.mult).then_inc(f_mul, 1)
                    for k in range(4):
                        c0, a = 512 * (k % 2), 2 * (i % 2) + k // 2
                        dve.wait_ge(f_hi, 4 * i + k + 1)
                        TT(AL[:, a, c0:c0 + 512], FU[:, k // 2, c0:c0 + 512], AH[:, a, c0:c0 + 512].bitcast(F32), ALU.subtract).then_inc(f_lo, 1)
                if i:
                    for s in range(4):
                        dve.wait_ge(w_used, ff0(i) + (8 if i < FF_ITERS else 0) + s + 1)
                        if i > 1:
                            dve.wait_ge(f_add, 16 * (i - 2) + 4 * s + 4)
                        for k in range(4):
                            xs = X[:, 2 * k:2 * k + 2, s * PW:(s + 1) * PW]
                            TT(xs, PS[:, 4 * (s % 2) + k, :].rearrange("p (t c) -> p t c", t=2), xs, ALU.add).then_inc(f_add, 1)
            dve.wait_ge(gain_in["final"], 16)
            for tt in range(NT):
                dve.wait_ge(l_std, tt + 1)
                link(dve.reciprocal(FR[:, tt:tt + 1], FS[:, tt:tt + 1]))
                STT(FO[:, tt % 2], X[:, tt], FR[:, tt:tt + 1], GBL[:, :], ALU.mult, ALU.mult).then_inc(l_o, 1)

        @block.tensor
        def _(pe):
            piece = [0]

            def take():
                p = piece[0]
                piece[0] += 1
                pe.wait_ge(w_hi, p + 1)
                pe.wait_ge(w_lo, p + 1)
                return WH[:, p % NW], WL[:, p % NW]

            def feature_job(npieces, ah, al, where, starts=lambda ct, i: True, cts=(0, 1), cols=((0, 512), (512, 512)), extra=None):
                for q in range(npieces):
                    wh, wl = take()
                    for k in range(PK):
                        kt = q * PK + k
                        first, last = kt == 0, kt == npieces * PK - 1
                        for ct in cts:
                            c = slice(ct * P, ct * P + P)
                            for i, (t0, n) in enumerate(cols):
                                pe.matmul(where(ct, i), wh[:, k, c], ah(kt)[:, t0:t0 + n], start=first and starts(ct, i), stop=False, skip_group_check=True)
                                pe.matmul(where(ct, i), wh[:, k, c], al(kt)[:, t0:t0 + n], start=False, stop=False, skip_group_check=True)
                            for i, (t0, n) in enumerate(cols):
                                mm = pe.matmul(where(ct, i), wl[:, k, c], ah(kt)[:, t0:t0 + n], start=False, stop=last, skip_group_check=True)
                        if extra:
                            mm = extra(wh, wl, k, kt, first, last)
                    mm.then_inc(w_used, 1)

            def token_mm(dst, wh, wl, ah, al, kt, tt, start, last):
                t = slice(tt * P, tt * P + P)
                pe.matmul(dst, ah(kt)[:, t], wh, start=start, stop=False, skip_group_check=True)
                pe.matmul(dst, ah(kt)[:, t], wl, start=False, stop=False, skip_group_check=True)
                return pe.matmul(dst, al(kt)[:, t], wh, start=False, stop=last, skip_group_check=True)

            def token_job(npieces, ah, al, bank, nt=NT):
                for q in range(npieces):
                    wh, wl = take()
                    for k in range(PK):
                        kt = q * PK + k
                        for tt in range(nt):
                            mm = token_mm(PS[:, bank + tt // 2, 256 * (tt % 2):256 * (tt % 2) + 256], wh[:, k, :], wl[:, k, :], ah, al, kt, tt,
                                          kt == 0 and tt % 2 == 0, kt == npieces * PK - 1)
                    mm.then_inc(w_used, 1)

            def norm(nn, src):
                for tt in range(nn.n):
                    pe.wait_ge(nn.xn, tt + 1)
                    for b in range(2):
                        if tt >= 4:
                            pe.wait_ge(nn.lo, 2 * (tt - 4) + b + 1)
                        for k in range(4):
                            kt = 4 * b + k
                            mm = pe.transpose(PS[:, 2 * (tt % 4) + b, k * P:(k + 1) * P], src(tt)[:, kt * P:(kt + 1) * P], ID)
                        mm.then_inc(nn.tr, 1)
                pe.wait_ge(nn.lo, 2 * nn.n)

            hh, hl = (lambda kt: HH[:, kt, :]), (lambda kt: HL[:, kt, :])

            pe.wait_ge(consts_in, 16)
            pe.wait_ge(vecs_in, 16 * 20)
            pe.transpose(PS[:, 7, 0:38], VROWS, ID[0:38, 0:38]).then_inc(vec_t, 1)
            pe.wait_ge(vec_c, 1)
            norm(n1, lambda tt: XN[:, tt % 2])

            def proj(j):
                if j >= 2:
                    pe.wait_ge(job_evac, 4 * (j - 1))
                c0, bank = proj_cols[j], 4 * (j % 2)
                if BV0 <= c0 < CI0:
                    token_job(4, hh, hl, bank)
                elif c0 == AK0:
                    def values(wh, wl, k, kt, first, last):
                        for tt in range(NT):
                            mm = token_mm(PS[:, bank + 2 + tt // 4, P * (tt % 4):P * (tt % 4) + P], wh[:, k, P:2 * P], wl[:, k, P:2 * P], hh, hl, kt, tt,
                                          first and tt % 4 == 0, last)
                        return mm

                    feature_job(4, hh, hl, lambda ct, i: PS[:, bank + i, :], cts=(0,), extra=values)
                else:
                    feature_job(4, hh, hl, lambda ct, i: PS[:, bank + 2 * ct + i, :])

            for j in range(6):
                proj(j)

            pe.wait_ge(job_evac, 24)

            def d_scores(u):
                h, qb = u // 8, u % 8
                for i, c in enumerate((1, 0)):
                    if u:
                        pe.wait_ge(s_read, 2 * (u - 1) + i + 1)
                    if i == 0:
                        pe.wait_ge(q_staged, u // 2 + 1)
                        pe.wait_ge(k_staged, h + 1)
                    for part in range(2):
                        for half in range(2):
                            mm = pe.matmul(PS[:, 2 * c + half, :], QST[:, u // 2 % 2, part, c, P * (u % 2):P * (u % 2) + P],
                                           KST[:, h % 2, c, 512 * half:512 * half + 512], start=part == 0, stop=part == 1, skip_group_check=True)
                    mm.then_inc(qk_done, 1)

            def d_head(h):
                pe.wait_ge(hn_done, h + 1)
                for b in range(2):
                    if b or h:
                        pe.wait_ge(hm_evac, 2 * h + b)
                    for k in range(4):
                        tt = 4 * b + k
                        mm = pe.transpose(PS[:, 7, k * P:(k + 1) * P], BQ[:, h, tt * P:(tt + 1) * P], ID)
                    mm.then_inc(ht_done, 1)

            d_scores(0)
            d_scores(1)
            for u in range(32):
                h, qb = u // 8, u % 8
                if u + 2 < 32:
                    d_scores(u + 2)
                pe.wait_ge(comb_done, u + 1)
                for b in range(2):
                    if u:
                        pe.wait_ge(at_evac, 2 * (u - 1) + b + 1)
                    for k in range(4):
                        kt = 4 * b + k
                        mm = pe.transpose(PS[:, 4 + b, k * P:(k + 1) * P], E_[:, (2 * u) % 4, kt * P:(kt + 1) * P], ID)
                    mm.then_inc(tr_done, 1)
                pe.wait_ge(at_evac, 2 * u + 2)
                if u:
                    pe.wait_ge(o_evac, u)
                for kt in range(NT):
                    mm = pe.matmul(PS[:, 6, 0:P], AT_[:, kt * P:(kt + 1) * P], BV[:, kt, h * P:(h + 1) * P], start=(kt == 0), stop=(kt == NT - 1))
                mm.then_inc(pv_done, 1)
                if qb == 4 and h:
                    d_head(h - 1)
            d_head(3)
            pe.wait_ge(hm_evac, 8)

            for j in range(6, NJ):
                proj(j)
            pe.wait_ge(job_evac, 4 * NJ)

            pe.wait_ge(qw_lo, 1)

            def w_scores(u):
                qb, kv, first, nk = window(u)
                if u >= 2:
                    pe.wait_ge(w_nm, u - 1)
                for g in range(2):
                    for part in range(2):
                        mm = pe.matmul(PS[:, 2 * (u % 2) + g, 0:nk * P], QW[:, 2 * kv + g, qb * P:(qb + 1) * P], KW[:, kv, part, first * P:(first + nk) * P],
                                       start=part == 0, stop=part == 1, skip_group_check=True)
                mm.then_inc(w_qk, 1)

            def w_values(u):
                qb, kv, first, nk = window(u)
                pe.wait_ge(w_pt, u + 1)
                if u >= 2:
                    pe.wait_ge(w_mix, u - 1)
                for k in range(nk):
                    for g in range(2):
                        mm = pe.matmul(PS[64 * g:64 * g + 64, 6 + u % 2, 0:P], AV[:, first + k, 64 * kv:64 * kv + 64], WT_[:, u % 2, nk * g + k, :],
                                       start=k == 0, stop=k == nk - 1, skip_group_check=True)
                mm.then_inc(w_pv, 1)

            w_scores(0)
            w_scores(1)
            for u in range(NWU):
                _, _, _, nk = window(u)
                if u + 2 < NWU:
                    w_scores(u + 2)
                pe.wait_ge(w_p, u + 1)
                if u:
                    pe.wait_ge(w_pt, u)
                for g in range(2):
                    for k in range(nk):
                        i = nk * g + k
                        mm = pe.transpose(PS[:, 4 + i // 4, P * (i % 4):P * (i % 4) + P], WP_[:, u % 3, g, k * P:(k + 1) * P], ID)
                mm.then_inc(w_tr, 1)
                if u:
                    w_values(u - 1)
            w_values(NWU - 1)
            pe.wait_ge(w_mix, NWU)

            pe.wait_ge(r_conv, 1)
            for tt in range(NT):
                for ct in range(2):
                    mm = pe.transpose(PS[:, tt // 2, 256 * (tt % 2) + P * ct:256 * (tt % 2) + P * ct + P], CV[:, 4 + ct, tt * P:(tt + 1) * P], ID)
                if tt % 2:
                    mm.then_inc(r_vt, 1)
            pe.wait_ge(r_act, 1)
            for ct in range(2):
                for half in range(2):
                    mm = pe.matmul(PS[:, 4 + 2 * ct + half, :], ONES, S1_[:, ct, 512 * half:512 * half + 512], start=True, stop=True)
            mm.then_inc(r_kn, 1)
            pe.wait_ge(r_act, 3)
            pe.wait_ge(r_vte, NT)
            pe.wait_ge(r_kk, 1)

            def tok(t, i, ct, tile):
                return t[:, i, ct, 2 * tile:2 * tile + 2, :].rearrange("p c k -> p (c k)")

            for d in range(2):
                for ct in range(2):
                    for half in range(2):
                        t0 = 512 * half
                        pe.matmul(PS[:, 2 * ct + half, :], WA[0:64, d, P * ct:P * ct + P], CV[0:64, 6, t0:t0 + 512], start=True, stop=True)
                        mm = pe.matmul(PS[:, 4 + 2 * ct + half, :], WA[64:128, d, P * ct:P * ct + P], CV[64:128, 6, t0:t0 + 512], start=True, stop=True)
                mm.then_inc(r_z, 1)
                pe.wait_ge(r_pre, d + 1)
                pe.wait_ge(r_exp, d + 1)
                for b in range(NB):
                    n = d * NB + b
                    dv0, ac0, po0 = G_DVE * n, G_ACT * n, G_POOL * n
                    if n:
                        pe.wait_ge(g_dve, dv0)
                        pe.wait_ge(g_act, ac0)
                    for kind in range(2):
                        for t in range(2):
                            for h2 in range(2):
                                for cp in range(2):
                                    for hp in range(2):
                                        cq = cp ^ hp
                                        c, r = 4 * b + 2 * t + cq, slice(64 * hp, 64 * hp + 64)
                                        mm = pe.matmul(PS[64 * cq:64 * cq + 64, 2 * t + hp, 256 * kind + 128 * h2:256 * kind + 128 * h2 + 128],
                                                       BKt[r, kind, h2, c, :], KR[r, :, h2, c, :], start=True, stop=True, skip_group_check=True)
                    mm.then_inc(g_pe, 1)
                    for t in range(2):
                        for h2 in range(2):
                            for cp in range(2):
                                for hp in range(2):
                                    cq = cp ^ hp
                                    c, r = 4 * b + 2 * t + cq, slice(64 * hp, 64 * hp + 64)
                                    mm = pe.matmul(PS[64 * cq:64 * cq + 64, 4 + hp, 128 * t + 64 * h2:128 * t + 64 * h2 + 64],
                                                   KR[r, 0, h2, c, :], BKt[r, 0, h2, c, :], start=True, stop=True, skip_group_check=True)
                    mm.then_inc(g_pe, 1)

                    def turn(bank, t4, i):
                        for t in range(2):
                            for ct in range(2):
                                o = PS[:, bank, 256 * t:256 * t + 256].rearrange("p (b a k) -> p a b k", b=2, a=2)[:, ct]
                                m = pe.transpose(o, tok(t4, i, ct, 2 * b + t), ID)
                        return m

                    turn(6, KR, 0)
                    turn(7, BKt, 0).then_inc(g_pe, 1)
                    pe.wait_ge(g_dve, dv0 + 1)
                    turn(0, BKt, 1).then_inc(g_pe, 1)

                    def units():
                        for t in range(2):
                            for hp in range(2):
                                for h2 in range(2):
                                    for cp in range(2):
                                        yield t, hp, h2, cp, 4 * t + 2 * hp + h2, slice(64 * cp, 64 * cp + 64)

                    def vtok(t, hp, h2, r):
                        return VT[r, 4 * (b // 2) + 2 * (b % 2) + t, hp, h2, :]

                    for t, hp, h2, cp, u, r in units():
                        mm = pe.matmul(PS[r, 1, 64 * u:64 * u + 64], G1[r, 2 * t + hp, 1, h2, 0, :], vtok(t, hp, h2, r), start=True, stop=True, skip_group_check=True)
                    mm.then_inc(g_pe, 1)
                    for l in range(5):
                        pe.wait_ge(g_pool, po0 + 2 + l)
                        pe.wait_ge(g_dve, dv0 + 2 + l)
                        for t, hp, h2, cp, u, r in units():
                            mm = pe.matmul(PS[r, 2, 64 * u:64 * u + 64], LT[r, u, :], QQ[r, 0, u, :], start=True, stop=True, skip_group_check=True)
                        mm.then_inc(g_pe, 1)
                        pe.wait_ge(g_act, ac0 + 5 + l)
                        if l < 4:
                            for t, hp, h2, cp, u, r in units():
                                pe.matmul(PS[r, 3, 64 * u:64 * u + 64], QQ[r, 1, u, :], XX[r, u, :], start=True, stop=True, skip_group_check=True)
                        for t, hp, h2, cp, u, r in units():
                            mm = pe.matmul(PS[r, 4, 64 * u:64 * u + 64], XX[r, u, :], QQ[r, 1, u, :], start=True, stop=True, skip_group_check=True)
                        mm.then_inc(g_pe, 1)
                    pe.wait_ge(g_dve, dv0 + 7)
                    for t, hp, h2, cp, u, r in units():
                        mm = pe.matmul(PS[r, 5 + t, 128 * (u % 4):128 * (u % 4) + 128], QQ[r, 1, u, :], RH[r, u, :, :].rearrange("p b k -> p (b k)"),
                                       start=True, stop=True, skip_group_check=True)
                    mm.then_inc(g_pe, 1)
                    pe.wait_ge(g_act, ac0 + 10)
                    for t in range(2):
                        for h2 in range(2):
                            for hp in range(2):
                                for cq in range(2):
                                    cp = cq ^ hp
                                    u, r, o = 4 * t + 2 * hp + h2, slice(64 * cp, 64 * cp + 64), slice(64 * hp, 64 * hp + 64)
                                    f = 128 * t + 64 * h2
                                    pe.matmul(PS[o, cp, f:f + 64], WU[r, u, 0, :], G1[r, 2 * t + hp, 0, h2, 1, :], start=True, stop=True, skip_group_check=True)
                                    pe.matmul(PS[o, cp, 256 + f:256 + f + 64], WU[r, u, 0, :], BT[r, u, :], start=True, stop=True, skip_group_check=True)
                                    pe.matmul(PS[o, 2 + cp, f:f + 64], KT[r, u, :], vtok(t, hp, h2, r), start=True, stop=False, skip_group_check=True)
                                    mm = pe.matmul(PS[o, 2 + cp, f:f + 64], BT[r, u, :], WU[r, u, 1, :], start=False, stop=True, skip_group_check=True)
                    mm.then_inc(g_pe, 1)
                    for t, hp, h2, cp, u, r in units():
                        pe.matmul(PS[r, 7, 64 * u:64 * u + 64], G1[r, 2 * t + hp, 1, h2, 1, :], vtok(t, hp, h2, r), start=True, stop=False, skip_group_check=True)
                        mm = pe.matmul(PS[r, 7, 64 * u:64 * u + 64], G1[r, 2 * t + hp, 0, h2, 1, :], WU[r, u, 1, :], start=False, stop=True, skip_group_check=True)
                    mm.then_inc(g_pe, 1)
                order = list(range(NCH)) if d == 0 else list(range(NCH - 1, -1, -1))
                for i in range(1, NCH - 1):
                    pe.wait_ge(c_z, 15 * d + i)
                    for ct in range(2):
                        for hp in range(2):
                            r = slice(64 * hp, 64 * hp + 64)
                            mm = pe.matmul(PS[r, 0, 64 * ct:64 * ct + 64], BKt[r, 0, ct, order[i], :], KR[r, 0, ct, order[i], :], start=True, stop=True, skip_group_check=True)
                    mm.then_inc(c_mm, 1)
                pe.wait_ge(c_z, 15 * d + 15)
                for q4 in range(2):
                    for t in range(4):
                        for h2 in range(2):
                            for cp in range(2):
                                for hp in range(2):
                                    cq = cp ^ hp
                                    c, r = 2 * (4 * q4 + t) + cq, slice(64 * hp, 64 * hp + 64)
                                    mm = pe.matmul(PS[64 * cq:64 * cq + 64, 2 + 2 * q4 + hp, 128 * t + 64 * h2:128 * t + 64 * h2 + 64],
                                                   KR[r, 1, h2, c, :], KR[r, 0, h2, c, :], start=True, stop=True, skip_group_check=True)
                    mm.then_inc(y_mm, 1)
                pe.wait_ge(y_add, 4 * (d + 1))

            pe.wait_ge(p_bon, 1)
            for tt in range(NT):
                for ct in range(2):
                    mm = pe.matmul(PS[:, 2, 4 * tt:4 * tt + 4], CV[:, ct, tt * P:(tt + 1) * P], RB[:, 4 * ct:4 * ct + 4], start=(ct == 0), stop=(ct == 1), skip_group_check=True)
            mm.then_inc(p_mm, 1)
            for tt in range(NT):
                mm = pe.matmul(PS[:, 4 + tt // 2, 256 * (tt % 2):256 * (tt % 2) + 256], CV[:, 7, tt * P:(tt + 1) * P], GU[:, :], start=True, stop=True, skip_group_check=True)
            mm.then_inc(p_mm, 1)
            pe.wait_ge(p_y, 1)
            for ct in range(2):
                for half in range(2):
                    if ct == 1 and half == 0:
                        pe.wait_ge(p_bon, 2)
                    for k in range(4):
                        mm = pe.transpose(PS[:, 2 * ct + half, k * P:(k + 1) * P], YF[:, 4 * half + k, ct].rearrange("p b k -> p (b k)"), ID)
                    mm.then_inc(p_tr, 1)

            pe.wait_ge(p_mix, 4)
            norm(nm, lambda tt: XN2[:, tt])
            mh, ml = ((lambda kt, t=t: t[:, kt // 4, 256 * (kt % 4):256 * (kt % 4) + 256]) for t in (AH, AL))
            oh, ol = (lambda kt: AH[:, kt, :]), (lambda kt: AL[:, kt, :])
            pe.wait_ge(mix_lo, 8)
            for j, (kind, i) in enumerate(jobs2):
                if j >= 2:
                    pe.wait_ge(*evac_of[j - 2])
                bank = 4 * (j % 2)
                if kind == "wout":
                    token_job(4, hh, hl, bank)
                elif kind == "wkv" and i < 2:
                    feature_job(4, mh, ml, lambda ct, _: PS[:, bank, 256 * ct:256 * ct + 256], starts=lambda ct, _: ct == 0, cols=((0, 256),))
                elif kind == "wkv":
                    token_job(4, mh, ml, bank, nt=2)
                elif kind == "wq":
                    if i == 0:
                        for e in evac_of[4:8]:
                            pe.wait_ge(*e)
                        norm(n2, lambda tt: XN2[:, tt % 2])
                    feature_job(4, hh, hl, lambda ct, k: PS[:, bank + 2 * ct + k, :])
                else:
                    if i == 0:
                        pe.wait_ge(*evac_of[9])
                        cross()
                    token_job(2, oh, ol, bank)
                if kind == "wq" and i == 1:
                    def cross():
                        def scores(qb):
                            if qb >= 2:
                                pe.wait_ge(c_exp, qb - 1)
                            for h in range(4):
                                mm = pe.matmul(PS[:, 6 * (qb % 2) + h // 2, 256 * (h % 2):256 * (h % 2) + 256], QC[:, h, qb * P:(qb + 1) * P], KM[:, h, :],
                                               start=True, stop=True, skip_group_check=True)
                            mm.then_inc(c_qk, 1)

                        def values(qb):
                            pe.wait_ge(c_pt, qb + 1)
                            if qb >= 2:
                                pe.wait_ge(c_lo, qb - 1)
                            for h in range(4):
                                for m in range(2):
                                    mm = pe.matmul(PS[:, 4 + qb % 2, P * h:P * h + P], VM[:, m, P * h:P * h + P], CPT[:, qb % 2, P * (2 * h + m):P * (2 * h + m) + P],
                                                   start=(m == 0), stop=(m == 1), skip_group_check=True)
                            mm.then_inc(c_pv, 1)

                        scores(0)
                        for qb in range(NT):
                            if qb + 1 < NT:
                                scores(qb + 1)
                            if qb:
                                values(qb - 1)
                            pe.wait_ge(c_p, qb + 1)
                            if qb:
                                pe.wait_ge(c_pt, qb)
                            for k in range(8):
                                mm = pe.transpose(PS[:, 2 + k // 4, P * (k % 4):P * (k % 4) + P], CP[:, qb % 2, P * k:P * k + P], ID)
                            mm.then_inc(c_tr, 1)
                        values(NT - 1)
                        pe.wait_ge(c_lo, NT)
            for e in evac_of[12:]:
                pe.wait_ge(*e)
            norm(n3, lambda tt: XN2[:, tt % 2])
            for i in range(FF_ITERS + 1):
                if i < FF_ITERS:
                    if i == 1:
                        pe.wait_ge(f_silu, 4)
                    elif i:
                        pe.wait_ge(f_add, 16 * (i - 2) + 12)
                    feature_job(4, hh, hl, lambda ct, k: PS[:, 2 * ct + k, :])
                    if i == 1:
                        pe.wait_ge(f_mul, 4)
                    elif i:
                        pe.wait_ge(f_add, 16 * (i - 2) + 16)
                    feature_job(4, hh, hl, lambda ct, k: PS[:, 4 + 2 * ct + k, :])
                if i:
                    m = i - 1
                    pe.wait_ge(f_lo, 4 * m + 4)
                    for s in range(4):
                        if s >= 2:
                            pe.wait_ge(f_add, 16 * m + 4 * (s - 1))
                        elif i < FF_ITERS:
                            pe.wait_ge(*((f_silu, 4 * i + 4) if s == 0 else (f_mul, 4 * i + 4)))
                        else:
                            pe.wait_ge(f_add, 16 * (m - 1) + 12 + 4 * s)
                        token_job(1, lambda kt: AH[:, 2 * (m % 2) + kt, :], lambda kt: AL[:, 2 * (m % 2) + kt, :], 4 * (s % 2))


INPUTS = ["x", "mem", "norm_mix", "w_in", "win_sink", "diff_lq1", "diff_lk1", "diff_lq2", "diff_lk2", "diff_subln",
          "rwkv_conv", "rwkv_w0", "rwkv_w_up", "rwkv_a0", "rwkv_a_up", "rwkv_g_up", "rwkv_k_k", "rwkv_k_a", "rwkv_r_k",
          "rwkv_ln_g", "rwkv_ln_b", "w_out", "norm_cross", "norm_mem", "x_wq", "x_wkv", "x_wo", "norm_ffn",
          "ffn_w_gu", "ffn_w_down", "norm_final"]


def shape_constants():
    import numpy as np

    row, colm = np.arange(P) % C, np.arange(C)
    j, t = row[:, None], colm[None, :]
    cn = np.zeros((P, C_LEN), np.float32)
    cn[:, C_ID:C_ID + P] = np.eye(P)
    cn[:, C_ONES:C_ONES + P] = np.kron(np.eye(2), np.ones((C, C)))
    cn[:, C_MASK[0]:C_MASK[0] + 128] = np.concatenate([t > j, t >= j], 1)
    cn[:, C_MASK[1]:C_MASK[1] + 128] = np.concatenate([t < j, t <= j], 1)
    for l, s in enumerate([1] + LEVELS):
        later = (t // s % 2 == 1) & (j // s == t // s - 1)
        earlier = (j // s % 2 == 1) & (t // s == j // s - 1)
        cn[:, C_LT[0] + 64 * l:C_LT[0] + 64 * l + 64] = later
        cn[:, C_LT[1] + 64 * l:C_LT[1] + 64 * l + 64] = earlier
    cn[:, C_I64:C_I64 + 64] = j == t
    p = np.arange(P)[:, None]
    dist = (-DIFF_SLOPES[0] * np.abs(np.arange(1920)[None, :] - 896 - p)).astype(np.float32)
    delta = np.abs(np.arange(384)[None, :] - P - p)
    win = np.concatenate([np.where(delta <= 128, -s * delta, -1e30) for s in WIN_SLOPES], 1).astype(np.float32)
    return {"consts": cn, "dist": dist, "win_bias": win}


def kernel(**inputs):
    import numpy as np
    import concourse.bacc as bacc
    from concourse.bass_utils import run_bass_kernel_spmd

    nc = bacc.Bacc("TRN2", target_bir_lowering=False, num_devices=1)
    arrays = {f"in_{k}": np.ascontiguousarray(inputs[k]) for k in INPUTS}
    arrays.update({f"in_{k}": v for k, v in shape_constants().items()})
    io = {k[3:]: nc.dram_tensor(k, v.shape, mybir.dt.from_np(v.dtype), kind="ExternalInput").ap() for k, v in arrays.items()}
    io["out"] = nc.dram_tensor("out_x", (1, T, D), F32, kind="ExternalOutput").ap()
    build(nc, io)
    r = run_bass_kernel_spmd(nc, [arrays], core_ids=[0])
    return r.results[0]["out_x"]
```

```python
import math
from contextlib import ExitStack

import concourse.bass as bass
from concourse import mybir

F32 = mybir.dt.float32
F32R = mybir.dt.float32r
ALU = mybir.AluOpType
ACT = mybir.ActivationFunctionType
AX_X = mybir.AxisListType.X

P = 128
D = 1024
T = 1024
NT = T // P
KD = D // P
MEM = 256
DFF = 2816
IN_W = 3072
PW = 256
PK = 2
NRAW = 3
NW = 6
RMS_EPS = 1e-6
GN_EPS = 64e-5
C = 64
NCH = T // C
LEVELS = [2, 4, 8, 16, 32]
E05 = math.exp(-0.5)
LAM_INIT = 0.8 - 0.6 * math.exp(-0.3 * 0)
FF_ITERS = DFF // PW

C_ID = 0
C_ONES = 128
C_LT = {0: 256, 1: 256 + 384}
C_I64 = 1024
C_LEN = 1088
MK_LEN = 3 * P
SLOPES = [2.0 ** -(k + 1) for k in range(8)]
WIN_SLOPES, DIFF_SLOPES = SLOPES[0::2], SLOPES[1::2]


def build(nc, io):
    out = io["out"]
    ctx = ExitStack()
    with ctx:
        base = 16512

        def at(name, kib, shape, dt=F32):
            return nc.alloc_sbuf_tensor_at(name, [P] + list(shape), dt, offset=base + int(kib * 1024))

        arena_end = 207.8
        ctx.enter_context(nc.sbuf_tensor("arena", [P, int(arena_end * 256)], F32))
        WH = at("WH", 0, [NW, PK, PW], F32R)
        WL = at("WL", 12, [NW, PK, PW], F32R)
        RAW = at("RAW", 24, [NRAW, PK, PW])
        CN = at("CN", 30, [C_LEN])
        WA = at("WA", 35.25, [2, 2, 256])
        GU = at("GU", 39.25, [256])
        BC = at("BC", 38.25, [1024])
        SM = at("SM", 42.25, [432])
        HH = at("HH", 44, [KD, T], F32R)
        HL = at("HL", 76, [KD, T], F32R)
        MIX = at("MIX", 108, [8, T])
        BQ = at("BQ", 140, [4, T])
        BK = at("BK", 156, [4, T])
        BV = at("BV", 172, [NT, 512])
        GB = at("GB", 124, [D])
        XT = at("XT", 172, [4, D])
        XN = at("XN", 188, [2, D])
        JX, JN = at("JX", 140, [D]), at("JN", 180, [D])
        VR = at("VR", 144, [P])
        E_ = at("E_", 124, [4, T])
        TAB = at("TAB", 188, [1920])
        AT_ = at("AT_", 195.5, [T])
        OB = at("OB", 199.5, [2, NT, 128])
        KST = at("KST", 0, [2, 2, T], F32R)
        QST = at("QST", 16, [2, 2, 2, 2 * P], F32R)
        CIN = at("CIN", 140, [8, T + 2])
        QW = at("QW", 173, [4, T], F32R)
        KW = at("KW", 189, [2, 2, T], F32R)
        AV = at("AV", 132, [NT, 128])
        WP_ = at("WP_", 44, [3, 2, 384])
        WT_ = at("WT_", 53, [2, 6, 128])
        WB_ = at("WB_", 84, [4, 384])
        CV = CIN[:, :, 2:T + 2]
        TMP = at("TMP", 136, [T])
        KK = at("KK", 76, [2, T])
        YY = at("YY", 196.25, [2, T])
        VT = at("VT", 92, [NT, 2 * P])
        KS = at("KS", 100, [2, T])
        KR = at("KR", 44, [2, 2, NCH, C])
        BKt = at("BKt", 60, [2, 2, NCH, C])
        S1_ = at("S1_", 0, [2, T])
        S2_ = at("S2_", 8, [2, T])
        S3_ = at("S3_", 16, [2, T])
        class Slot:
            def __init__(self, i):
                b, n = 172.25 * i, f"s{i}_"
                self.bank = 4 * i
                self.G = at(n + "G", b, [2, 4, 2, P])
                self.PAD = at(n + "PAD", b + 8, [2, 2, 2, P])
                self.QQ = at(n + "QQ", b + 12, [2, 4, P])
                self.RH = at(n + "RH", b + 16, [4, 2, C])
                self.LT = at(n + "LT", b + 18, [4, P])
                self.XX = at(n + "XX", b + 20, [4, P])
                self.WU = at(n + "WU", b + 22, [4, 2, C])
                self.BT = at(n + "BT", 132 + 2 * i, [4, C])
                self.KT = at(n + "KT", 133 + 2 * i, [4, C])

        slots = [Slot(0), Slot(1)]
        MK = at("MK", 204.5, [2, MK_LEN])
        KDN = at("KDN", 172.25, [2, T])
        SQY, RSY, VB = (at(n, b, [2, T]) for n, b in (("SQY", 172.25), ("RSY", 180.25), ("VB", 188.25)))
        SCM = at("SCM", 136, [T])
        FO = at("FO", 180, [2, D])
        X = at("X", 140, [NT, D])
        AH = at("AH", 108, [4, T], F32R)
        AL = at("AL", 124, [4, T], F32R)
        XN2 = at("XN2", 172, [2, D])
        QC = at("QC", 180, [4, T])
        KM = at("KM", 196, [4, MEM])
        VM = at("VM", 200, [2, 512])
        GBM = at("GBM", 116, [D])
        GBC = at("GBC", 120, [D])
        GBF = at("GBF", 196, [D])
        GBL = at("GBL", 200, [D])
        MX = at("MX", 180, [2, D])
        JM = at("JM", 188, [D])
        CP = at("CP", 44, [2, 1024])
        CPT = at("CPT", 52, [2, 1024])
        ACTB = at("ACTB", 172, [2, T])
        FU = at("FU", 180, [2, T])

        PS = ctx.enter_context(nc.psum_tensor("PS", [P, 8, 512], F32))

        def sem(name):
            return ctx.enter_context(nc.semaphore(name))

        ID = CN[:, C_ID:C_ID + 128]
        ONES = CN[:, C_ONES:C_ONES + 128]
        I64 = CN[:, C_I64:C_I64 + 64]
        SUB, SINK = BC[:, 512:640], BC[:, 640:644]
        LQ = [BC[:, 648 + 64 * i:712 + 64 * i] for i in range(4)]
        SS, RS = SM[:, 0:8], SM[:, 8:16]
        EH, DD, HT = (SM[:, c:c + 32] for c in (112, 144, 176))
        NSINK = SM[:, 240:244]
        NR = SM[:, 208:240]
        OKA = SM[:, 76:78]
        LAM = SM[:, 16:20]
        MM, NM, LL = SM[:, 20:24], SM[:, 24:28], SM[:, 28:32]
        PT = SM[:, 32:74]
        CO = SM[:, 80:96]
        HS, HR = SM[:, 96:104], SM[:, 104:112]
        WM, WSUM, WSNK, WR = (SM[:, c:c + 6] for c in (332, 338, 344, 350))
        CM, CL, CR = (SM[:, c:c + 8] for c in (356, 364, 372))
        MS, MR = SM[:, 268:270], SM[:, 270:272]
        FS, FR = SM[:, 272:280], SM[:, 280:288]
        AS, AR = SM[:, 288:296], SM[:, 296:304]
        BS, BR = SM[:, 304:312], SM[:, 312:320]
        NMD, MD, LD = SM[:, 320:324], SM[:, 324:328], SM[:, 328:332]
        VROWS = VR[0:42, :]
        PTC_CONV, PTC_W0, PTC_A0, PTC_KK, PTC_KA, PTC_RK, PTC_LNG, PTC_LNB = 0, 24, 28, 32, 34, 36, 38, 40

        def col(i):
            return PT[:, i:i + 1]

        raw_full = [sem(f"raw_full{i}") for i in range(NRAW)]
        w_hi, w_lo, w_used = sem("w_hi"), sem("w_lo"), sem("w_used")
        consts_in, vecs_in, tab_in = sem("consts_in"), sem("vecs_in"), sem("tab_in")
        vec_t, vec_c = sem("vec_t"), sem("vec_c")
        dve_chain, act_chain, pool_chain = sem("dve_chain"), sem("act_chain"), sem("pool_chain")

        w_in, w_out_, wq, wkv, wo = io["w_in"][0], io["w_out"][0], io["x_wq"][0], io["x_wkv"][0], io["x_wo"][0]
        w_gu, w_dn = io["ffn_w_gu"][0], io["ffn_w_down"][0]
        BQ0, BK0, BV0, CI0, AQ0, AK0 = 512, 1024, 1536, 2048, 0, 256

        def slab(w, c0, rows=D):
            return [(w, r, c0) for r in range(0, rows, PK * P)]

        proj_cols = [BQ0, BQ0 + PW, BK0, BK0 + PW, BV0, BV0 + PW, CI0, CI0 + PW, CI0 + 2 * PW, CI0 + 3 * PW, AQ0, AK0]
        pieces = []
        for c0 in proj_cols:
            pieces += slab(w_in, c0)
        for c0 in range(0, D, PW):
            pieces += slab(w_out_, c0)
        for c0 in range(0, 1024, PW):
            pieces += slab(wkv, c0)
        for c0 in range(0, 512, PW):
            pieces += slab(wq, c0)
        for c0 in range(0, D, PW):
            pieces += slab(wo, c0, 512)
        N_LIN = len(pieces)
        for i in range(FF_ITERS + 1):
            if i < FF_ITERS:
                pieces += slab(w_gu, i * PW) + slab(w_gu, DFF + i * PW)
            if i >= 1:
                pieces += [(w_dn, (i - 1) * PW, c0) for c0 in range(0, D, PW)]

        class Norm:
            def __init__(self, name, n, nbuf=2):
                self.n = n
                self.full = [sem(f"{name}_full{i}") for i in range(nbuf)]
                self.std, self.xn, self.tr, self.hi, self.lo = (sem(f"{name}_{k}") for k in ("std", "xn", "tr", "hi", "lo"))

        n1, nm, n2, n3 = Norm("n1", NT, 4), Norm("nm", 2), Norm("n2", NT), Norm("n3", NT)
        gain_in = {k: sem(f"gain_{k}") for k in ("mix", "mem", "cross", "ffn", "final")}

        job_evac = sem("job_evac")
        NJ = len(proj_cols)
        jobs2 = ([("wout", i) for i in range(4)] + [("wkv", i) for i in range(4)] + [("wq", i) for i in range(2)]
                 + [("wo", i) for i in range(4)])
        job2_act, job2_dve = sem("job2_act"), sem("job2_dve")
        end2, e = [], 4 * NJ
        for kind, _ in jobs2:
            e += 2 if kind == "wo" else 4
            end2.append(e)

        def ff0(i):
            return N_LIN + 12 * i - (4 if i else 0)

        evac_of, n_act, n_dve = [], 0, 0
        for kind, _ in jobs2:
            if kind in ("wkv", "wq"):
                n_act += 1
                evac_of.append((job2_act, n_act))
            else:
                n_dve += 1
                evac_of.append((job2_dve, n_dve))

        qk_done, s_read, nm_done, exp_done = sem("qk_done"), sem("s_read"), sem("nm_done"), sem("exp_done")
        comb_done, tr_done, at_evac, pv_done, o_evac = (sem(k) for k in ("comb_done", "tr_done", "at_evac", "pv_done", "o_evac"))
        sq_done, hs_done, hstd, hn_done, ht_done, hm_evac = (sem(k) for k in ("sq_done", "hs_done", "hstd", "hn_done", "ht_done", "hm_evac"))
        lam_s, lam_e = sem("lam_s"), sem("lam_e")
        co_done = sem("co_done")
        k_staged, q_staged, k_first, k_second = sem("k_staged"), sem("q_staged"), sem("k_first"), sem("k_second")

        w_r = sem("w_r")
        wb_in, qw_lo, w_qk, w_nm, w_exp, w_p, w_tr, w_pt, w_pv, w_mix = (
            sem(k) for k in ("wb_in", "qw_lo", "w_qk", "w_nm", "w_exp", "w_p", "w_tr", "w_pt", "w_pv", "w_mix"))
        NWU = 2 * NT

        def window(u):
            qb, kv = u // 2, u % 2
            first, last = max(0, qb - 1), min(NT - 1, qb + 1)
            return qb, kv, first, last - first + 1


        r_kd, r_ks, r_kd_used = sem("r_kd"), sem("r_ks"), sem("r_kd_used")
        r_spread, r_back, p_spread, p_back, p_nrm = (sem(k) for k in ("r_spread", "r_back", "p_spread", "p_back", "p_nrm"))
        pads, r_conv, r_vt, r_vte, r_sq, r_kn, r_std, r_act, r_kk = (
            sem(k) for k in ("pads", "r_conv", "r_vt", "r_vte", "r_sq", "r_kn", "r_std", "r_act", "r_kk"))
        r_z, r_sig, r_c, r_exp, r_pre, r_scm = (sem(k) for k in ("r_z", "r_sig", "r_c", "r_exp", "r_pre", "r_scm"))
        g_pe, g_act, g_dve, g_pool = ([sem(f"{k}{i}") for i in range(2)] for k in ("g_pe", "g_act", "g_dve", "g_pool"))
        pad_zero, masks_in = sem("pad_zero"), sem("masks_in")
        pad_done = [sem("pad_done0"), sem("pad_done1")]
        c_mm, c_z, y_mm, y_add = sem("c_mm"), sem("c_z"), sem("y_mm"), sem("y_add")
        p_rk, p_mm, p_cen, p_sq, p_std, p_bon, p_y = (sem(k) for k in ("p_rk", "p_mm", "p_cen", "p_sq", "p_std", "p_bon", "p_y"))
        x_added = sem("x_added")
        mix_hi, mix_lo_dve, mix_lo_pool, x_in = sem("mix_hi"), sem("mix_lo_dve"), sem("mix_lo_pool"), sem("x_in")
        c_qk, c_max, c_exp, c_p, c_tr, c_pt, c_pv, c_hi, c_lo = (
            sem(k) for k in ("c_qk", "c_max", "c_exp", "c_p", "c_tr", "c_pt", "c_pv", "c_hi", "c_lo"))
        f_silu, f_mul, f_hi, f_lo, f_add = (sem(k) for k in ("f_silu", "f_mul", "f_hi", "f_lo", "f_add"))
        f_mm = sem("f_mm")
        l_std, l_o, out_done = sem("l_std"), sem("l_o"), [sem("out_done0"), sem("out_done1")]

        NPR = NT // 2
        LV = len(LEVELS)
        G_PE, G_ACT, G_DVE, G_POOL = 8 + 2 * LV + 2, 3 + LV + 1, 5 + LV + 1, 1 + LV

        MIX_SRC = (4, 5, 0, 1, 2, 3, 6, 7)

        X_TILES = (1, 3, 5, 7, 9, 10, 12, 13)

        def tile_of(d, m, i):
            return 2 * m + i if d == 0 else NT - 1 - 2 * m - i

        def first_chunk(d, m):
            return 4 * m if d == 0 else 4 * (NPR - 1 - m)

        block = ctx.enter_context(nc.Block())

        @block.sync
        def _(sp):
            def load(p):
                w, r0, c0 = pieces[p]
                if p >= NRAW:
                    sp.wait_ge(w_hi, p - NRAW + 1)
                    sp.wait_ge(w_lo, p - NRAW + 1)
                sp.dma_start(RAW[:, p % NRAW], w[r0:r0 + PK * P, c0:c0 + PW].rearrange("(k p) c -> p k c", p=P)
                             ).then_inc(raw_full[p % NRAW], 16)

            sp.dma_start(XT[:, 0], io["x"][0, 0:P, :]).then_inc(n1.full[0], 16)
            sp.dma_start(GB[:, :], io["norm_mix"][0:1, :].broadcast_to([P, D])).then_inc(gain_in["mix"], 16)
            sp.dma_start(CN[:, :], io["consts"]).then_inc(consts_in, 16)
            for tt in range(1, 4):
                sp.dma_start(XT[:, tt], io["x"][0, tt * P:(tt + 1) * P, :]).then_inc(n1.full[tt], 16)
            for p in range(NRAW):
                load(p)
            for tt in range(4, NT):
                sp.wait_ge(n1.xn, tt - 3)
                sp.dma_start(XT[:, tt % 4], io["x"][0, tt * P:(tt + 1) * P, :]).then_inc(n1.full[tt % 4], 16)
            for p in range(NRAW, 4 * NJ):
                load(p)
            for p in range(4 * NJ, 4 * NJ + NRAW):
                load(p)
            p = 4 * NJ + NRAW
            for _ in range(3):
                load(p)
                p += 1
            sp.wait_ge(p_y, 1)
            for tt in range(NT):
                sp.dma_start(X[:, tt], io["x"][0, tt * P:(tt + 1) * P, :]).then_inc(x_in, 16)
                if tt % 2:
                    load(p)
                    p += 1
            for tt in range(2):
                sp.dma_start(MX[:, tt], io["mem"][0, tt * P:(tt + 1) * P, :]).then_inc(nm.full[tt], 16)
            sp.wait_ge(mix_lo_dve, 2)
            sp.wait_ge(mix_lo_pool, 6)
            sp.wait_ge(mix_hi, 8)
            sp.dma_start(GBM[:, :], io["norm_mem"].rearrange("(a d) -> a d", a=1).broadcast_to([P, D])).then_inc(gain_in["mem"], 16)
            sp.dma_start(GBC[:, :], io["norm_cross"][0:1, :].broadcast_to([P, D])).then_inc(gain_in["cross"], 16)
            for p in range(p, N_LIN + NRAW):
                load(p)
            sp.wait_ge(c_lo, NT)
            sp.dma_start(GBF[:, :], io["norm_ffn"][0:1, :].broadcast_to([P, D])).then_inc(gain_in["ffn"], 16)
            sp.dma_start(GBL[:, :], io["norm_final"].rearrange("(a d) -> a d", a=1).broadcast_to([P, D])).then_inc(gain_in["final"], 16)
            for p in range(N_LIN + NRAW, len(pieces)):
                load(p)
            for tt in range(NT):
                sp.wait_ge(l_o, tt + 1)
                sp.dma_start(out[0, tt * P:(tt + 1) * P, :], FO[:, tt % 2]).then_inc(out_done[tt % 2], 16)
            for s in out_done:
                sp.wait_ge(s, 8 * NT)

        @block.gpsimd
        def _(pool):
            chain = [0]

            def link(ins):
                chain[0] += 1
                ins.then_inc(pool_chain, 1)
                pool.wait_ge(pool_chain, chain[0])

            pool.dma_start(VROWS[0:24, :], io["rwkv_conv"][0].rearrange("j (c p) -> (j c) p", p=P)).then_inc(vecs_in, 16)
            pool.dma_start(VROWS[24:28, :], io["rwkv_w0"][0].rearrange("d (c p) -> (d c) p", p=P)).then_inc(vecs_in, 16)
            pool.dma_start(VROWS[28:32, :], io["rwkv_a0"][0].rearrange("d (c p) -> (d c) p", p=P)).then_inc(vecs_in, 16)
            pool.dma_start(VROWS[32:34, :], io["rwkv_k_k"].rearrange("l (c p) -> (l c) p", p=P)).then_inc(vecs_in, 16)
            pool.dma_start(VROWS[34:36, :], io["rwkv_k_a"].rearrange("l (c p) -> (l c) p", p=P)).then_inc(vecs_in, 16)
            pool.dma_start(VROWS[36:38, :], io["rwkv_r_k"][0].rearrange("(c h) p -> c (h p)", h=2)).then_inc(vecs_in, 16)
            pool.dma_start(VROWS[38:40, :], io["rwkv_ln_g"].rearrange("l (c p) -> (l c) p", p=P)).then_inc(vecs_in, 16)
            pool.dma_start(VROWS[40:42, :], io["rwkv_ln_b"].rearrange("l (c p) -> (l c) p", p=P)).then_inc(vecs_in, 16)
            link(pool.memset(WA[:, :, :, :], 0.0))
            pool.dma_start(WA[0:64, :, 0], io["rwkv_w_up"][0].rearrange("d l c -> l d c")).then_inc(vecs_in, 16)
            pool.dma_start(WA[64:128, :, 1], io["rwkv_a_up"][0].rearrange("d l c -> l d c")).then_inc(vecs_in, 16)
            pool.dma_start(GU[:, :], io["rwkv_g_up"][0]).then_inc(vecs_in, 16)
            pool.dma_start(SUB, io["diff_subln"].broadcast_to([P, 128])).then_inc(vecs_in, 16)
            pool.dma_start(SINK, io["win_sink"].broadcast_to([P, 4])).then_inc(vecs_in, 16)
            for i, k in enumerate(("diff_lq1", "diff_lk1", "diff_lq2", "diff_lk2")):
                pool.dma_start(LQ[i], io[k].broadcast_to([P, 64])).then_inc(vecs_in, 16)

            def lo(p):
                pool.wait_ge(w_hi, p + 1)
                pool.tensor_tensor(WL[:, p % NW], RAW[:, p % NRAW], WH[:, p % NW].bitcast(F32), ALU.subtract).then_inc(w_lo, 1)

            for p in range(24):
                lo(p)
            pool.dma_start(TAB[:, :], io["dist"]).then_inc(tab_in, 16)
            pool.wait_ge(w_used, 24)
            pool.wait_ge(w_lo, 24)
            pool.wait_ge(job_evac, 24)

            def stage(dst_hi, dst_lo, src):
                link(pool.tensor_copy(dst_hi, src))
                return pool.tensor_tensor(dst_lo, src, dst_hi.bitcast(F32), ALU.subtract)

            def stage_keys(h):
                for i, c in enumerate((1, 0)):
                    same, other = slice(64 * c, 64 * c + 64), slice(64 - 64 * c, 128 - 64 * c)
                    pool.wait_ge(k_first, 2 * h + i + 1)
                    ins = pool.tensor_tensor(KST[other, h % 2, c, :], BK[same, h, :], KST[same, h % 2, c, :].bitcast(F32), ALU.subtract)
                ins.then_inc(k_staged, 1)

            for h in range(4):
                for g in range(0 if h else 1, 4):
                    n = 4 * h + g
                    if n >= 2:
                        pool.wait_ge(qk_done, 4 * (n - 1))
                    for c in (1, 0):
                        same, other = slice(64 * c, 64 * c + 64), slice(64 - 64 * c, 128 - 64 * c)
                        src = BQ[same, h, 2 * P * g:2 * P * (g + 1)]
                        link(stage(QST[same, n % 2, 0, c, :], QST[same, n % 2, 1, c, :], src))
                        for part in range(2):
                            ins = pool.tensor_copy(QST[other, n % 2, part, c, :], QST[same, n % 2, part, c, :].bitcast(F32))
                    ins.then_inc(q_staged, 1)
                    if g == 3 and h < 3:
                        stage_keys(h + 1)
            for p in range(24, 28):
                lo(p)
            pool.wait_ge(hm_evac, 8)
            pool.memset(CIN[:, :, 0:1], 0.0)
            pool.memset(CIN[:, :, T + 1:T + 2], 0.0).then_inc(pads, 1)
            for p in range(28, 4 * NJ):
                lo(p)
            pool.wait_ge(w_used, 4 * NJ)
            pool.dma_start(WB_[:, :, :], io["win_bias"].rearrange("p (h k) -> p h k", h=4)).then_inc(wb_in, 16)
            pool.wait_ge(r_conv, 8)
            link(pool.memset(SCM[:, :], 1.0))
            pool.memset(SCM[:, 0:T:C], 0.0).then_inc(r_scm, 1)
            def kd_steps(d):
                if d:
                    pool.wait_ge(g_pe[1], G_PE * NPR)
                kd = KDN if d else KS
                for ct in range(2):
                    pool.wait_ge(r_sig, 4 * d + 3 + ct)
                    link(pool.tensor_scalar(kd[:, ct, :], S3_[:, ct, :], col(PTC_KA + ct), OKA[:, ct:ct + 1], ALU.mult, ALU.add))
                    link(pool.tensor_tensor(kd[:, ct, :], kd[:, ct, :], CV[:, 2 + ct, :], ALU.mult))
                    yield
                    pool.wait_ge(r_kk, ct + 1)
                    pool.tensor_tensor(S3_[:, ct, :], S3_[:, ct, :], KK[:, ct, :], ALU.mult).then_inc(r_kd, 1)
                    yield

            kd0 = kd_steps(0)
            for u in range(NWU):
                nk, c = window(u)[3], slice(2 * (u % 3), 2 * (u % 3) + 2)
                pool.wait_ge(w_r, u + 1)
                pr = WP_[:, u % 3, :, 0:nk * P]
                pool.tensor_tensor(pr, pr, WR[:, c].unsqueeze(2).broadcast_to([P, 2, nk * P]), ALU.mult).then_inc(w_p, 1)
                if u >= 6 and u % 2 == 0:
                    next(kd0, None)

            for d in range(2):
                if d:
                    for step in kd_steps(1):
                        pass
                if d == 0:
                    pool.wait_ge(w_mix, NWU)
                    pool.dma_start(MK[:, :, :], io["masks"].rearrange("p (d k) -> p d k", d=2)).then_inc(masks_in, 16)
                pool.memset(slots[1].PAD[:, :, :, :, :], 0.0)
                pool.wait_ge(r_exp, 7 * (d + 1))
                pool.memset(slots[0].PAD[:, :, :, :, :], 0.0).then_inc(pad_zero, 1)
                if d:
                    pool.tensor_tensor(KS[:, :, :], KS[:, :, :], KDN[:, :, :], ALU.add).then_inc(r_ks, 1)
                lvl = C_LT[d]
                for m in range(NPR):
                    n = NPR * d + m
                    for i, sl in enumerate(slots):
                        pool.wait_ge(g_pe[i], G_PE * n)
                        pool.wait_ge(g_dve[i], G_DVE * n + 2)
                        qt = sl.QQ[:, 1]
                        link(pool.tensor_tensor(qt.rearrange("p u (c k) -> p u c k", c=2), sl.G[:, 0, :, 0, :].rearrange("p u (c k) -> p u c k", c=2),
                                                CN[:, lvl:lvl + 64].unsqueeze(1).unsqueeze(1).broadcast_to([P, 4, 2, C]), ALU.mult))
                        pool.tensor_tensor(qt, qt, ID.unsqueeze(1).broadcast_to([P, 4, P]), ALU.subtract).then_inc(g_pool[i], 1)
                        pool.tensor_tensor(sl.LT[:, :, :].rearrange("p u (c k) -> p u c k", c=2), sl.G[:, 0, :, 0, :].rearrange("p u (c k) -> p u c k", c=2),
                                           CN[:, lvl + 64:lvl + 128].unsqueeze(1).unsqueeze(1).broadcast_to([P, 4, 2, C]), ALU.mult).then_inc(g_pool[i], 1)
                    for l in range(1, LV):
                        for i, sl in enumerate(slots):
                            pool.wait_ge(g_pe[i], G_PE * n + 9 + 2 * (l - 1))
                            m0 = lvl + 64 * (l + 1)
                            pool.tensor_tensor(sl.LT[:, :, :].rearrange("p u (c k) -> p u c k", c=2), sl.G[:, 0, :, 0, :].rearrange("p u (c k) -> p u c k", c=2),
                                               CN[:, m0:m0 + 64].unsqueeze(1).unsqueeze(1).broadcast_to([P, 4, 2, C]), ALU.mult).then_inc(g_pool[i], 1)
            def mix_second(k):
                pool.wait_ge(mix_hi, k + 1)
                pool.tensor_tensor(HL[:, k, :], MIX[:, MIX_SRC[k], :], HH[:, k, :].bitcast(F32), ALU.subtract).then_inc(mix_lo_pool, 1)

            pool.wait_ge(y_add, 2 * NPR)
            for k in range(6):
                if k % 2 == 0:
                    lo(4 * NJ + k // 2)
                mix_second(k)
            for p in range(4 * NJ + NRAW, len(pieces)):
                lo(p)

        @block.scalar
        def _(act):
            chain = [0]
            done_hi = [0]

            def link(ins):
                chain[0] += 1
                ins.then_inc(act_chain, 1)
                act.wait_ge(act_chain, chain[0])

            def hi(upto):
                while done_hi[0] < min(upto, len(pieces)):
                    p = done_hi[0]
                    act.wait_ge(raw_full[p % NRAW], 16 * (p // NRAW + 1))
                    if p >= NW:
                        act.wait_ge(w_used, p - NW + 1)
                        act.wait_ge(w_lo, p - NW + 1)
                    act.activation(WH[:, p % NW], RAW[:, p % NRAW], ACT.Copy).then_inc(w_hi, 1)
                    done_hi[0] += 1

            def stat(nn, tt, src, junk, S, wait_src):
                wait_src(tt)
                link(act.activation(junk, src(tt), ACT.Square, accum_out=S[:, tt:tt + 1]))
                act.activation(S[:, tt:tt + 1], S[:, tt:tt + 1], ACT.Sqrt, bias=RMS_EPS, scale=1.0 / D).then_inc(nn.std, 1)

            def norm_hi(nn, tt, hdst, bank=lambda tt: 2 * (tt % 4)):
                for b in range(2):
                    act.wait_ge(nn.tr, 2 * tt + b + 1)
                    act.activation(hdst(tt, b), PS[:, bank(tt) + b, :].rearrange("p (k t) -> p k t", k=4), ACT.Copy).then_inc(nn.hi, 1)

            def norm(nn, src, junk, S, hdst, wait_src):
                for tt in range(2):
                    stat(nn, tt, src, junk, S, wait_src)
                for tt in range(nn.n):
                    if tt + 2 < nn.n:
                        stat(nn, tt + 2, src, junk, S, wait_src)
                    norm_hi(nn, tt, hdst)

            norm(n1, lambda tt: XT[:, tt % 4], JX[:, :], SS, lambda tt, b: HH[:, 4 * b:4 * b + 4, tt * P:(tt + 1) * P],
                 lambda tt: act.wait_ge(n1.full[tt % 4], 16 * (tt // 4 + 1)))

            def evac_proj(j):
                c0 = proj_cols[j]
                act.wait_ge(w_used, 4 * (j + 1))
                bank = [PS[:, 4 * (j % 2) + i, :] for i in range(4)]
                for i in range(4):
                    ct, half = i // 2, i % 2
                    t0 = half * 512
                    if BQ0 <= c0 < BK0:
                        k = (c0 - BQ0) // P + ct
                        act.activation(BQ[:, k, t0:t0 + 512], bank[i], ACT.Copy, scale=0.125).then_inc(job_evac, 1)
                    elif BK0 <= c0 < BV0:
                        k = (c0 - BK0) // P + ct
                        act.activation(BK[:, k, t0:t0 + 512], bank[i], ACT.Copy).then_inc(job_evac, 1)
                    elif BV0 <= c0 < CI0:
                        act.activation(BV[:, 2 * i:2 * i + 2, c0 - BV0:c0 - BV0 + PW], bank[i].rearrange("p (t c) -> p t c", t=2),
                                       ACT.Copy).then_inc(job_evac, 1)
                    elif c0 >= CI0:
                        k = (c0 - CI0) // P + ct
                        act.activation(CIN[:, k, 1 + t0:1 + t0 + 512], bank[i], ACT.Copy).then_inc(job_evac, 1)
                    elif c0 == AQ0:
                        for hp in range(2):
                            rows = slice(64 * hp, 64 * hp + 64)
                            a = act.activation(QW[rows, 2 * ct + hp, t0:t0 + 512], bank[i][rows], ACT.Copy, scale=0.125)
                        a.then_inc(job_evac, 1)
                    elif i < 2:
                        t0 = i * 512
                        for kv in range(2):
                            for hp in range(2):
                                a = act.activation(KW[64 * hp:64 * hp + 64, kv, 0, t0:t0 + 512], bank[i][64 * kv:64 * kv + 64], ACT.Copy)
                        a.then_inc(job_evac, 1)
                    else:
                        act.activation(AV[:, 4 * (i - 2):4 * (i - 2) + 4, :], bank[i].rearrange("p (t c) -> p t c", t=4),
                                       ACT.Copy).then_inc(job_evac, 1)

            for j in range(6):
                hi(min(4 * j + 10, 24))
                evac_proj(j)

            def k_first_parts(h):
                if h >= 2:
                    act.wait_ge(qk_done, 16 * (h - 1))
                for c in (1, 0):
                    rows = slice(64 * c, 64 * c + 64)
                    act.activation(KST[rows, h % 2, c, :], BK[rows, h, :], ACT.Copy).then_inc(k_first, 1)

            act.wait_ge(w_lo, 24)
            k_first_parts(0)
            act.wait_ge(lam_s, 1)
            act.activation(LAM[:, 0:2], LAM[:, 0:2], ACT.Exp).then_inc(lam_e, 1)

            def d_exp(u):
                for i, c in enumerate((1, 0)):
                    n = 2 * u + c
                    act.wait_ge(nm_done, 2 * u + i + 1)
                    e = E_[:, n % 4, :]
                    if u >= 2:
                        act.wait_ge(comb_done, u - 1)
                    act.activation(e, e, ACT.Exp, bias=NMD[:, n % 4:n % 4 + 1], accum_out=LD[:, n % 4:n % 4 + 1]).then_inc(exp_done, 1)

            def d_square(h):
                act.wait_ge(o_evac, 8 * h + 8)
                sq = BQ[:, h, :].rearrange("p (t c) -> p t c", t=NT)
                act.activation(sq, OB[:, h % 2], ACT.Square).then_inc(sq_done, 1)

            def d_std(h):
                act.wait_ge(hs_done, h + 1)
                act.activation(HS, HS, ACT.Sqrt, bias=RMS_EPS, scale=1.0 / 128).then_inc(hstd, 1)

            def d_evac(h, halves):
                for b in halves:
                    act.wait_ge(ht_done, 2 * h + b + 1)
                    act.activation(MIX[:, h, b * 512:b * 512 + 512], PS[:, 7, :], ACT.Copy).then_inc(hm_evac, 1)

            d_exp(0)
            d_exp(1)
            for u in range(32):
                h, qb = u // 8, u % 8
                for b in range(2):
                    act.wait_ge(tr_done, 2 * u + b + 1)
                    if u and b == 0:
                        act.wait_ge(pv_done, u)
                    act.activation(AT_[:, b * 512:b * 512 + 512], PS[:, 4 + b, :], ACT.Copy).then_inc(at_evac, 1)
                if u + 2 < 32:
                    d_exp(u + 2)
                act.wait_ge(pv_done, u + 1)
                if h >= 2 and qb == 0:
                    act.wait_ge(hn_done, h - 1)
                act.activation(OB[:, h % 2, qb, :], PS[:, 6, 0:128], ACT.Copy, scale=CO[:, 4 * (u % 2):4 * (u % 2) + 1]).then_inc(o_evac, 1)
                if qb == 1 and h < 3:
                    k_first_parts(h + 1)
                if h and qb == 0:
                    d_square(h - 1)
                if h and qb == 2:
                    d_std(h - 1)
                if h and qb in (4, 5):
                    d_evac(h - 1, (qb - 4,))
            d_square(3)
            d_std(3)

            act.wait_ge(qk_done, 64)
            hi(24 + NW)
            d_evac(3, (0, 1))
            for j in range(6, NJ):
                hi(min(4 * j + 10, 4 * NJ))
                evac_proj(j)
                if j == NJ - 2:
                    act.wait_ge(r_conv, 7)
                    act.activation(CV[0:64, 6, :], CV[0:64, 6, :], ACT.Tanh).then_inc(r_act, 1)
                    act.wait_ge(r_conv, 8)
                    act.activation(CV[:, 7, :], CV[:, 7, :], ACT.Sigmoid).then_inc(r_act, 1)

            def r_sigmoids(d):
                for kind, dst, vec in ((0, S1_, PTC_W0), (1, S3_, PTC_A0)):
                    for ct in range(2):
                        act.wait_ge(r_z, 4 * d + 2 * kind + ct + 1)
                        act.activation(dst[:, ct, :].rearrange("p (b c) -> p b c", c=512), PS[:, 3 * ct:3 * ct + 2, :], ACT.Sigmoid,
                                       bias=col(vec + 2 * d + ct)).then_inc(r_sig, 1)

            act.wait_ge(r_sq, 1)
            act.activation(S2_[:, :, :], KK[:, :, :], ACT.Square).then_inc(r_act, 1)
            r_sigmoids(0)
            act.wait_ge(r_kn, 1)
            act.activation(NR, PS[:, 5, 0:32], ACT.Sqrt).then_inc(r_std, 1)
            for b in range(4):
                act.wait_ge(r_vt, b + 1)
                act.activation(VT[:, 2 * b:2 * b + 2, :], PS[:, b, :].rearrange("p (t c) -> p t c", t=2), ACT.Copy).then_inc(r_vte, 1)

            def w_exps(u):
                _, _, _, nk = window(u)
                act.wait_ge(w_nm, u + 1)
                for g in range(2):
                    c = 2 * (u % 3) + g
                    act.activation(WP_[:, u % 3, g, 0:nk * P], WP_[:, u % 3, g, 0:nk * P], ACT.Exp, bias=WM[:, c:c + 1], accum_out=WSUM[:, c:c + 1])
                for g in range(2):
                    c, h = 2 * (u % 3) + g, 2 * window(u)[1] + g
                    a = act.activation(WSNK[:, c:c + 1], SINK[:, h:h + 1], ACT.Exp, bias=WM[:, c:c + 1])
                a.then_inc(w_exp, 1)

            def w_out_evac(u):
                qb, kv, _, _ = window(u)
                act.wait_ge(w_pv, u + 1)
                act.activation(MIX[:, 4 + kv, qb * P:(qb + 1) * P], PS[:, 6 + u % 2, 0:P], ACT.Copy).then_inc(w_mix, 1)

            def r_exp_b(d, ct):
                act.wait_ge(r_c, 2 * d + ct + 1)
                t, sg = ((S2_, 1.0), (S1_, -1.0))[d]
                act.activation(BKt[:, 0, ct], t[:, ct, :].rearrange("p (c k) -> p c k", k=C), ACT.Exp, scale=-sg).then_inc(r_exp, 1)

            def r_exp_k(d, ct):
                (t1, s1), (tx, sx) = ((S2_, 1.0), (S1_, 1.0)) if d == 0 else ((S1_, -1.0), (S2_, -1.0))
                act.activation(KR[:, 1, ct], t1[:, ct, :].rearrange("p (c k) -> p c k", k=C), ACT.Exp, scale=s1).then_inc(r_exp, 1)
                act.activation(KR[:, 0, ct], tx[:, ct, :].rearrange("p (c k) -> p c k", k=C), ACT.Exp, scale=sx).then_inc(r_exp, 1)

            w_exps(0)
            w_exps(1)
            for u in range(NWU):
                if u in (NWU - 5, NWU - 4):
                    r_exp_b(0, u - (NWU - 5))
                _, _, _, nk = window(u)
                if u + 2 < NWU:
                    w_exps(u + 2)
                act.wait_ge(w_tr, u + 1)
                if u >= 2:
                    act.wait_ge(w_pv, u - 1)
                a = act.activation(WT_[:, u % 2, 0:4, :], PS[:, 4, :].rearrange("p (k q) -> p k q", k=4), ACT.Copy)
                if nk == 3:
                    a = act.activation(WT_[:, u % 2, 4:6, :], PS[:, 5, 0:256].rearrange("p (k q) -> p k q", k=2), ACT.Copy)
                a.then_inc(w_pt, 1)
                if u:
                    w_out_evac(u - 1)
            w_out_evac(NWU - 1)

            for d in range(2):
                if d:
                    for i in range(2):
                        act.wait_ge(g_pe[i], G_PE * NPR)
                        act.wait_ge(g_dve[i], G_DVE * NPR)
                    r_sigmoids(1)
                    act.wait_ge(y_add, NPR)
                if d == 0:
                    for ct in range(2):
                        r_exp_k(0, ct)
                else:
                    for ct in range(2):
                        r_exp_b(1, ct)
                        r_exp_k(1, ct)
                act.activation(EH, HT, ACT.Exp).then_inc(r_exp, 1)

                def pad(i, m):
                    sl, t = slots[i], tile_of(d, m, i)
                    for hp in range(2):
                        rows = slice(64 * hp, 64 * hp + 64)
                        for kr in range(2):
                            a = act.activation(sl.PAD[rows, :, hp, kr, :].rearrange("p a (c k) -> p a c k", c=2), KR[rows, kr, :, 2 * t:2 * t + 2, :], ACT.Copy)
                    a.then_inc(pad_done[i], 1)

                act.wait_ge(r_pre, d + 1)
                act.wait_ge(pad_zero, d + 1)
                for i in range(2):
                    pad(i, 0)
                for m in range(NPR):
                    n = NPR * d + m
                    pe0 = G_PE * n
                    for i, sl in enumerate(slots):
                        act.wait_ge(g_pe[i], pe0 + 1)
                        act.activation(sl.RH[:, :, 0, :], PS[:, sl.bank + 3, 0:256].rearrange("p (u k) -> p u k", k=C), ACT.Copy)
                        act.activation(sl.BT[:, :, :], PS[:, sl.bank + 3, 256:512].rearrange("p (u k) -> p u k", k=C), ACT.Copy).then_inc(g_act[i], 1)
                    for i, sl in enumerate(slots):
                        act.wait_ge(g_pe[i], pe0 + 7)
                        act.activation(sl.KT[:, :, :], PS[:, sl.bank + 1, 0:256].rearrange("p (u k) -> p u k", k=C), ACT.Copy).then_inc(g_act[i], 1)
                        act.wait_ge(g_pe[i], pe0 + 8)
                        act.activation(sl.RH[:, :, 1, :], PS[:, sl.bank + 2, 0:256].rearrange("p (u k) -> p u k", k=C), ACT.Copy).then_inc(g_act[i], 1)
                    for l in range(LV):
                        for i, sl in enumerate(slots):
                            act.wait_ge(g_pe[i], pe0 + 9 + 2 * l)
                            act.activation(sl.XX[:, :, :].rearrange("p u k -> p (u k)"), PS[:, sl.bank + 3, :], ACT.Copy).then_inc(g_act[i], 1)
                        if l == 2 and m + 1 < NPR:
                            for i in range(2):
                                pad(i, m + 1)
                    for i, sl in enumerate(slots):
                        act.wait_ge(g_pe[i], pe0 + 9 + 2 * LV)
                        act.activation(sl.WU[:, :, :, :].rearrange("p u b k -> p (u b k)"), PS[:, sl.bank + 2, :], ACT.Copy).then_inc(g_act[i], 1)

            def mix_first(ks):
                for k in ks:
                    act.activation(HH[:, k, :], MIX[:, MIX_SRC[k], :], ACT.Copy).then_inc(mix_hi, 1)

            act.wait_ge(y_add, 2 * NPR)
            hi(4 * NJ + NRAW)
            mix_first((0, 1, 2, 3))
            act.wait_ge(p_cen, 1)
            act.activation(SQY[:, :, :], YY[:, :, :], ACT.Square).then_inc(p_sq, 1)
            act.wait_ge(p_mm, 3)
            act.activation(NR, PS[:, 0, 0:32], ACT.Sqrt, bias=GN_EPS, scale=1.0 / C).then_inc(p_std, 1)
            mix_first((4, 5))
            hi(4 * NJ + NW)
            act.wait_ge(p_y, 1)
            mix_first((6, 7))

            def from_dram(nn):
                return lambda tt: act.wait_ge(nn.full[tt % 2], 16 * (tt // 2 + 1))

            hi(4 * NJ + 2 * NW)
            act.wait_ge(mix_lo_dve, 2)
            act.wait_ge(mix_lo_pool, 6)
            for tt in range(2):
                stat(nm, tt, lambda tt: MX[:, tt], JM[:, :], MS, from_dram(nm))
            for tt in range(2):
                norm_hi(nm, tt, lambda tt, b: AH[:, :, :].rearrange("p a (k t) -> p (a k) t", k=4)[:, 4 * b:4 * b + 4, tt * P:(tt + 1) * P],
                        bank=lambda tt: 4 + 2 * tt)

            def evac2(j):
                kind, i = jobs2[j]
                bank = 4 * ((j + 1) % 2)
                act.wait_ge(w_used, end2[j])
                if kind == "wkv" and i < 2:
                    act.activation(KM[:, 2 * i:2 * i + 2, :], PS[:, bank, :].rearrange("p (c t) -> p c t", c=2), ACT.Copy).then_inc(job2_act, 1)
                elif kind == "wkv":
                    act.activation(VM[:, :, (i - 2) * PW:(i - 1) * PW], PS[:, bank, :].rearrange("p (t c) -> p t c", t=2), ACT.Copy).then_inc(job2_act, 1)
                elif kind == "wq":
                    act.activation(QC[:, 2 * i:2 * i + 2, :].rearrange("p k (b c) -> p (k b) c", c=512), PS[:, bank:bank + 4, :], ACT.Copy).then_inc(job2_act, 1)

            p0 = 4 * NJ
            x_hi = lambda tt, b: HH[:, 4 * b:4 * b + 4, tt * P:(tt + 1) * P]
            hi(p0 + 20)
            args = (lambda tt: X[:, tt], JN[:, :], AS, lambda tt: act.wait_ge(job2_dve, 4))
            for tt in range(2):
                stat(n2, tt, *args)
            for tt in range(NT):
                g = X_TILES[tt]
                if tt and g // 4 > X_TILES[tt - 1] // 4:
                    evac2(4 + g // 4 - 1)
                hi(p0 + 16 + g + 5)
                if tt + 2 < NT:
                    stat(n2, tt + 2, *args)
                norm_hi(n2, tt, x_hi, bank=lambda tt: 2 + 4 * (tt % 2))
            evac2(7)
            for j in (8, 9):
                hi(p0 + 4 * j + 10)
                evac2(j)
            sc = 128 ** -0.5
            def c_exps(qb):
                act.wait_ge(c_max, qb + 1)
                if qb >= 2:
                    act.wait_ge(c_tr, qb - 1)
                for h in range(4):
                    c = 4 * (qb % 2) + h
                    a = act.activation(CP[:, qb % 2, h * 256:h * 256 + 256], PS[:, 6 * (qb % 2) + h // 2, 256 * (h % 2):256 * (h % 2) + 256], ACT.Exp,
                                       bias=CM[:, c:c + 1], scale=sc, accum_out=CL[:, c:c + 1])
                a.then_inc(c_exp, 1)

            def c_first(qb):
                act.wait_ge(c_pv, qb + 1)
                act.activation(AH[:, :, qb * P:(qb + 1) * P], PS[:, 4 + qb % 2, :].rearrange("p (k t) -> p k t", k=4), ACT.Copy).then_inc(c_hi, 1)

            c_exps(0)
            for qb in range(NT):
                if qb + 1 < NT:
                    c_exps(qb + 1)
                act.wait_ge(c_tr, qb + 1)
                if qb >= 2:
                    act.wait_ge(c_pv, qb - 1)
                act.activation(CPT[:, qb % 2, :].rearrange("p (b c) -> p b c", c=512), PS[:, 2:4, :], ACT.Copy).then_inc(c_pt, 1)
                if qb:
                    c_first(qb - 1)
            c_first(NT - 1)
            hi(p0 + 40 + 6)
            for j in range(10, 14):
                hi(p0 + 40 + 2 * (j - 9) + 5)
            norm(n3, lambda tt: X[:, tt], JN[:, :], BS, x_hi, lambda tt: act.wait_ge(*((x_added, tt // 2 + 1) if tt < 6 else (job2_dve, 8))))
            for i in range(FF_ITERS + 1):
                q0 = ff0(i)
                if i < FF_ITERS:
                    hi(q0 + 9)
                    act.wait_ge(w_used, ff0(i) + 4)
                    for k in range(4):
                        if k == 0 and i:
                            act.wait_ge(f_mul, 4 * i)
                        act.activation(ACTB[:, k // 2, 512 * (k % 2):512 * (k % 2) + 512], PS[:, k, :], ACT.Silu).then_inc(f_silu, 1)
                    hi(q0 + 12)
                    if i >= 2:
                        act.wait_ge(w_used, ff0(i))
                    for k in range(4):
                        act.wait_ge(f_mul, 4 * i + k + 1)
                        act.activation(AH[:, 2 * (i % 2) + k // 2, 512 * (k % 2):512 * (k % 2) + 512],
                                       FU[:, k // 2, 512 * (k % 2):512 * (k % 2) + 512], ACT.Copy).then_inc(f_hi, 1)
                hi(q0 + 16)
            for tt in range(NT):
                act.wait_ge(f_add, 16 * (FF_ITERS - 1) + 4 * (tt // 2 + 1))
                if tt >= 2:
                    act.wait_ge(l_o, tt - 1)
                    act.wait_ge(out_done[tt % 2], 16 * (tt // 2))
                link(act.activation(FO[:, tt % 2], X[:, tt], ACT.Square, accum_out=FS[:, tt:tt + 1]))
                act.activation(FS[:, tt:tt + 1], FS[:, tt:tt + 1], ACT.Sqrt, bias=RMS_EPS, scale=1.0 / D).then_inc(l_std, 1)

        @block.vector
        def _(dve):
            chain = [0]

            def link(ins):
                chain[0] += 1
                ins.then_inc(dve_chain, 1)
                dve.wait_ge(dve_chain, chain[0])

            TT, TS, STT = dve.tensor_tensor, dve.tensor_scalar, dve.scalar_tensor_tensor

            def scale(nn, tt, src, dst, S, R, gb):
                dve.wait_ge(nn.std, tt + 1)
                if tt >= 2:
                    dve.wait_ge(nn.tr, 2 * (tt - 1))
                link(dve.reciprocal(R[:, tt:tt + 1], S[:, tt:tt + 1]))
                STT(dst(tt), src(tt), R[:, tt:tt + 1], gb, ALU.mult, ALU.mult).then_inc(nn.xn, 1)

            def norm_lo(nn, tt, hdst, ldst, bank=lambda tt: 2 * (tt % 4)):
                for b in range(2):
                    dve.wait_ge(nn.hi, 2 * tt + b + 1)
                    TT(ldst(tt, b), PS[:, bank(tt) + b, :].rearrange("p (k t) -> p k t", k=4), hdst(tt, b).bitcast(F32),
                       ALU.subtract).then_inc(nn.lo, 1)

            def norm(nn, src, dst, S, R, gb, gain, hdst, ldst, bank=lambda tt: 2 * (tt % 4)):
                dve.wait_ge(gain_in[gain], 16)
                scale(nn, 0, src, dst, S, R, gb)
                for tt in range(nn.n):
                    if tt + 1 < nn.n:
                        scale(nn, tt + 1, src, dst, S, R, gb)
                    norm_lo(nn, tt, hdst, ldst, bank)

            norm(n1, lambda tt: XT[:, tt % 4], lambda tt: XN[:, tt % 2], SS, RS, GB[:, :], "mix",
                 lambda tt, b: HH[:, 4 * b:4 * b + 4, tt * P:(tt + 1) * P], lambda tt, b: HL[:, 4 * b:4 * b + 4, tt * P:(tt + 1) * P])
            dve.wait_ge(vec_t, 1)
            dve.tensor_copy(PT, PS[:, 7, 0:42]).then_inc(vec_c, 1)
            dve.wait_ge(vec_c, 1)
            TS(NSINK, SINK, -1.0, None, ALU.mult)
            TS(OKA, PT[:, PTC_KA:PTC_KA + 2], -1.0, 1.0, ALU.mult, ALU.add)
            for i in range(2):
                link(TT(LQ[2 * i], LQ[2 * i], LQ[2 * i + 1], ALU.mult))
                s = dve.tensor_reduce(LAM[:, i:i + 1], LQ[2 * i], AX_X, ALU.add)
            s.then_inc(lam_s, 1)

            dve.wait_ge(w_used, 24)
            dve.wait_ge(w_lo, 24)
            for i, c in enumerate((1, 0)):
                same, other = slice(64 * c, 64 * c + 64), slice(64 - 64 * c, 128 - 64 * c)
                src = BQ[same, 0, 0:2 * P]
                dve.wait_ge(job_evac, 24)
                link(dve.tensor_copy(QST[same, 0, 0, c, :], src))
                dve.tensor_copy(QST[other, 0, 0, c, :], QST[same, 0, 0, c, :].bitcast(F32))
                link(TT(QST[same, 0, 1, c, :], src, QST[same, 0, 0, c, :].bitcast(F32), ALU.subtract))
                dve.tensor_copy(QST[other, 0, 1, c, :], QST[same, 0, 1, c, :].bitcast(F32))
                dve.wait_ge(k_first, i + 1)
                TT(KST[other, 0, c, :], BK[same, 0, :], KST[same, 0, c, :].bitcast(F32), ALU.subtract).then_inc(k_second, 1)
            dve.wait_ge(lam_e, 1)
            link(TT(LAM[:, 2:3], LAM[:, 1:2], LAM[:, 0:1], ALU.subtract))
            link(TS(LAM[:, 2:3], LAM[:, 2:3], -LAM_INIT, None, ALU.add))
            dve.wait_ge(tab_in, 16)

            def d_coef(u):
                dve.wait_ge(exp_done, 2 * u + 2)
                k = 4 * (u % 2)
                e0 = (2 * u) % 4
                if u >= 2:
                    dve.wait_ge(o_evac, u - 1)
                link(dve.reciprocal(CO[:, k:k + 2], LD[:, e0:e0 + 2]))
                TS(CO[:, k + 2:k + 3], LD[:, e0:e0 + 1], CO[:, k + 1:k + 2], LAM[:, 2:3], ALU.mult, ALU.mult).then_inc(co_done, 1)

            def d_max(u):
                h, qb = u // 8, u % 8
                if qb == 0 and h:
                    link(TS(TAB[:, :], TAB[:, :], DIFF_SLOPES[h] / DIFF_SLOPES[h - 1], None, ALU.mult))
                for i, c in enumerate((1, 0)):
                    n = 2 * u + c
                    if u >= 2 and c == 0:
                        d_coef(u - 1)
                    dve.wait_ge(qk_done, 2 * u + i + 1)
                    if u >= 2 and c == 1:
                        dve.wait_ge(comb_done, u - 1)
                    if u >= 2 and c == 0:
                        dve.wait_ge(tr_done, 2 * (u - 1))
                    t0 = 896 - P * qb
                    ins = dve.tensor_tensor_reduce(E_[:, n % 4, :].rearrange("p (b c) -> p b c", c=512), PS[:, 2 * c:2 * c + 2, :],
                                                   TAB[:, t0:t0 + T].rearrange("p (b c) -> p b c", c=512), 1.0, -3.0e38, ALU.add, ALU.max,
                                                   MD[:, n % 4:n % 4 + 1])
                    ins.then_inc(s_read, 1)
                    dve.wait_ge(s_read, 2 * u + i + 1)
                    TS(NMD[:, n % 4:n % 4 + 1], MD[:, n % 4:n % 4 + 1], -1.0, None, ALU.mult).then_inc(nm_done, 1)

            def d_sums(h):
                dve.wait_ge(sq_done, h + 1)
                dve.tensor_reduce(HS, BQ[:, h, :].rearrange("p (t c) -> p t c", t=NT), AX_X, ALU.add).then_inc(hs_done, 1)

            def d_scale(h):
                dve.wait_ge(hstd, h + 1)
                link(dve.reciprocal(HR, HS))
                o = OB[:, h % 2]
                link(TT(o, o, HR.unsqueeze(2).broadcast_to([P, NT, 128]), ALU.mult))
                link(TS(o, o, 1.0 - LAM_INIT, None, ALU.mult))
                TT(BQ[:, h, :].rearrange("p (t c) -> p t c", t=NT), o, SUB.unsqueeze(1).broadcast_to([P, NT, 128]), ALU.mult).then_inc(hn_done, 1)

            d_max(0)
            d_max(1)
            for u in range(32):
                k = 4 * (u % 2)
                e0, e1 = (2 * u) % 4, (2 * u + 1) % 4
                if u in (0, 31):
                    d_coef(u)
                dve.wait_ge(co_done, u + 1)
                STT(E_[:, e0, :], E_[:, e1, :], CO[:, k + 2:k + 3], E_[:, e0, :], ALU.mult, ALU.add).then_inc(comb_done, 1)
                if u + 2 < 32:
                    d_max(u + 2)
                if u % 8 == 1 and u > 8:
                    d_sums(u // 8 - 1)
                if u % 8 == 3 and u > 8:
                    d_scale(u // 8 - 1)
            d_sums(3)
            d_scale(3)

            dve.wait_ge(pads, 1)
            for c in range(8):
                dve.wait_ge(job_evac, 4 * (6 + c // 2 + 1))
                link(TS(TMP[:, :], CIN[:, c, 0:T], col(PTC_CONV + c), None, ALU.mult))
                link(STT(TMP[:, :], CIN[:, c, 1:T + 1], col(PTC_CONV + 8 + c), TMP[:, :], ALU.mult, ALU.add))
                STT(CV[:, c, :], CV[:, c, :], col(PTC_CONV + 16 + c), TMP[:, :], ALU.mult, ALU.add).then_inc(r_conv, 1)
                dve.wait_ge(r_conv, c + 1)

            dve.wait_ge(job_evac, 4 * (NJ - 1))
            for ct in range(2):
                for half in range(2):
                    for hp in range(2):
                        rows, other, t = slice(64 * hp, 64 * hp + 64), slice(64 - 64 * hp, 128 - 64 * hp), slice(512 * half, 512 * half + 512)
                        ins = STT(QW[other, 2 * ct + hp, t], PS[rows, 4 * ((NJ - 2) % 2) + 2 * ct + half, :], 0.125, QW[rows, 2 * ct + hp, t].bitcast(F32),
                            ALU.mult, ALU.subtract)
            ins.then_inc(qw_lo, 1)
            dve.wait_ge(job_evac, 4 * (NJ - 1) + 2)
            for half in range(2):
                for kv in range(2):
                    for hp in range(2):
                        rows, t = slice(64 * kv, 64 * kv + 64), slice(512 * half, 512 * half + 512)
                        ins = TT(KW[64 * hp:64 * hp + 64, kv, 1, t], PS[rows, 4 * ((NJ - 1) % 2) + half, :], KW[rows, kv, 0, t].bitcast(F32), ALU.subtract)
            ins.then_inc(qw_lo, 1)
            dve.wait_ge(job_evac, 4 * NJ)
            for ct in range(2):
                ins = TS(KK[:, ct, :], CV[:, 2 + ct, :], col(PTC_KK + ct), None, ALU.mult)
            ins.then_inc(r_sq, 1)
            dve.wait_ge(wb_in, 16)

            dve.wait_ge(r_std, 1)
            link(TS(NR, NR, 1e-12, None, ALU.max))
            link(dve.reciprocal(NR, NR))
            dve.tensor_copy(S2_[:, :, :].rearrange("p a (u k) -> p (a u) k", k=C), NR.unsqueeze(2).broadcast_to([P, 32, C])).then_inc(r_spread, 1)

            def ch(t):
                return t.rearrange("p (c k) -> p c k", k=C)

            def r_kk_steps():
                for ct in range(2):
                    dve.wait_ge(r_back, ct + 1)
                    TT(KK[:, ct, :].rearrange("p (b c) -> p b c", c=512), KK[:, ct, :].rearrange("p (b c) -> p b c", c=512), PS[:, 4 + 2 * ct:6 + 2 * ct, :],
                       ALU.mult).then_inc(r_kk, 1)
                    dve.wait_ge(r_kk, ct + 1)
                    yield

            def r_decay_steps(d):
                if d == 0:
                    dve.wait_ge(r_scm, 1)
                for ct in range(2):
                    dve.wait_ge(r_sig, 4 * d + ct + 1)
                    link(TS(S1_[:, ct, :], S1_[:, ct, :], -E05, None, ALU.mult))
                    link(dve.tensor_tensor_scan(S2_[:, ct, :], SCM[:, :], S1_[:, ct, :], 0.0, ALU.mult, ALU.add))
                    yield
                    h = HT[:, 16 * ct:16 * ct + 16]
                    link(TS(h, S2_[:, ct, C - 1:T:C], 0.5, None, ALU.mult))
                    link(TT(ch(S2_[:, ct, :]), ch(S2_[:, ct, :]), h.unsqueeze(2).broadcast_to([P, NCH, C]), ALU.subtract))
                    yield
                    TT(S1_[:, ct, :], S2_[:, ct, :], S1_[:, ct, :], ALU.subtract).then_inc(r_c, 1)
                    yield

            def w_max(u):
                _, kv, first, nk = window(u)
                off, n, m = (first - (u // 2 - 1)) * P, nk * P, WM[:, 2 * (u % 3):2 * (u % 3) + 2]
                dve.wait_ge(w_qk, u + 1)
                if u >= 3:
                    dve.wait_ge(w_tr, u - 2)
                for g in range(2):
                    ins = dve.tensor_tensor_reduce(WP_[:, u % 3, g, 0:n], PS[:, 2 * (u % 2) + g, 0:n], WB_[:, 2 * kv + g, off:off + n], 1.0, -3.0e38,
                                                   ALU.add, ALU.max, m[:, g:g + 1])
                link(ins)
                STT(m, m, -1.0, NSINK[:, 2 * kv:2 * kv + 2], ALU.mult, ALU.min).then_inc(w_nm, 1)

            def w_norm(u):
                _, _, _, nk = window(u)
                c = slice(2 * (u % 3), 2 * (u % 3) + 2)
                dve.wait_ge(w_exp, u + 1)
                link(TT(WR[:, c], WSUM[:, c], WSNK[:, c], ALU.add))
                dve.reciprocal(WR[:, c], WR[:, c]).then_inc(w_r, 1)

            steps = [r_kk_steps(), r_decay_steps(0)]

            def prepare():
                while steps:
                    try:
                        return next(steps[0])
                    except StopIteration:
                        steps.pop(0)

            def row(t, ct):
                return t[:, ct, :].rearrange("p (c k) -> p c k", k=C)

            def r_keys(d, ct):
                kd = KDN if d else KS
                dve.wait_ge(r_kd, 2 * d + ct + 1)
                dve.wait_ge(r_exp, 7 + 3 * ct + 1 if d else ct + 1)
                TT(BKt[:, 1, ct], row(kd, ct), BKt[:, 0, ct], ALU.mult).then_inc(r_kd_used, 1)
                dve.wait_ge(r_kd_used, 2 * d + ct + 1)
                TT(BKt[:, 0, ct], row(S3_, ct), BKt[:, 0, ct], ALU.mult)

            w_max(0)
            w_max(1)
            prepare()
            prepare()
            w_norm(0)
            for u in range(NWU):
                prepare()
                if u + 2 < NWU:
                    w_max(u + 2)
                if u + 1 < NWU:
                    w_norm(u + 1)
                if u >= NWU - 2:
                    r_keys(0, u - (NWU - 2))

            while steps:
                prepare()

            for d in range(2):
                if d:
                    for _ in decay1:
                        pass
                for ct in range(2):
                    if d:
                        r_keys(1, ct)
                    base = 7 + 3 * ct if d else 1 + 2 * ct
                    dve.wait_ge(r_exp, base + 2)
                    TT(KR[:, 1, ct], KR[:, 1, ct], row(CV, ct), ALU.mult)
                    dve.wait_ge(r_exp, base + 3)
                    TT(KR[:, 0, ct], KR[:, 0, ct], row(KK, ct), ALU.mult)
                dve.wait_ge(r_exp, 7 * (d + 1))
                link(dve.memset(DD, 0.0))
                e2, d2 = EH.rearrange("p (a c) -> p a c", a=2), DD.rearrange("p (a c) -> p a c", a=2)
                dst = d2[:, :, 0:15] if d == 0 else d2[:, :, 1:16]
                TT(dst, e2[:, :, 0:15], e2[:, :, 1:16], ALU.mult).then_inc(r_pre, 1)
                if d == 0:
                    dve.wait_ge(masks_in, 16)
                else:
                    dve.wait_ge(r_ks, 1)
                    dve.wait_ge(r_kd_used, 4)
                order = list(range(NCH)) if d == 0 else list(range(NCH - 1, -1, -1))

                def chain_step(j):
                    dve.wait_ge(c_mm, (NCH - 2) * d + j)
                    for ct in range(2):
                        ins = STT(KR[:, 0, ct, order[j + 1], :], PS[:, 2, 64 * ct:64 * ct + 64], DD[:, 16 * ct + order[j]:16 * ct + order[j] + 1],
                                  BKt[:, 1, ct, order[j], :], ALU.mult, ALU.add)
                    ins.then_inc(c_z, 1)

                def chain_start(m):
                    for i in range(2):
                        dve.wait_ge(g_dve[i], G_DVE * (NPR * d + m + 1))
                    if m == 0:
                        dve.memset(KR[:, 0, :, order[0], :], 0.0)
                        dve.tensor_copy(KR[:, 0, :, order[1], :], BKt[:, 1, :, order[0], :]).then_inc(c_z, 1)

                def add_y(m):
                    dve.wait_ge(y_mm, NPR * d + m + 1)
                    y = YY[:, :, C * first_chunk(d, m):C * (first_chunk(d, m) + 4)]
                    TT(y, PS[:, 6, :].rearrange("p (a t) -> p a t", a=2), y, ALU.add).then_inc(y_add, 1)

                for m in range(NPR):
                    n = NPR * d + m
                    pe0 = G_PE * n
                    for i, sl in enumerate(slots):
                        for k in range(4):
                            dve.wait_ge(g_pe[i], pe0 + 2 + k)
                            kind, ct = k // 2, k % 2
                            TT(sl.G[:, kind, 2 * ct:2 * ct + 2].rearrange("p u r t -> p u (r t)"), PS[:, sl.bank + k, :].rearrange("p (u c) -> p u c", u=2),
                               MK[:, d, 0:256].unsqueeze(1).broadcast_to([P, 2, 256]), ALU.mult).then_inc(g_dve[i], 1)
                    for i, sl in enumerate(slots):
                        dve.wait_ge(g_pe[i], pe0 + 6)
                        q = sl.QQ[:, 0]
                        link(TT(q, PS[:, sl.bank, :].rearrange("p (u c) -> p u c", u=4), MK[:, d, 256:384].unsqueeze(1).broadcast_to([P, 4, P]), ALU.mult))
                        TT(q, q, ID.unsqueeze(1).broadcast_to([P, 4, P]), ALU.subtract).then_inc(g_dve[i], 1)
                    if m:
                        chain_start(m - 1)
                    for l in range(LV):
                        for i, sl in enumerate(slots):
                            if l == 0:
                                dve.wait_ge(g_pool[i], G_POOL * n + 1)
                            dve.wait_ge(g_pe[i], pe0 + 10 + 2 * l)
                            if l < LV - 1:
                                qq = sl.QQ[:, :, :, :].rearrange("p a u k -> p a (u k)")
                                TT(qq, PS[:, sl.bank:sl.bank + 2, :], qq, ALU.add).then_inc(g_dve[i], 1)
                            else:
                                qq = sl.QQ[:, 1].rearrange("p u k -> p (u k)")
                                TT(qq, PS[:, sl.bank + 1, :], qq, ALU.add).then_inc(g_dve[i], 1)
                        j = 4 * (m - 1) + l
                        if m and l < 4 and j:
                            chain_step(j)
                        if m and l == 3:
                            add_y(m - 1)
                    for i, sl in enumerate(slots):
                        t = tile_of(d, m, i)
                        dve.wait_ge(g_pe[i], pe0 + G_PE)
                        g = KR[:, 1, :, 2 * t:2 * t + 2, :]
                        TT(g, PS[:, sl.bank + 1, 0:256].rearrange("p (a c k) -> p a c k", a=2, c=2), g, ALU.add)
                        for cp in range(2):
                            TT(BKt[:, 0, :, 2 * t + cp, :], PS[:, sl.bank + (3, 0)[cp], 0:128].rearrange("p (a k) -> p a k", a=2),
                               I64.unsqueeze(1).broadcast_to([P, 2, C]), ALU.add)
                            c = 2 * t + cp
                            TT(BKt[:, 1, :, c, :], PS[:, sl.bank + (3, 0)[cp], 128:256].rearrange("p (a k) -> p a k", a=2),
                               DD[:, c:32:16].unsqueeze(2).broadcast_to([P, 2, C]), ALU.mult)
                        y, h = YY[:, :, t * P:(t + 1) * P], PS[:, sl.bank + 1, 256:512].rearrange("p (a t) -> p a t", a=2)
                        if d == 0:
                            dve.tensor_copy(y, h).then_inc(g_dve[i], 1)
                        else:
                            TT(y, h, y, ALU.add).then_inc(g_dve[i], 1)
                chain_start(NPR - 1)
                if d == 0:
                    decay1 = r_decay_steps(1)
                for j in range(4 * (NPR - 1), NCH - 1):
                    chain_step(j)
                    if d == 0:
                        next(decay1)
                add_y(NPR - 1)
            dve.wait_ge(y_add, 2 * NPR)
            for ct in range(2):
                ins = STT(CV[:, ct, :], CV[:, ct, :], col(PTC_RK + ct), KS[:, ct, :], ALU.mult, ALU.mult)
            ins.then_inc(p_rk, 1)

            def flat(t):
                return t.rearrange("p a (b c) -> p (a b) c", c=512)

            dve.wait_ge(p_mm, 1)
            STT(flat(YY[:, :, :]), PS[:, 0:4, :], -1.0 / C, flat(YY[:, :, :]), ALU.mult, ALU.add).then_inc(p_cen, 1)
            dve.wait_ge(p_mm, 2)
            for ct in range(2):
                ins = TT(VB[:, ct, :].rearrange("p (b c) -> p b c", c=512), PS[:, 4 + 2 * ct:6 + 2 * ct, :], CV[:, 4 + ct, :].rearrange("p (b c) -> p b c", c=512), ALU.mult)
            ins.then_inc(p_bon, 1)
            dve.wait_ge(p_std, 1)
            link(dve.reciprocal(NR, NR))
            dve.tensor_copy(RSY[:, :, :].rearrange("p a (u k) -> p (a u) k", k=C), NR.unsqueeze(2).broadcast_to([P, 32, C])).then_inc(p_spread, 1)
            dve.wait_ge(p_cen, 1)
            dve.wait_ge(p_back, 2)
            TT(flat(YY[:, :, :]), flat(YY[:, :, :]), PS[:, 0:4, :], ALU.mult).then_inc(p_nrm, 1)
            dve.wait_ge(p_nrm, 1)
            for ct in range(2):
                ins = TS(YY[:, ct, :], YY[:, ct, :], col(PTC_LNG + ct), col(PTC_LNB + ct), ALU.mult, ALU.add)
            link(ins)
            dve.wait_ge(p_bon, 1)
            link(TT(YY[:, :, :], YY[:, :, :], VB[:, :, :], ALU.add))
            dve.wait_ge(p_mm, 4)
            TT(flat(MIX[:, 6:8, :]), PS[:, 0:4, :], flat(YY[:, :, :]), ALU.mult).then_inc(p_y, 1)
            dve.wait_ge(p_y, 1)
            for k in (6, 7):
                dve.wait_ge(mix_hi, k + 1)
                TT(HL[:, k, :], MIX[:, MIX_SRC[k], :], HH[:, k, :].bitcast(F32), ALU.subtract).then_inc(mix_lo_dve, 1)

            def add_x(j, i):
                dve.wait_ge(w_used, end2[j])
                for k in range(4):
                    xs = X[:, 2 * k:2 * k + 2, i * PW:(i + 1) * PW]
                    ins = TT(xs, PS[:, 4 * ((j + 1) % 2) + k, :].rearrange("p (t c) -> p t c", t=2), xs, ALU.add)
                    if j == 13 and k < 3:
                        ins.then_inc(x_added, 1)
                ins.then_inc(job2_dve, 1)

            dve.wait_ge(x_in, 16 * NT)
            add_x(0, 0)
            mt = "p a (k t) -> p (a k) t"
            norm(nm, lambda tt: MX[:, tt], lambda tt: XN2[:, tt], MS, MR, GBM[:, :], "mem",
                 lambda tt, b: AH[:, :, :].rearrange(mt, k=4)[:, 4 * b:4 * b + 4, tt * P:(tt + 1) * P],
                 lambda tt, b: AL[:, :, :].rearrange(mt, k=4)[:, 4 * b:4 * b + 4, tt * P:(tt + 1) * P], bank=lambda tt: 4 + 2 * tt)
            for i in range(1, 4):
                add_x(i, i)
            dve.wait_ge(job2_dve, 4)
            norm(n2, lambda tt: X[:, tt], lambda tt: XN2[:, tt % 2], AS, AR, GBC[:, :], "cross",
                 lambda tt, b: HH[:, 4 * b:4 * b + 4, tt * P:(tt + 1) * P], lambda tt, b: HL[:, 4 * b:4 * b + 4, tt * P:(tt + 1) * P],
                 bank=lambda tt: 2 + 4 * (tt % 2))
            def c_prob(qb):
                c = slice(4 * (qb % 2), 4 * (qb % 2) + 4)
                dve.wait_ge(c_qk, qb + 1)
                link(dve.tensor_reduce(CM[:, c], PS[:, 6 * (qb % 2):6 * (qb % 2) + 2, :].rearrange("p b (h c) -> p (b h) c", h=2), AX_X, ALU.max))
                TS(CM[:, c], CM[:, c], -(128 ** -0.5), None, ALU.mult).then_inc(c_max, 1)
                dve.wait_ge(c_exp, qb + 1)
                link(dve.reciprocal(CR[:, c], CL[:, c]))
                p4 = CP[:, qb % 2, :].rearrange("p (h c) -> p h c", h=4)
                TT(p4, p4, CR[:, c].unsqueeze(2).broadcast_to([P, 4, 256]), ALU.mult).then_inc(c_p, 1)

            def c_second(qb):
                dve.wait_ge(c_hi, qb + 1)
                TT(AL[:, :, qb * P:(qb + 1) * P], PS[:, 4 + qb % 2, :].rearrange("p (k t) -> p k t", k=4),
                   AH[:, :, qb * P:(qb + 1) * P].bitcast(F32), ALU.subtract).then_inc(c_lo, 1)

            c_prob(0)
            for qb in range(NT):
                if qb + 1 < NT:
                    c_prob(qb + 1)
                if qb:
                    c_second(qb - 1)
            c_second(NT - 1)
            for i in range(4):
                add_x(10 + i, i)
            dve.wait_ge(job2_dve, 8)
            norm(n3, lambda tt: X[:, tt], lambda tt: XN2[:, tt % 2], BS, BR, GBF[:, :], "ffn",
                 lambda tt, b: HH[:, 4 * b:4 * b + 4, tt * P:(tt + 1) * P], lambda tt, b: HL[:, 4 * b:4 * b + 4, tt * P:(tt + 1) * P])
            def final(tt):
                dve.wait_ge(l_std, tt + 1)
                link(dve.reciprocal(FR[:, tt:tt + 1], FS[:, tt:tt + 1]))
                STT(FO[:, tt % 2], X[:, tt], FR[:, tt:tt + 1], GBL[:, :], ALU.mult, ALU.mult).then_inc(l_o, 1)

            for i in range(FF_ITERS + 1):
                if i < FF_ITERS:
                    dve.wait_ge(w_used, ff0(i) + 8)
                    for k in range(4):
                        c0 = 512 * (k % 2)
                        dve.wait_ge(f_silu, 4 * i + k + 1)
                        if i:
                            dve.wait_ge(f_lo, 4 * (i - 1) + k + 1)
                        TT(FU[:, k // 2, c0:c0 + 512], PS[:, 4 + k, :], ACTB[:, k // 2, c0:c0 + 512], ALU.mult).then_inc(f_mul, 1)
                    for k in range(4):
                        c0, a = 512 * (k % 2), 2 * (i % 2) + k // 2
                        dve.wait_ge(f_hi, 4 * i + k + 1)
                        TT(AL[:, a, c0:c0 + 512], FU[:, k // 2, c0:c0 + 512], AH[:, a, c0:c0 + 512].bitcast(F32), ALU.subtract).then_inc(f_lo, 1)
                if i == FF_ITERS:
                    dve.wait_ge(gain_in["final"], 16)
                    for k in range(4):
                        for s in range(4):
                            dve.wait_ge(f_mm, 4 * k + s + 1)
                            xs = X[:, 2 * k:2 * k + 2, s * PW:(s + 1) * PW]
                            if k == 0:
                                dve.wait_ge(f_add, 16 * (i - 2) + 4 * s + 4)
                            TT(xs, PS[:, 4 * (k % 2) + s, :].rearrange("p (t c) -> p t c", t=2), xs, ALU.add).then_inc(f_add, 1)
                        if k:
                            final(2 * k - 2)
                            final(2 * k - 1)
                    final(6)
                    final(7)
                elif i:
                    for s in range(4):
                        dve.wait_ge(w_used, ff0(i) + 8 + s + 1)
                        if i > 1:
                            dve.wait_ge(f_add, 16 * (i - 2) + 4 * s + 4)
                        for k in range(4):
                            xs = X[:, 2 * k:2 * k + 2, s * PW:(s + 1) * PW]
                            TT(xs, PS[:, 4 * (s % 2) + k, :].rearrange("p (t c) -> p t c", t=2), xs, ALU.add).then_inc(f_add, 1)
        @block.tensor
        def _(pe):
            piece = [0]

            def take():
                p = piece[0]
                piece[0] += 1
                pe.wait_ge(w_hi, p + 1)
                pe.wait_ge(w_lo, p + 1)
                return WH[:, p % NW], WL[:, p % NW]

            def feature_job(npieces, ah, al, where, starts=lambda ct, i: True, cts=(0, 1), cols=((0, 512), (512, 512)), extra=None, after=None):
                for q in range(npieces):
                    wh, wl = take()
                    for k in range(PK):
                        kt = q * PK + k
                        first, last = kt == 0, kt == npieces * PK - 1
                        for ct in cts:
                            c = slice(ct * P, ct * P + P)
                            for i, (t0, n) in enumerate(cols):
                                pe.matmul(where(ct, i), wh[:, k, c], ah(kt)[:, t0:t0 + n], start=first and starts(ct, i), stop=False, skip_group_check=True)
                                pe.matmul(where(ct, i), wh[:, k, c], al(kt)[:, t0:t0 + n], start=False, stop=False, skip_group_check=True)
                            for i, (t0, n) in enumerate(cols):
                                mm = pe.matmul(where(ct, i), wl[:, k, c], ah(kt)[:, t0:t0 + n], start=False, stop=last, skip_group_check=True)
                        if extra:
                            mm = extra(wh, wl, k, kt, first, last)
                    mm.then_inc(w_used, 1)
                    if after:
                        after(q)

            def token_mm(dst, wh, wl, ah, al, kt, tt, start, last):
                t = slice(tt * P, tt * P + P)
                pe.matmul(dst, ah(kt)[:, t], wh, start=start, stop=False, skip_group_check=True)
                pe.matmul(dst, ah(kt)[:, t], wl, start=False, stop=False, skip_group_check=True)
                return pe.matmul(dst, al(kt)[:, t], wh, start=False, stop=last, skip_group_check=True)

            def token_job(npieces, ah, al, bank, nt=NT, ready=None, after=None):
                for q in range(npieces):
                    if ready:
                        ready(q)
                    wh, wl = take()
                    for k in range(PK):
                        kt = q * PK + k
                        for tt in range(nt):
                            mm = token_mm(PS[:, bank + tt // 2, 256 * (tt % 2):256 * (tt % 2) + 256], wh[:, k, :], wl[:, k, :], ah, al, kt, tt,
                                          kt == 0 and tt % 2 == 0, kt == npieces * PK - 1)
                    mm.then_inc(w_used, 1)
                    if after:
                        after(q)

            def norm_tile(nn, tt, src, bank=lambda tt: 2 * (tt % 4), reuse=4):
                pe.wait_ge(nn.xn, tt + 1)
                for b in range(2):
                    if tt >= reuse:
                        pe.wait_ge(nn.lo, 2 * (tt - reuse) + b + 1)
                    for k in range(4):
                        kt = 4 * b + k
                        mm = pe.transpose(PS[:, bank(tt) + b, k * P:(k + 1) * P], src(tt)[:, kt * P:(kt + 1) * P], ID)
                    mm.then_inc(nn.tr, 1)

            def norm(nn, src):
                for tt in range(nn.n):
                    norm_tile(nn, tt, src)
                pe.wait_ge(nn.lo, 2 * nn.n)

            hh, hl = (lambda kt: HH[:, kt, :]), (lambda kt: HL[:, kt, :])

            pe.wait_ge(consts_in, 16)
            norm(n1, lambda tt: XN[:, tt % 2])
            pe.wait_ge(vecs_in, 16 * 17)
            pe.transpose(PS[:, 7, 0:42], VROWS, ID[0:42, 0:42]).then_inc(vec_t, 1)

            def proj(j):
                if j == 1:
                    pe.wait_ge(vec_c, 1)
                if j >= 2:
                    pe.wait_ge(job_evac, 4 * (j - 1))
                c0, bank = proj_cols[j], 4 * (j % 2)
                if BV0 <= c0 < CI0:
                    token_job(4, hh, hl, bank)
                elif c0 == AK0:
                    def values(wh, wl, k, kt, first, last):
                        for tt in range(NT):
                            mm = token_mm(PS[:, bank + 2 + tt // 4, P * (tt % 4):P * (tt % 4) + P], wh[:, k, P:2 * P], wl[:, k, P:2 * P], hh, hl, kt, tt,
                                          first and tt % 4 == 0, last)
                        return mm

                    feature_job(4, hh, hl, lambda ct, i: PS[:, bank + i, :], cts=(0,), extra=values)
                else:
                    feature_job(4, hh, hl, lambda ct, i: PS[:, bank + 2 * ct + i, :])

            for j in range(6):
                proj(j)

            pe.wait_ge(job_evac, 24)

            def d_scores(u, maps=(0, 1)):
                h, qb = u // 8, u % 8
                for i in maps:
                    c = 1 - i
                    if u:
                        pe.wait_ge(s_read, 2 * (u - 1) + i + 1)
                    if h == 0:
                        pe.wait_ge(k_second, i + 1)
                    elif i == 0:
                        pe.wait_ge(k_staged, h)
                    if u >= 2:
                        pe.wait_ge(q_staged, u // 2)
                    for part in range(2):
                        for half in range(2):
                            mm = pe.matmul(PS[:, 2 * c + half, :], QST[:, u // 2 % 2, part, c, P * (u % 2):P * (u % 2) + P],
                                           KST[:, h % 2, c, 512 * half:512 * half + 512], start=part == 0, stop=part == 1, skip_group_check=True)
                    mm.then_inc(qk_done, 1)

            def d_head(h, halves=(0, 1)):
                pe.wait_ge(hn_done, h + 1)
                for b in halves:
                    if b or h:
                        pe.wait_ge(hm_evac, 2 * h + b)
                    for k in range(4):
                        tt = 4 * b + k
                        mm = pe.transpose(PS[:, 7, k * P:(k + 1) * P], BQ[:, h, tt * P:(tt + 1) * P], ID)
                    mm.then_inc(ht_done, 1)

            d_scores(0)
            d_scores(1)
            for u in range(32):
                h, qb = u // 8, u % 8
                if u + 2 < 32:
                    d_scores(u + 2, (0,))
                pe.wait_ge(comb_done, u + 1)
                for b in range(2):
                    if u:
                        pe.wait_ge(at_evac, 2 * (u - 1) + b + 1)
                    for k in range(4):
                        kt = 4 * b + k
                        mm = pe.transpose(PS[:, 4 + b, k * P:(k + 1) * P], E_[:, (2 * u) % 4, kt * P:(kt + 1) * P], ID)
                    mm.then_inc(tr_done, 1)
                if u + 2 < 32:
                    d_scores(u + 2, (1,))
                pe.wait_ge(at_evac, 2 * u + 2)
                if u:
                    pe.wait_ge(o_evac, u)
                for kt in range(NT):
                    mm = pe.matmul(PS[:, 6, 0:P], AT_[:, kt * P:(kt + 1) * P], BV[:, kt, h * P:(h + 1) * P], start=(kt == 0), stop=(kt == NT - 1))
                mm.then_inc(pv_done, 1)
                if qb in (4, 5) and h:
                    d_head(h - 1, (qb - 4,))
            for j in range(6, NJ):
                proj(j)
                if j == 6:
                    d_head(3)
                    pe.wait_ge(hm_evac, 8)
            pe.wait_ge(job_evac, 4 * NJ)

            def token_sums(bank, src, done):
                for tt in range(NT):
                    for ct in range(2):
                        mm = pe.matmul(PS[:, bank, 4 * tt + 2 * ct:4 * tt + 2 * ct + 2], src[:, ct, tt * P:(tt + 1) * P], ONES[:, 0:P:C],
                                       start=True, stop=True, skip_group_check=True)
                mm.then_inc(done, 1)

            def turn_back(src, bank, ready, done):
                pe.wait_ge(ready, 1)
                for ct in range(2):
                    for tt in range(NT):
                        c = 256 * (tt % 4) + P * ct
                        mm = pe.transpose(PS[:, bank + 2 * ct + tt // 4, P * (tt % 4):P * (tt % 4) + P], src[:, tt // 4, c:c + P], ID)
                    mm.then_inc(done, 1)

            def r_inputs(d, k):
                kind, ct = k // 2, k % 2
                for half in range(2):
                    mm = pe.matmul(PS[:, 3 * ct + half, :], WA[:, d, kind, P * ct:P * ct + P], CV[:, 6, 512 * half:512 * half + 512], start=True, stop=True)
                mm.then_inc(r_z, 1)

            pe.wait_ge(qw_lo, 1)
            pe.wait_ge(r_act, 2)
            for k in range(4):
                if k == 1:
                    pe.wait_ge(qw_lo, 2)
                    pe.wait_ge(job_evac, 4 * NJ)
                if k >= 2:
                    pe.wait_ge(r_sig, k - 1)
                r_inputs(0, k)
            pe.wait_ge(r_sig, 4)
            pe.wait_ge(r_act, 3)
            token_sums(5, S2_, r_kn)
            for tt in range(NT):
                for ct in range(2):
                    mm = pe.transpose(PS[:, tt // 2, 256 * (tt % 2) + P * ct:256 * (tt % 2) + P * ct + P], CV[:, 4 + ct, tt * P:(tt + 1) * P], ID)
                if tt % 2:
                    mm.then_inc(r_vt, 1)
            pe.wait_ge(r_vte, 4)
            turn_back(S2_, 4, r_spread, r_back)


            def w_scores(u):
                qb, kv, first, nk = window(u)
                if u >= 2:
                    pe.wait_ge(w_nm, u - 1)
                for g in range(2):
                    for part in range(2):
                        mm = pe.matmul(PS[:, 2 * (u % 2) + g, 0:nk * P], QW[:, 2 * kv + g, qb * P:(qb + 1) * P], KW[:, kv, part, first * P:(first + nk) * P],
                                       start=part == 0, stop=part == 1, skip_group_check=True)
                mm.then_inc(w_qk, 1)

            def w_values(u):
                qb, kv, first, nk = window(u)
                pe.wait_ge(w_pt, u + 1)
                if u >= 2:
                    pe.wait_ge(w_mix, u - 1)
                for k in range(nk):
                    for g in range(2):
                        mm = pe.matmul(PS[64 * g:64 * g + 64, 6 + u % 2, 0:P], AV[:, first + k, 64 * kv:64 * kv + 64], WT_[:, u % 2, nk * g + k, :],
                                       start=k == 0, stop=k == nk - 1, skip_group_check=True)
                mm.then_inc(w_pv, 1)

            w_scores(0)
            w_scores(1)
            pe.wait_ge(r_kk, 2)
            for u in range(NWU):
                _, _, _, nk = window(u)
                if u + 2 < NWU:
                    w_scores(u + 2)
                pe.wait_ge(w_p, u + 1)
                if u:
                    pe.wait_ge(w_pt, u)
                for g in range(2):
                    for k in range(nk):
                        i = nk * g + k
                        mm = pe.transpose(PS[:, 4 + i // 4, P * (i % 4):P * (i % 4) + P], WP_[:, u % 3, g, k * P:(k + 1) * P], ID)
                mm.then_inc(w_tr, 1)
                if u:
                    w_values(u - 1)
            w_values(NWU - 1)
            pe.wait_ge(w_mix, NWU)

            for d in range(2):
                pe.wait_ge(r_pre, d + 1)
                pe.wait_ge(r_exp, 7 * (d + 1))
                order = list(range(NCH)) if d == 0 else list(range(NCH - 1, -1, -1))

                def mm1(dst, lhsT, rhs, start=True, stop=True):
                    return pe.matmul(dst, lhsT, rhs, start=start, stop=stop, skip_group_check=True)

                def chain_step(j):
                    pe.wait_ge(c_z, (NCH - 1) * d + j)
                    for ct in range(2):
                        for hp in range(2):
                            r = slice(64 * hp, 64 * hp + 64)
                            mm = mm1(PS[r, 2, 64 * ct:64 * ct + 64], BKt[r, 0, ct, order[j], :], KR[r, 0, ct, order[j], :])
                    mm.then_inc(c_mm, 1)

                def state_out(m):
                    for k in range(4):
                        c = first_chunk(d, m) + k
                        for ct in range(2):
                            for hp in range(2):
                                r = slice(64 * hp, 64 * hp + 64)
                                mm = mm1(PS[r, 6, 256 * ct + 64 * k:256 * ct + 64 * k + 64], KR[r, 0, ct, c, :], KR[r, 1, ct, c, :])
                    mm.then_inc(y_mm, 1)

                for m in range(NPR):
                    n = NPR * d + m
                    dv0, ac0, po0 = G_DVE * n, G_ACT * n, G_POOL * n

                    def both(t, t4, i, ct):
                        return t4[:, i, ct, 2 * t:2 * t + 2, :].rearrange("p c k -> p (c k)")

                    for i, sl in enumerate(slots):
                        t, b0 = tile_of(d, m, i), sl.bank
                        pe.wait_ge(g_act[i], ac0)
                        pe.wait_ge(g_dve[i], dv0)
                        for ct in range(2):
                            pe.transpose(PS[:, b0 + 3, P * ct:P * ct + P], both(t, KR, 0, ct), ID)
                            mm = pe.transpose(PS[:, b0 + 3, 256 + P * ct:256 + P * ct + P], both(t, BKt, 0, ct), ID)
                        mm.then_inc(g_pe[i], 1)
                        pe.wait_ge(pad_done[i], n + 1)
                        for k in range(4):
                            if k == 3:
                                pe.wait_ge(g_act[i], ac0 + 1)
                            kind, ct = k // 2, k % 2
                            mm1(PS[:, b0 + k, :], both(t, BKt, kind, ct), sl.PAD[:, ct].rearrange("p u r t -> p (u r t)")).then_inc(g_pe[i], 1)
                    for i, sl in enumerate(slots):
                        t, b0 = tile_of(d, m, i), sl.bank
                        pe.wait_ge(g_dve[i], dv0 + 1)
                        for u in range(4):
                            mm = mm1(PS[:, b0, P * u:P * u + P], sl.PAD[:, u // 2, u % 2, 0, :], both(t, BKt, 0, u // 2))
                        mm.then_inc(g_pe[i], 1)
                        pe.wait_ge(g_dve[i], dv0 + 2)
                        for ct in range(2):
                            mm = pe.transpose(PS[:, b0 + 1, P * ct:P * ct + P], both(t, BKt, 1, ct), ID)
                        mm.then_inc(g_pe[i], 1)
                        pe.wait_ge(g_dve[i], dv0 + 4)
                        for u in range(4):
                            for cp in range(2):
                                r = slice(64 * cp, 64 * cp + 64)
                                mm = mm1(PS[r, b0 + 2, 64 * u:64 * u + 64], sl.G[r, 1, u, 0, r], VT[r, t, 64 * u:64 * u + 64])
                        mm.then_inc(g_pe[i], 1)
                    for l in range(LV):
                        for i, sl in enumerate(slots):
                            pe.wait_ge(g_pool[i], po0 + 2 + l)
                            pe.wait_ge(g_dve[i], dv0 + 5 + l)
                            for u in range(4):
                                mm = mm1(PS[:, sl.bank + 3, P * u:P * u + P], sl.LT[:, u, :], sl.QQ[:, 0, u, :])
                            mm.then_inc(g_pe[i], 1)
                        for i, sl in enumerate(slots):
                            pe.wait_ge(g_act[i], ac0 + 4 + l)
                            if l < LV - 1:
                                for u in range(4):
                                    mm1(PS[:, sl.bank, P * u:P * u + P], sl.QQ[:, 1, u, :], sl.XX[:, u, :])
                            for u in range(4):
                                mm = mm1(PS[:, sl.bank + 1, P * u:P * u + P], sl.XX[:, u, :], sl.QQ[:, 1, u, :])
                            mm.then_inc(g_pe[i], 1)
                        j = 4 * (m - 1) + l
                        if m and l < 4 and j:
                            chain_step(j)
                        if m and l == 3:
                            state_out(m - 1)
                    for i, sl in enumerate(slots):
                        pe.wait_ge(g_dve[i], dv0 + 5 + LV)
                        if m:
                            pe.wait_ge(*((c_z, (NCH - 1) * d + 4 * m) if i == 0 else (y_add, n)))
                        for u in range(4):
                            mm = mm1(PS[:, sl.bank + 2, P * u:P * u + P], sl.QQ[:, 1, u, :], sl.RH[:, u, :, :].rearrange("p b k -> p (b k)"))
                        mm.then_inc(g_pe[i], 1)
                    for i, sl in enumerate(slots):
                        t, b0 = tile_of(d, m, i), sl.bank
                        pe.wait_ge(g_act[i], ac0 + 4 + LV)
                        for ct in range(2):
                            for hp in range(2):
                                for cq in range(2):
                                    cp = cq ^ hp
                                    u, r, o, bk, f = 2 * ct + hp, slice(64 * cp, 64 * cp + 64), slice(64 * hp, 64 * hp + 64), b0 + (3, 0)[cp], 64 * ct
                                    mm1(PS[o, bk, f:f + 64], sl.WU[r, u, 0, :], sl.BT[r, u, :])
                                    mm1(PS[o, bk, 128 + f:128 + f + 64], sl.KT[r, u, :], VT[r, t, 64 * u:64 * u + 64], stop=False)
                                    mm1(PS[o, bk, 128 + f:128 + f + 64], sl.BT[r, u, :], sl.WU[r, u, 1, :], start=False)
                        for ct in range(2):
                            for step in range(3):
                                for hp in range(2):
                                    u, o = 2 * ct + hp, slice(64 * hp, 64 * hp + 64)
                                    if step == 0:
                                        mm1(PS[o, b0 + 1, P * ct:P * ct + P], sl.WU[:, u, 0, :], sl.G[:, 0, u, 1, :])
                                    elif step == 1:
                                        mm1(PS[o, b0 + 1, 256 + P * ct:256 + P * ct + P], VT[:, t, 64 * u:64 * u + 64], sl.G[:, 1, u, 1, :], stop=False)
                                    else:
                                        mm = mm1(PS[o, b0 + 1, 256 + P * ct:256 + P * ct + P], sl.WU[:, u, 1, :], sl.G[:, 0, u, 1, :], start=False)
                        mm.then_inc(g_pe[i], 1)
                for i in range(2):
                    pe.wait_ge(g_act[i], G_ACT * NPR * (d + 1))
                    pe.wait_ge(g_dve[i], G_DVE * NPR * (d + 1))
                for k, j in enumerate(range(4 * (NPR - 1), NCH - 1)):
                    if d == 0:
                        if k >= 2:
                            pe.wait_ge(r_sig, 4 + k - 1)
                        r_inputs(1, k)
                    chain_step(j)
                if d == 0:
                    pe.wait_ge(r_sig, 4 + 2)
                    r_inputs(1, 3)
                pe.wait_ge(c_z, (NCH - 1) * (d + 1))
                state_out(NPR - 1)
                pe.wait_ge(y_add, NPR * (d + 1))

            def head_sums(bank, src):
                for ct in range(2):
                    for half in range(2):
                        mm = pe.matmul(PS[:, bank + 2 * ct + half, :], ONES, src[:, ct, 512 * half:512 * half + 512], start=True, stop=True)
                mm.then_inc(p_mm, 1)

            head_sums(0, YY)
            pe.wait_ge(p_rk, 1)
            head_sums(4, CV)
            pe.wait_ge(p_sq, 1)
            pe.wait_ge(p_cen, 1)
            token_sums(0, SQY, p_mm)
            pe.wait_ge(p_bon, 1)

            mh, ml = ((lambda kt, t=t: t[:, kt // 4, 256 * (kt % 4):256 * (kt % 4) + 256]) for t in (AH, AL))
            oh, ol = (lambda kt: AH[:, kt, :]), (lambda kt: AL[:, kt, :])
            def out_ready(q):
                if q == 1:
                    pe.wait_ge(p_std, 1)
                    turn_back(RSY, 0, p_spread, p_back)
                if q == 2:
                    pe.wait_ge(p_nrm, 1)
                    for ct in range(2):
                        for half in range(2):
                            mm = pe.matmul(PS[:, 2 * ct + half, :], GU[:, P * ct:P * ct + P], CV[:, 7, 512 * half:512 * half + 512], start=True, stop=True)
                    mm.then_inc(p_mm, 1)
                pe.wait_ge(*mix_parts[q])

            mix_parts = ((mix_lo_pool, 2), (mix_lo_pool, 4), (mix_lo_pool, 6), (mix_lo_dve, 2))
            for j, (kind, i) in enumerate(jobs2):
                if j >= 2:
                    pe.wait_ge(*evac_of[j - 2])
                bank = 4 * ((j + 1) % 2)

                def x_tile(q):
                    g = 4 * i + q
                    if g == X_TILES[0]:
                        for e in evac_of[2:4]:
                            pe.wait_ge(*e)
                    if g in X_TILES:
                        norm_tile(n2, X_TILES.index(g), lambda tt: XN2[:, tt % 2], bank=lambda tt: 2 + 4 * (tt % 2), reuse=2)

                if kind == "wout":
                    token_job(4, hh, hl, bank, ready=out_ready if i == 0 else None)
                    if i == 1:
                        pe.wait_ge(*evac_of[0])
                        for tt in range(2):
                            norm_tile(nm, tt, lambda tt: XN2[:, tt], bank=lambda tt: 4 + 2 * tt)
                        pe.wait_ge(nm.lo, 4)
                elif kind == "wkv" and i < 2:
                    feature_job(4, mh, ml, lambda ct, _: PS[:, bank, 256 * ct:256 * ct + 256], starts=lambda ct, _: ct == 0, cols=((0, 256),), after=x_tile)
                elif kind == "wkv":
                    token_job(4, mh, ml, bank, nt=2, after=x_tile)
                elif kind == "wq":
                    if i == 0:
                        for e in evac_of[4:8]:
                            pe.wait_ge(*e)
                        pe.wait_ge(n2.lo, 2 * NT)
                    feature_job(4, hh, hl, lambda ct, k: PS[:, bank + 2 * ct + k, :])
                else:
                    if i == 0:
                        pe.wait_ge(*evac_of[9])
                        cross()
                    token_job(2, oh, ol, bank)
                if kind == "wq" and i == 1:
                    def cross():
                        def scores(qb):
                            if qb >= 2:
                                pe.wait_ge(c_exp, qb - 1)
                            for h in range(4):
                                mm = pe.matmul(PS[:, 6 * (qb % 2) + h // 2, 256 * (h % 2):256 * (h % 2) + 256], QC[:, h, qb * P:(qb + 1) * P], KM[:, h, :],
                                               start=True, stop=True, skip_group_check=True)
                            mm.then_inc(c_qk, 1)

                        def values(qb):
                            pe.wait_ge(c_pt, qb + 1)
                            if qb >= 2:
                                pe.wait_ge(c_lo, qb - 1)
                            for h in range(4):
                                for m in range(2):
                                    mm = pe.matmul(PS[:, 4 + qb % 2, P * h:P * h + P], VM[:, m, P * h:P * h + P], CPT[:, qb % 2, P * (2 * h + m):P * (2 * h + m) + P],
                                                   start=(m == 0), stop=(m == 1), skip_group_check=True)
                            mm.then_inc(c_pv, 1)

                        scores(0)
                        for qb in range(NT):
                            if qb + 1 < NT:
                                scores(qb + 1)
                            if qb:
                                values(qb - 1)
                            pe.wait_ge(c_p, qb + 1)
                            if qb:
                                pe.wait_ge(c_pt, qb)
                            for k in range(8):
                                mm = pe.transpose(PS[:, 2 + k // 4, P * (k % 4):P * (k % 4) + P], CP[:, qb % 2, P * k:P * k + P], ID)
                            mm.then_inc(c_tr, 1)
                        values(NT - 1)
                        pe.wait_ge(c_lo, NT)
            for e in evac_of[12:]:
                pe.wait_ge(*e)
            norm(n3, lambda tt: XN2[:, tt % 2])
            for i in range(FF_ITERS + 1):
                if i < FF_ITERS:
                    if i == 1:
                        pe.wait_ge(f_silu, 4)
                    elif i:
                        pe.wait_ge(f_add, 16 * (i - 2) + 12)
                    feature_job(4, hh, hl, lambda ct, k: PS[:, 2 * ct + k, :])
                    if i == 1:
                        pe.wait_ge(f_mul, 4)
                    elif i:
                        pe.wait_ge(f_add, 16 * (i - 2) + 16)
                    feature_job(4, hh, hl, lambda ct, k: PS[:, 4 + 2 * ct + k, :])
                if i:
                    m = i - 1
                    pe.wait_ge(f_lo, 4 * m + 4)
                    if i == FF_ITERS:
                        ws = [take() for _ in range(4)]
                        for k in range(4):
                            for s, (wh, wl) in enumerate(ws):
                                pe.wait_ge(f_add, 16 * (m - 1) + 12 + 4 * k if k < 2 else 16 * m + 4 * (k - 2) + s + 1)
                                for kt in range(PK):
                                    for t in range(2):
                                        tt = 2 * k + t
                                        mm = token_mm(PS[:, 4 * (k % 2) + s, 256 * t:256 * t + 256], wh[:, kt, :], wl[:, kt, :],
                                                      lambda kt: AH[:, 2 * (m % 2) + kt, :], lambda kt: AL[:, 2 * (m % 2) + kt, :], kt, tt,
                                                      kt == 0 and t == 0, kt == PK - 1)
                                mm.then_inc(f_mm, 1)
                        continue
                    for s in range(4):
                        if s >= 2:
                            pe.wait_ge(f_add, 16 * m + 4 * (s - 1))
                        else:
                            pe.wait_ge(*((f_silu, 4 * i + 4) if s == 0 else (f_mul, 4 * i + 4)))
                        token_job(1, lambda kt: AH[:, 2 * (m % 2) + kt, :], lambda kt: AL[:, 2 * (m % 2) + kt, :], 4 * (s % 2))


INPUTS = ["x", "mem", "norm_mix", "w_in", "win_sink", "diff_lq1", "diff_lk1", "diff_lq2", "diff_lk2", "diff_subln",
          "rwkv_conv", "rwkv_w0", "rwkv_w_up", "rwkv_a0", "rwkv_a_up", "rwkv_g_up", "rwkv_k_k", "rwkv_k_a", "rwkv_r_k",
          "rwkv_ln_g", "rwkv_ln_b", "w_out", "norm_cross", "norm_mem", "x_wq", "x_wkv", "x_wo", "norm_ffn",
          "ffn_w_gu", "ffn_w_down", "norm_final"]


def shape_constants():
    import numpy as np

    row, colm = np.arange(P) % C, np.arange(C)
    j, t = row[:, None], colm[None, :]
    cn = np.zeros((P, C_LEN), np.float32)
    cn[:, C_ID:C_ID + P] = np.eye(P)
    cn[:, C_ONES:C_ONES + P] = np.kron(np.eye(2), np.ones((C, C)))
    own = np.kron(np.eye(2), np.ones((C, C)))
    masks = []
    for a, b in ((t > j, t >= j), (t < j, t <= j)):
        masks += [np.tile(a, 2) * own, np.tile(b, 2) * own, None]
    for l, s in enumerate([1] + LEVELS):
        later = (t // s % 2 == 1) & (j // s == t // s - 1)
        earlier = (j // s % 2 == 1) & (t // s == j // s - 1)
        cn[:, C_LT[0] + 64 * l:C_LT[0] + 64 * l + 64] = later
        cn[:, C_LT[1] + 64 * l:C_LT[1] + 64 * l + 64] = earlier
    for d in range(2):
        masks[3 * d + 2] = np.tile(cn[:, C_LT[1 - d]:C_LT[1 - d] + C], 2) * own
    cn[:, C_I64:C_I64 + 64] = j == t
    p = np.arange(P)[:, None]
    dist = (-DIFF_SLOPES[0] * np.abs(np.arange(1920)[None, :] - 896 - p)).astype(np.float32)
    delta = np.abs(np.arange(384)[None, :] - P - p)
    win = np.concatenate([np.where(delta <= 128, -s * delta, -1e30) for s in WIN_SLOPES], 1).astype(np.float32)
    return {"consts": cn, "dist": dist, "win_bias": win, "masks": np.concatenate(masks, 1).astype(np.float32)}


def kernel(**inputs):
    import numpy as np
    import concourse.bacc as bacc
    from concourse.bass_utils import run_bass_kernel_spmd

    nc = bacc.Bacc("TRN2", target_bir_lowering=False, num_devices=1)
    arrays = {f"in_{k}": np.ascontiguousarray(inputs[k]) for k in INPUTS}
    arrays.update({f"in_{k}": v for k, v in shape_constants().items()})
    io = {k[3:]: nc.dram_tensor(k, v.shape, mybir.dt.from_np(v.dtype), kind="ExternalInput").ap() for k, v in arrays.items()}
    io["out"] = nc.dram_tensor("out_x", (1, T, D), F32, kind="ExternalOutput").ap()
    build(nc, io)
    r = run_bass_kernel_spmd(nc, [arrays], core_ids=[0])
    return r.results[0]["out_x"]
```
